# Optimizing a Trainium2 kernel written in Bass

```python
import math
import jax, jax.numpy as jnp
from jax import lax
import numpy as np

D_MODEL = 2048
BATCH = 1
SEQ = 512
DEPTH = 1

D_MIX = D_MODEL
NSA_HEADS = 8
NSA_KV_HEADS = 2
NSA_GROUP = NSA_HEADS // NSA_KV_HEADS
NSA_HEAD_DIM = 128
NSA_WIDTH = NSA_HEADS * NSA_HEAD_DIM
NSA_KV_WIDTH = NSA_KV_HEADS * NSA_HEAD_DIM
CMP_BLOCK = 32
CMP_STRIDE = 16
SLC_BLOCK = 64
SLC_TOP_N = 16
WINDOW = 512
SLC_QBLK = 64
WIN_QBLK = 128
RWKV_WIDTH = D_MIX - NSA_WIDTH
RWKV_HEAD_DIM = 64
RWKV_HEADS = RWKV_WIDTH // RWKV_HEAD_DIM
DECAY_LORA = 64
AAA_LORA = 64
SHIFT_COLS = 3 * RWKV_WIDTH + DECAY_LORA + AAA_LORA
NUM_BUCKETS = 32
MAX_DISTANCE = 1024
NORM_EPS = 1e-6
RWKV_GN_EPS = 64e-5
COL_Q = NSA_WIDTH
COL_KV = 6 * NSA_KV_WIDTH
COL_GATE = 3 * NSA_HEADS
COL_ZA = NSA_WIDTH
COL_ZB = RWKV_WIDTH
IN_COLS = COL_Q + COL_KV + COL_GATE + COL_ZA + SHIFT_COLS + COL_ZB


def rms_norm(x, g):
    xf = x.astype(jnp.float32)
    y = xf * lax.rsqrt(jnp.mean(xf * xf, axis=-1, keepdims=True) + NORM_EPS)
    return (y * g.astype(jnp.float32)).astype(x.dtype)

def rel_bucket(dist):
    n = jnp.maximum(dist, 0)
    max_exact = NUM_BUCKETS // 2
    nf = jnp.maximum(n, 1).astype(jnp.float32)
    large = max_exact + (jnp.log(nf / max_exact) / math.log(MAX_DISTANCE / max_exact)
                         * (NUM_BUCKETS - max_exact)).astype(jnp.int32)
    large = jnp.minimum(large, NUM_BUCKETS - 1)
    return jnp.where(n < max_exact, n, large)

def masked_softmax(logits, mask, axis):
    logits = jnp.where(mask, logits, -jnp.inf)
    m = jnp.max(logits, axis=axis, keepdims=True)
    m = jnp.where(jnp.isfinite(m), m, 0.0)
    e = jnp.where(mask, jnp.exp(logits - m), 0.0)
    s = jnp.sum(e, axis=axis, keepdims=True)
    return e / jnp.maximum(s, 1e-30)

def compress(kv, pos, w1, w2):
    B, S, G, D = kv.shape
    n_cmp = (S - CMP_BLOCK) // CMP_STRIDE + 1
    idx = jnp.arange(n_cmp)[:, None] * CMP_STRIDE + jnp.arange(CMP_BLOCK)[None, :]
    blocks = kv[:, idx] + pos[None, None, :, None, :]
    flat = blocks.transpose(0, 1, 3, 2, 4).reshape(B, n_cmp, G, CMP_BLOCK * D)
    return jax.nn.silu(flat @ w1) @ w2

def nsa_mixer(q, k_cmp, v_cmp, k_slc, v_slc, k_win, v_win, gates, rel_bias_table,
              cmp_pos_k, cmp_pos_v, cmp_k_w1, cmp_k_w2, cmp_v_w1, cmp_v_w2):
    f32 = jnp.float32
    B, S = q.shape[:2]
    G, HG, D = NSA_KV_HEADS, NSA_GROUP, NSA_HEAD_DIM
    qf = q.astype(f32).reshape(B, S, G, HG, D) * (D ** -0.5)
    t = jnp.arange(S)
    table = rel_bias_table.astype(f32)

    kc = compress(k_cmp.astype(f32).reshape(B, S, G, D), cmp_pos_k.astype(f32),
                  cmp_k_w1.astype(f32), cmp_k_w2.astype(f32))
    vc = compress(v_cmp.astype(f32).reshape(B, S, G, D), cmp_pos_v.astype(f32),
                  cmp_v_w1.astype(f32), cmp_v_w2.astype(f32))
    n_cmp = kc.shape[1]
    blk_end = jnp.arange(n_cmp) * CMP_STRIDE + CMP_BLOCK - 1
    dist_c = t[:, None] - blk_end[None, :]
    mask_c = dist_c >= 0
    bias_c = table[rel_bucket(dist_c)].reshape(S, n_cmp, G, HG).transpose(2, 3, 0, 1)
    logits_c = jnp.einsum('bsghd,bigd->bghsi', qf, kc) + bias_c
    p_c = masked_softmax(logits_c, mask_c, -1)
    o_c = jnp.einsum('bghsi,bigd->bsghd', p_c, vc)

    n_blk = S // SLC_BLOCK
    cmp_start = jnp.arange(n_cmp) * CMP_STRIDE
    slc_start = jnp.arange(n_blk) * SLC_BLOCK
    overlap = ((cmp_start[:, None] < slc_start[None, :] + SLC_BLOCK)
               & (cmp_start[:, None] + CMP_BLOCK > slc_start[None, :])).astype(f32)
    imp = jnp.einsum('bghsi,ij->bgsj', p_c, overlap)
    cur = t // SLC_BLOCK
    j = jnp.arange(n_blk)
    forced = (j[None, :] == 0) | (j[None, :] == cur[:, None]) | (j[None, :] == cur[:, None] - 1)
    causal_blk = j[None, :] <= cur[:, None]
    score = jnp.where(forced, jnp.inf, jnp.where(causal_blk, imp, -jnp.inf))
    n_sel = min(SLC_TOP_N, n_blk)
    _, sel_idx = lax.top_k(score, n_sel)

    kb = k_slc.astype(f32).reshape(B, n_blk, SLC_BLOCK, G, D).transpose(0, 3, 1, 2, 4)
    vb = v_slc.astype(f32).reshape(B, n_blk, SLC_BLOCK, G, D).transpose(0, 3, 1, 2, 4)
    nqb = S // SLC_QBLK
    q_blocks = qf.reshape(B, nqb, SLC_QBLK, G, HG, D).transpose(1, 0, 2, 3, 4, 5)
    idx_blocks = sel_idx.reshape(B, G, nqb, SLC_QBLK, n_sel).transpose(2, 0, 1, 3, 4)
    t_blocks = t.reshape(nqb, SLC_QBLK)
    b_ix = jnp.arange(B)[:, None, None, None]
    g_ix = jnp.arange(G)[None, :, None, None]
    g_ix5 = jnp.arange(G)[None, :, None, None, None]
    tab = table.reshape(NUM_BUCKETS, G, HG)

    def slc_block(args):
        qb, ib, tb = args
        kg = kb[b_ix, g_ix, ib]
        vg = vb[b_ix, g_ix, ib]
        s_pos = ib[..., None] * SLC_BLOCK + jnp.arange(SLC_BLOCK)
        dist = tb[None, None, :, None, None] - s_pos
        valid_blk = ib <= (tb // SLC_BLOCK)[None, None, :, None]
        mask = (dist >= 0) & valid_blk[..., None]
        bias = tab[rel_bucket(dist), g_ix5]
        logits = jnp.einsum('bqghd,bgqnkd->bgqnkh', qb, kg) + bias
        m_tok = n_sel * SLC_BLOCK
        logits = logits.reshape(B, G, SLC_QBLK, m_tok, HG)
        p = masked_softmax(logits, mask.reshape(B, G, SLC_QBLK, m_tok)[..., None], -2)
        return jnp.einsum('bgqmh,bgqmd->bqghd', p, vg.reshape(B, G, SLC_QBLK, m_tok, D))

    o_s = lax.map(slc_block, (q_blocks, idx_blocks, t_blocks))
    o_s = o_s.transpose(1, 0, 2, 3, 4, 5).reshape(B, S, G, HG, D)

    nwb = S // WIN_QBLK
    n_pre = WINDOW // WIN_QBLK
    band = n_pre + 1
    m_win = band * WIN_QBLK
    pad = ((0, 0), (WINDOW, 0), (0, 0), (0, 0))
    kw = jnp.pad(k_win.astype(f32).reshape(B, S, G, D), pad).reshape(B, nwb + n_pre, WIN_QBLK, G, D)
    vw = jnp.pad(v_win.astype(f32).reshape(B, S, G, D), pad).reshape(B, nwb + n_pre, WIN_QBLK, G, D)
    kband = jnp.concatenate([kw[:, i:i + nwb] for i in range(band)], axis=2)
    vband = jnp.concatenate([vw[:, i:i + nwb] for i in range(band)], axis=2)
    qw = qf.reshape(B, nwb, WIN_QBLK, G, HG, D)
    tq = t.reshape(nwb, WIN_QBLK)
    s_pos = (jnp.arange(nwb) * WIN_QBLK - WINDOW)[:, None] + jnp.arange(m_win)[None, :]
    dist = tq[:, :, None] - s_pos[:, None, :]
    mask_w = (dist >= 0) & (dist < WINDOW) & (s_pos[:, None, :] >= 0)
    bias_w = table[rel_bucket(dist)].reshape(nwb, WIN_QBLK, m_win, G, HG).transpose(0, 3, 4, 1, 2)
    logits_w = jnp.einsum('bnqghd,bnmgd->bnghqm', qw, kband) + bias_w[None]
    p_w = masked_softmax(logits_w, mask_w[None, :, None, None], -1)
    o_w = jnp.einsum('bnghqm,bnmgd->bnqghd', p_w, vband).reshape(B, S, G, HG, D)

    gt = jax.nn.sigmoid(gates.astype(f32)).reshape(B, S, 3, G, HG, 1)
    o = gt[:, :, 0] * o_c + gt[:, :, 1] * o_s + gt[:, :, 2] * o_w
    return o.reshape(B, S, NSA_WIDTH)

def rwkv7_mixer(feat, mu, w0, w2, a0, a2, k_k, k_a, r_k, ln_w, ln_b):
    f32 = jnp.float32
    B, S, _ = feat.shape
    H, N, W = RWKV_HEADS, RWKV_HEAD_DIM, RWKV_WIDTH
    pf = feat.astype(f32)
    prev = jnp.pad(pf[:, :-1], ((0, 0), (1, 0), (0, 0)))
    pf = pf + mu.astype(f32) * (prev - pf)
    r, k, v, wd, ad = jnp.split(pf, [W, 2 * W, 3 * W, 3 * W + DECAY_LORA], axis=-1)
    w = -jax.nn.softplus(-(w0.astype(f32) + jnp.tanh(wd) @ w2.astype(f32))) - 0.5
    decay = jnp.exp(-jnp.exp(w))
    a = jax.nn.sigmoid(a0.astype(f32) + ad @ a2.astype(f32))
    kk = (k * k_k.astype(f32)).reshape(B, S, H, N)
    kk = kk / jnp.maximum(jnp.sqrt(jnp.sum(kk * kk, axis=-1, keepdims=True)), 1e-12)
    k = k * (1.0 + (a - 1.0) * k_a.astype(f32))
    r4, w4, k4, v4, a4 = (z.reshape(B, S, H, N) for z in (r, decay, k, v, a))
    aa = -kk
    bb = kk * a4

    def step(state, inp):
        r_t, w_t, k_t, v_t, a_t, b_t = inp
        sa = jnp.einsum('bhij,bhj->bhi', state, a_t)
        state = (state * w_t[:, :, None, :] + sa[..., None] * b_t[:, :, None, :]
                 + v_t[..., None] * k_t[:, :, None, :])
        return state, jnp.einsum('bhij,bhj->bhi', state, r_t)

    xs = tuple(z.transpose(1, 0, 2, 3) for z in (r4, w4, k4, v4, aa, bb))
    state0 = jnp.zeros((B, H, N, N), f32)
    _, y = lax.scan(step, state0, xs)
    y = y.transpose(1, 0, 2, 3)
    mean = jnp.mean(y, axis=-1, keepdims=True)
    var = jnp.mean(jnp.square(y - mean), axis=-1, keepdims=True)
    y = ((y - mean) * lax.rsqrt(var + RWKV_GN_EPS)).reshape(B, S, W) * ln_w.astype(f32) + ln_b.astype(f32)
    bonus = jnp.sum(r4 * k4 * r_k.astype(f32), axis=-1, keepdims=True) * v4
    return y + bonus.reshape(B, S, W)

def first_inputs(seed: int = 0) -> dict:
    key = jax.random.key(seed)
    ks = jax.random.split(key, 24)
    f32 = jnp.float32
    L = DEPTH
    HD = NSA_HEAD_DIM

    def nrm(k, shape, scale):
        return jax.random.normal(k, shape, f32) * scale

    return {
        'x': nrm(ks[0], (BATCH, SEQ, D_MODEL), 1.0),
        'pre_norm_g': 1.0 + nrm(ks[1], (L, D_MODEL), 0.05),
        'w_in': nrm(ks[2], (L, D_MODEL, IN_COLS), D_MODEL ** -0.5),
        'rel_bias_table': nrm(ks[3], (NUM_BUCKETS, NSA_HEADS), 0.5),
        'cmp_pos_k': nrm(ks[4], (L, CMP_BLOCK, HD), 0.1),
        'cmp_pos_v': nrm(ks[5], (L, CMP_BLOCK, HD), 0.1),
        'cmp_k_w1': nrm(ks[6], (L, CMP_BLOCK * HD, HD), (CMP_BLOCK * HD) ** -0.5),
        'cmp_k_w2': nrm(ks[7], (L, HD, HD), HD ** -0.5),
        'cmp_v_w1': nrm(ks[8], (L, CMP_BLOCK * HD, HD), (CMP_BLOCK * HD) ** -0.5),
        'cmp_v_w2': nrm(ks[9], (L, HD, HD), HD ** -0.5),
        'rwkv_mu': jax.random.uniform(ks[10], (L, SHIFT_COLS), f32),
        'rwkv_w0': jax.random.uniform(ks[11], (L, RWKV_WIDTH), f32, -6.0, -1.0),
        'rwkv_w2': nrm(ks[12], (L, DECAY_LORA, RWKV_WIDTH), 0.1),
        'rwkv_a0': nrm(ks[13], (L, RWKV_WIDTH), 0.1),
        'rwkv_a2': nrm(ks[14], (L, AAA_LORA, RWKV_WIDTH), 0.1),
        'rwkv_k_k': 0.85 + nrm(ks[15], (L, RWKV_WIDTH), 0.05),
        'rwkv_k_a': 1.0 + nrm(ks[16], (L, RWKV_WIDTH), 0.05),
        'rwkv_r_k': nrm(ks[17], (L, RWKV_HEADS, RWKV_HEAD_DIM), 0.1),
        'rwkv_ln_w': 1.0 + nrm(ks[18], (L, RWKV_WIDTH), 0.05),
        'rwkv_ln_b': nrm(ks[19], (L, RWKV_WIDTH), 0.02),
        'w_out': nrm(ks[20], (L, D_MIX, D_MODEL), D_MIX ** -0.5),
        'post_norm_g': 1.0 + nrm(ks[21], (L, D_MODEL), 0.05),
    }

def first_block(x, pre_norm_g, w_in, rel_bias_table, cmp_pos_k, cmp_pos_v, cmp_k_w1, cmp_k_w2,
              cmp_v_w1, cmp_v_w2, rwkv_mu, rwkv_w0, rwkv_w2, rwkv_a0, rwkv_a2, rwkv_k_k, rwkv_k_a,
              rwkv_r_k, rwkv_ln_w, rwkv_ln_b, w_out, post_norm_g):
    o1 = COL_Q
    o2 = o1 + COL_KV
    o3 = o2 + COL_GATE
    o4 = o3 + COL_ZA
    o5 = o4 + SHIFT_COLS
    h = x
    for l in range(DEPTH):
        hn = rms_norm(h, pre_norm_g[l])
        proj = hn @ w_in[l]
        q, kv6, gates, z_a, feat_b, z_b = jnp.split(proj, [o1, o2, o3, o4, o5], axis=-1)
        k_cmp, v_cmp, k_slc, v_slc, k_win, v_win = jnp.split(kv6, 6, axis=-1)
        o_a = nsa_mixer(q, k_cmp, v_cmp, k_slc, v_slc, k_win, v_win, gates, rel_bias_table,
                        cmp_pos_k[l], cmp_pos_v[l], cmp_k_w1[l], cmp_k_w2[l], cmp_v_w1[l], cmp_v_w2[l])
        o_b = rwkv7_mixer(feat_b, rwkv_mu[l], rwkv_w0[l], rwkv_w2[l], rwkv_a0[l], rwkv_a2[l],
                          rwkv_k_k[l], rwkv_k_a[l], rwkv_r_k[l], rwkv_ln_w[l], rwkv_ln_b[l])
        mix = jnp.concatenate([o_a * jax.nn.silu(z_a.astype(jnp.float32)),
                               o_b * jax.nn.silu(z_b.astype(jnp.float32))], axis=-1).astype(h.dtype)
        y = mix @ w_out[l]
        h = h + rms_norm(y, post_norm_g[l])
    return h


DEPTH_2 = 2

CHUNK = 64
Q_BLOCK = 128
N_MIXERS = 2
EPS = 1e-6

A_HEADS = 16
A_NOPE = 128
A_ROPE = 64
A_QK = A_NOPE + A_ROPE
A_V = 128
A_Q_LORA = 512
A_KV_LORA = 512
A_WIDTH = A_HEADS * A_V
A_IN = A_Q_LORA + A_KV_LORA + A_ROPE + A_WIDTH
ROPE_THETA = 10000.0

B_HEADS = 8
B_HD = 128
B_V = 2 * B_HD
B_WIDTH = B_HEADS * B_V
B_QK = B_HEADS * 2 * B_HD
B_IN = 2 * B_QK + B_WIDTH + B_WIDTH

N_A = (DEPTH_2 + 1) // 2
N_B = DEPTH_2 // 2


def rms_norm_2(x, gain):
    xf = x.astype(jnp.float32)
    y = xf * lax.rsqrt(jnp.mean(xf * xf, axis=-1, keepdims=True) + EPS)
    return (y * gain.astype(jnp.float32)).astype(x.dtype)

def rope(x, pos):
    r = x.shape[-1]
    inv_freq = ROPE_THETA ** (-jnp.arange(0, r, 2, dtype=jnp.float32) / r)
    ang = pos.astype(jnp.float32)[..., None] * inv_freq
    cos = jnp.cos(ang)[:, :, None, :]
    sin = jnp.sin(ang)[:, :, None, :]
    xf = x.astype(jnp.float32)
    x1, x2 = xf[..., : r // 2], xf[..., r // 2:]
    return jnp.concatenate([x1 * cos - x2 * sin, x1 * sin + x2 * cos], axis=-1).astype(x.dtype)

def chunk_allowed(pos_q, pos_k):
    return (pos_k // CHUNK)[:, None, :] <= (pos_q // CHUNK)[:, :, None]

def mla_attend(q, k, v, pos):
    b, s, h, d = q.shape
    nblk = s // Q_BLOCK
    scale = 1.0 / math.sqrt(d)
    k_t = k.transpose(0, 2, 1, 3)
    v_t = v.transpose(0, 2, 1, 3)
    q_blk = q.reshape(b, nblk, Q_BLOCK, h, d).transpose(1, 0, 3, 2, 4)
    p_blk = pos.reshape(b, nblk, Q_BLOCK).transpose(1, 0, 2)

    def one_block(args):
        qi, pi = args
        sc = jnp.einsum('bhqd,bhkd->bhqk', qi, k_t).astype(jnp.float32) * scale
        sc = jnp.where(chunk_allowed(pi, pos)[:, None], sc, -jnp.inf)
        p = jax.nn.softmax(sc, axis=-1)
        return jnp.einsum('bhqk,bhkd->bhqd', p.astype(v_t.dtype), v_t)

    o = lax.map(one_block, (q_blk, p_blk))
    return o.transpose(1, 0, 3, 2, 4).reshape(b, s, h, v.shape[-1])

def diff_attend(q, k, v, pos, lam):
    b, s, h, _, d = q.shape
    nblk = s // Q_BLOCK
    scale = 1.0 / math.sqrt(d)
    slopes = 2.0 ** (-8.0 * jnp.arange(1, h + 1, dtype=jnp.float32) / h)
    k_t = k.transpose(0, 2, 3, 1, 4)
    v_t = v.transpose(0, 2, 1, 3)
    q_blk = q.reshape(b, nblk, Q_BLOCK, h, 2, d).transpose(1, 0, 3, 4, 2, 5)
    p_blk = pos.reshape(b, nblk, Q_BLOCK).transpose(1, 0, 2)

    def one_block(args):
        qi, pi = args
        sc = jnp.einsum('bhcqd,bhckd->bhcqk', qi, k_t).astype(jnp.float32) * scale
        dist = jnp.abs(pi[:, :, None] - pos[:, None, :]).astype(jnp.float32)
        bias = -slopes[None, :, None, None] * dist[:, None]
        sc = sc + bias[:, :, None]
        sc = jnp.where(chunk_allowed(pi, pos)[:, None, None], sc, -jnp.inf)
        p = jax.nn.softmax(sc, axis=-1)
        p_diff = p[:, :, 0] - lam * p[:, :, 1]
        return jnp.einsum('bhqk,bhkd->bhqd', p_diff.astype(v_t.dtype), v_t)

    o = lax.map(one_block, (q_blk, p_blk))
    return o.transpose(1, 0, 3, 2, 4).reshape(b, s, h, v.shape[-1])

def mla_layer(x, pos, norm_g, w_in, q_norm_g, w_q_up, kv_norm_g, w_kv_up, q_gain, k_gain, w_out):
    b, s, _ = x.shape
    z = rms_norm_2(x, norm_g) @ w_in
    cq, ckv, k_pe, gate = jnp.split(
        z, [A_Q_LORA, A_Q_LORA + A_KV_LORA, A_Q_LORA + A_KV_LORA + A_ROPE], axis=-1)
    q = (rms_norm_2(cq, q_norm_g) @ w_q_up).reshape(b, s, A_HEADS, A_QK)
    kv = (rms_norm_2(ckv, kv_norm_g) @ w_kv_up).reshape(b, s, A_HEADS, A_NOPE + A_V)
    k_nope, v = kv[..., :A_NOPE], kv[..., A_NOPE:]
    k = jnp.concatenate(
        [k_nope, jnp.broadcast_to(k_pe[:, :, None, :], (b, s, A_HEADS, A_ROPE))], axis=-1)
    q = rms_norm_2(q, q_gain)
    k = rms_norm_2(k, k_gain)
    q = jnp.concatenate([q[..., :A_NOPE], rope(q[..., A_NOPE:], pos)], axis=-1)
    k = jnp.concatenate([k[..., :A_NOPE], rope(k[..., A_NOPE:], pos)], axis=-1)
    o = mla_attend(q, k, v, pos).reshape(b, s, A_WIDTH)
    return x + (o * jax.nn.silu(gate)) @ w_out

def diff_layer(x, pos, layer_idx, norm_g, w_in, q_gain, k_gain, lq1, lk1, lq2, lk2, subln_g, w_out):
    b, s, _ = x.shape
    z = rms_norm_2(x, norm_g) @ w_in
    q, k, v, gate = jnp.split(z, [B_QK, 2 * B_QK, 2 * B_QK + B_WIDTH], axis=-1)
    q = rms_norm_2(q.reshape(b, s, B_HEADS, 2, B_HD), q_gain)
    k = rms_norm_2(k.reshape(b, s, B_HEADS, 2, B_HD), k_gain)
    v = v.reshape(b, s, B_HEADS, B_V)
    lam_init = 0.8 - 0.6 * math.exp(-0.3 * layer_idx)
    lam = (jnp.exp(jnp.sum(lq1.astype(jnp.float32) * lk1.astype(jnp.float32)))
           - jnp.exp(jnp.sum(lq2.astype(jnp.float32) * lk2.astype(jnp.float32))) + lam_init)
    o = diff_attend(q, k, v, pos, lam)
    o = rms_norm_2(o, subln_g) * (1.0 - lam_init)
    return x + (o.reshape(b, s, B_WIDTH) * jax.nn.silu(gate)) @ w_out

def second_inputs(seed: int = 0) -> dict:
    key = jax.random.key(seed)
    ks = jax.random.split(key, 24)
    f32 = jnp.float32

    def nrm(k, shape, scale):
        return jax.random.normal(k, shape, f32) * scale

    def gain(k, shape):
        return 1.0 + 0.02 * jax.random.normal(k, shape, f32)

    x = jax.random.normal(ks[0], (BATCH, SEQ, D_MODEL), f32)
    positions = jnp.broadcast_to(jnp.arange(SEQ, dtype=jnp.int32)[None], (BATCH, SEQ))
    return {
        "x": x,
        "positions": positions,
        "a_norm": gain(ks[1], (N_A, D_MODEL)),
        "a_w_in": nrm(ks[2], (N_A, D_MODEL, A_IN), D_MODEL ** -0.5),
        "a_q_norm": gain(ks[3], (N_A, A_Q_LORA)),
        "a_w_q_up": nrm(ks[4], (N_A, A_Q_LORA, A_HEADS * A_QK), A_Q_LORA ** -0.5),
        "a_kv_norm": gain(ks[5], (N_A, A_KV_LORA)),
        "a_w_kv_up": nrm(ks[6], (N_A, A_KV_LORA, A_HEADS * (A_NOPE + A_V)), A_KV_LORA ** -0.5),
        "a_q_gain": gain(ks[7], (N_A, A_QK)),
        "a_k_gain": gain(ks[8], (N_A, A_QK)),
        "a_w_out": nrm(ks[9], (N_A, A_WIDTH, D_MODEL), A_WIDTH ** -0.5),
        "b_norm": gain(ks[10], (N_B, D_MODEL)),
        "b_w_in": nrm(ks[11], (N_B, D_MODEL, B_IN), D_MODEL ** -0.5),
        "b_q_gain": gain(ks[12], (N_B, B_HD)),
        "b_k_gain": gain(ks[13], (N_B, B_HD)),
        "b_lambda_q1": nrm(ks[14], (N_B, B_HD), 0.1),
        "b_lambda_k1": nrm(ks[15], (N_B, B_HD), 0.1),
        "b_lambda_q2": nrm(ks[16], (N_B, B_HD), 0.1),
        "b_lambda_k2": nrm(ks[17], (N_B, B_HD), 0.1),
        "b_subln": gain(ks[18], (N_B, B_V)),
        "b_w_out": nrm(ks[19], (N_B, B_WIDTH, D_MODEL), B_WIDTH ** -0.5),
    }

def second_block(x, positions, a_norm, a_w_in, a_q_norm, a_w_q_up, a_kv_norm, a_w_kv_up,
              a_q_gain, a_k_gain, a_w_out, b_norm, b_w_in, b_q_gain, b_k_gain,
              b_lambda_q1, b_lambda_k1, b_lambda_q2, b_lambda_k2, b_subln, b_w_out):
    for i in range(DEPTH_2):
        j = i // N_MIXERS
        if i % N_MIXERS == 0:
            x = mla_layer(x, positions, a_norm[j], a_w_in[j], a_q_norm[j], a_w_q_up[j],
                          a_kv_norm[j], a_w_kv_up[j], a_q_gain[j], a_k_gain[j], a_w_out[j])
        else:
            x = diff_layer(x, positions, i, b_norm[j], b_w_in[j], b_q_gain[j], b_k_gain[j],
                           b_lambda_q1[j], b_lambda_k1[j], b_lambda_q2[j], b_lambda_k2[j],
                           b_subln[j], b_w_out[j])
    return x


def setup_inputs(seed=0):
    out = dict(first_inputs(seed))
    for name, value in second_inputs(seed + 1).items():
        if name != "x":
            out[name + "_2"] = value
    return out


def reference(
    x, pre_norm_g, w_in, rel_bias_table, cmp_pos_k, cmp_pos_v, cmp_k_w1, cmp_k_w2, cmp_v_w1,
    cmp_v_w2, rwkv_mu, rwkv_w0, rwkv_w2, rwkv_a0, rwkv_a2, rwkv_k_k, rwkv_k_a, rwkv_r_k,
    rwkv_ln_w, rwkv_ln_b, w_out, post_norm_g, positions_2, a_norm_2, a_w_in_2, a_q_norm_2,
    a_w_q_up_2, a_kv_norm_2, a_w_kv_up_2, a_q_gain_2, a_k_gain_2, a_w_out_2, b_norm_2, b_w_in_2,
    b_q_gain_2, b_k_gain_2, b_lambda_q1_2, b_lambda_k1_2, b_lambda_q2_2, b_lambda_k2_2,
    b_subln_2, b_w_out_2,
):
    x = first_block(
        x, pre_norm_g, w_in, rel_bias_table, cmp_pos_k, cmp_pos_v, cmp_k_w1, cmp_k_w2, cmp_v_w1,
        cmp_v_w2, rwkv_mu, rwkv_w0, rwkv_w2, rwkv_a0, rwkv_a2, rwkv_k_k, rwkv_k_a, rwkv_r_k,
        rwkv_ln_w, rwkv_ln_b, w_out, post_norm_g,
    )
    return second_block(
        x, positions_2, a_norm_2, a_w_in_2, a_q_norm_2, a_w_q_up_2, a_kv_norm_2, a_w_kv_up_2,
        a_q_gain_2, a_k_gain_2, a_w_out_2, b_norm_2, b_w_in_2, b_q_gain_2, b_k_gain_2,
        b_lambda_q1_2, b_lambda_k1_2, b_lambda_q2_2, b_lambda_k2_2, b_subln_2, b_w_out_2,
    )


_drawn_inputs = setup_inputs


def setup_inputs(seed=0):
    import zlib

    import numpy as np

    out = dict(_drawn_inputs(seed))
    spreads = {}
    factors = {'cmp_pos_k': 8.0,
     'rwkv_ln_b': 3.672,
     'a_norm_2': 8.0,
     'a_q_norm_2': 8.0,
     'a_kv_norm_2': 8.0,
     'a_q_gain_2': 8.0,
     'a_k_gain_2': 8.0,
     'b_norm_2': 4.89,
     'b_q_gain_2': 8.0,
     'b_k_gain_2': 8.0,
     'b_lambda_q2_2': 36.07,
     'b_lambda_k2_2': 9.693,
     'b_subln_2': 178.058,
     'b_lambda_q1_2': 2.824,
     'b_lambda_k1_2': 5.071}
    for name, (base, spread) in spreads.items():
        noise = np.random.default_rng([zlib.crc32(name.encode()), seed]).standard_normal(out[name].shape)
        drawn = base * np.exp(spread * noise) if base else spread * noise
        out[name] = __import__('jax').numpy.asarray(drawn.astype(out[name].dtype))
    for name, factor in factors.items():
        out[name] = (out[name] * factor).astype(out[name].dtype)
    return out
```

```python
from contextlib import ExitStack

import numpy as np

import concourse.bass as bass
from concourse import mybir

F32 = mybir.dt.float32
F32R = mybir.dt.float32r
I32 = mybir.dt.int32
ALU = mybir.AluOpType
ACT = mybir.ActivationFunctionType
AX = mybir.AxisListType.X

P = 128
T = 512
TB = T // P
D = 2048
KT = D // P
BIG = 1e30
MAX_FLOOR = 1e20
EPS = 1e-6

NH, NKV, HD = 8, 2, 128
CMP, STRIDE = 32, 16
NCMP = (T - CMP) // STRIDE + 1
RW = 1024
NPAIR = RW // P
CH = 64
NCH = T // CH
LEVELS = [1, 2, 4, 8, 16, 32]
GN_EPS = 64e-5
NBUCKET, MAXDIST = 32, 1024
Q0, KC0, VC0, KS0, VS0, KW0, VW0, G0 = 0, 8, 10, 12, 14, 16, 18, 20
ZA0 = 21
R0, K0, V0, WA0 = 29, 37, 45, 53
ZB0 = 54
NGATE = 24
AH, AV = 16, 128
CQ0, CKV0, KPE0, AG0 = 0, 4, 8, 9
QN0, QR0, KV0 = 25, 41, 49
BH = 8
BQ0, BK0, BV0, BG0 = 0, 16, 32, 48
LAM_INIT = 0.8 - 0.6 * float(np.exp(-0.3))
NPROJ = 81
ARENA = 16000

CONST = dict(ident=128, ones=128, bones=128, hone0=128, hone1=128, swap=128, flip=128, mt=512,
             lev=(1 + len(LEVELS)) * 128, cmask=2, rst=512, freq=1, nslope=8)


def const_cols():
    at, out = 0, {}
    for k, n in CONST.items():
        out[k] = (at, n)
        at += n
    return out, at


def constants():
    cols, n = const_cols()
    c = np.zeros((P, n), np.float32)
    i = np.arange(P)

    def put(name, a):
        at, w = cols[name]
        c[:, at:at + w] = a

    put("ident", np.eye(P))
    put("ones", 1.0)
    put("flip", np.eye(P)[::-1])
    put("bones", (i[:, None] // 64 == i[None, :] // 64))
    put("hone0", np.repeat((i < 64)[:, None], P, 1))
    put("hone1", np.repeat((i >= 64)[:, None], P, 1))
    swap = np.zeros((P, P))
    for m in range(P):
        if m % 64 < 32:
            swap[m + 32, m] = -1.0
        else:
            swap[m - 32, m] = 1.0
    put("swap", swap)
    same = i[:, None] // CH == i[None, :] // CH
    strict = same & (i[:, None] < i[None, :])
    incl = same & (i[:, None] <= i[None, :])
    put("mt", np.concatenate([strict, incl, strict, incl], 1))
    put("cmask", (i[:, None] // CH == np.arange(2)[None]))
    lev = []
    for m in LEVELS:
        low = (i[:, None] // (2 * m) == i[None, :] // (2 * m)) & (i[:, None] % (2 * m) >= m) & (i[None, :] % (2 * m) < m)
        lev += [low, low.T] if m == 1 else [low.T]
    put("lev", np.concatenate(lev, 1))
    put("rst", np.repeat((np.arange(T) % CH != 0)[None], P, 0))
    freq = np.float32(10000.0) ** (-np.arange(0, 64, 2, dtype=np.float32) / np.float32(64))
    put("freq", freq[i % 32][:, None])
    put("nslope", np.repeat(-(2.0 ** -(np.arange(1, BH + 1) * 8.0 / BH))[None], P, 0))
    dist = np.arange(-(T - 1), T)
    nd = np.maximum(dist, 0)
    nf = np.maximum(nd, 1).astype(np.float32)
    half = NBUCKET // 2
    large = half + (np.log(nf / np.float32(half)) / np.float32(np.log(MAXDIST / half)) * np.float32(half)).astype(np.int32)
    b = np.where(nd < half, nd, np.minimum(large, NBUCKET - 1))
    b = np.where(dist < 0, NBUCKET, b)
    oh = (np.arange(NBUCKET + 1)[:, None] == b[None]).astype(np.float32)
    rev = oh[:, ::-1][:, :T + P]
    return c, np.ascontiguousarray(np.concatenate([rev, oh], 1).astype(np.float32))


ROWS0 = [("pre_g", 16), ("mu", 25), ("w0", 8), ("a0", 8), ("k_k", 8), ("k_a", 8), ("r_k", 8), ("ln_w", 8),
         ("ln_b", 8), ("post_g", 16)]
ROWS1 = [("a_norm", 16), ("q_norm", 4), ("kv_norm", 4), ("q_gain", 2), ("k_gain", 2), ("b_norm", 16),
         ("bq_gain", 1), ("bk_gain", 1), ("subln", 2), ("lam", 4), ("pos_k", 32), ("pos_v", 32)]


def param_cols():
    out = {}
    for base, rows in ((0, ROWS0), (P, ROWS1)):
        at = base
        for name, n in rows:
            out[name] = at
            at += n
        assert at - base <= P
    return out


PC = param_cols()


def loop(eng, n, body):
    turns = n // 2
    if turns >= 2:
        with eng.Fori(0, turns) as it:
            body(it * 2, 0)
            body(it * 2 + 1, 1)
    else:
        turns = 0
    for i in range(2 * turns, n):
        body(i, i % 2)


class Kernel:

    def __init__(self, nc, ctx, dram):
        self.nc, self.ctx, self.d = nc, ctx, dram
        cc, nconst = const_cols()
        self.RES = self.sb("RES", [P, KT, T])
        self.XH = self.sb("XH", [P, KT, T], F32R)
        self.XL = self.sb("XL", [P, KT, T], F32R)
        self.C = self.sb("C", [P, nconst])
        self.PRM = self.sb("PRM", [P, 2 * P])
        self.WHT = self.sb("WHT", [P, 2, KT, P], F32R)
        self.WLT = self.sb("WLT", [P, 2, KT, P], F32R)
        self.STG = self.sb("STG", [P, 2, T])
        self.AR = self.sb("AR", [P, ARENA])
        self.PSB = [ctx.enter_context(nc.psum_tensor(f"PS{i}", [P, T], F32)) for i in range(8)]
        self.PROJ = nc.dram_tensor("proj_scratch", [NPROJ, P, T], F32).ap()
        self.FBIAS = nc.dram_tensor("bias_scratch", [NH, T + P], F32).ap()
        w = KT * P
        self.WRAW = [self.AR[:, j * w:(j + 1) * w].rearrange("p (k n) -> p k n", n=P) for j in range(2)]
        self.WH = [self.WHT[:, j, :, :] for j in range(2)]
        self.WL = [self.WLT[:, j, :, :] for j in range(2)]
        self.SG = [self.AR[:, 2 * w + j * T:2 * w + (j + 1) * T] for j in range(2)]
        self.cc = cc
        self.dump_res = False
        self.nt = 0
        self.ng = 0
        self.ns = 0
        s = self.sem
        self.w_loaded = [s(f"w_loaded{j}") for j in range(2)]
        self.w_hi = s("w_hi")
        self.w_split = s("w_split")
        self.tile_done = s("tile_done")
        self.bank_free = s("bank_free")
        self.sig_done = s("sig_done")
        self.stored = [s(f"stored{j}") for j in range(2)]

    def sb(self, name, shape, dt=F32):
        return self.ctx.enter_context(self.nc.sbuf_tensor(name, shape, dt))

    def sem(self, name):
        return self.ctx.enter_context(self.nc.semaphore(name))

    def c(self, name, a=0, b=None):
        at, n = self.cc[name]
        return self.C[:, at + a:at + (n if b is None else b)]

    def prm(self, name, i=0):
        return self.PRM[:, bass.ds(i + PC[name], 1)]

    def arena(self, *sizes):
        at, out = 0, []
        for n in sizes:
            out.append(self.AR[:, at:at + n])
            at += n
        assert at <= ARENA, at
        return out


def r32(ap):
    return ap.bitcast(F32R)


def f32(ap):
    return ap.bitcast(F32)


def setup(k):
    nc, d = k.nc, k.d
    X = k.AR[:, 0:TB * D].rearrange("p (b n) -> p b n", n=D)
    rows = k.AR[:, TB * D:TB * D + 2 * P].rearrange("p (b n) -> p b n", n=P)
    c_in, r_in, x_in, x_in2 = k.sem("consts_in"), k.sem("rows_in"), k.sem("x_in"), k.sem("x_in2")
    r_t, r_c = k.sem("rows_turned"), k.sem("rows_copied")
    x_t, x_c = k.sem("x_turned"), k.sem("x_copied")
    rz = k.sem("rows_zeroed")
    nrow = []

    with nc.Block() as block:
        @block.sync
        def _(sp):
            sp.dma_start(k.C[:, :], d["consts"]).then_inc(c_in, 16)
            sp.wait_ge(rz, 1)
            for b, table in ((0, ROWS0), (1, ROWS1)):
                at = 0
                for name, n in table:
                    if name in ("q_gain", "k_gain"):
                        src = d[f"a_{name}_2"]
                        parts = [(0, 0, src[0:1, 0:P]), (1, 0, src[0:1, P:192]), (1, 64, src[0:1, P:192])]
                    elif name == "lam":
                        parts = [(i, 0, d[x][0:1, :]) for i, x in enumerate(
                            ("b_lambda_q1_2", "b_lambda_k1_2", "b_lambda_q2_2", "b_lambda_k2_2"))]
                    elif name in ("pos_k", "pos_v"):
                        parts = [(0, 0, d["cmp_" + name][0, :, :])]
                    else:
                        src = {"pre_g": "pre_norm_g", "mu": "rwkv_mu", "w0": "rwkv_w0", "a0": "rwkv_a0",
                               "k_k": "rwkv_k_k", "k_a": "rwkv_k_a", "r_k": "rwkv_r_k", "ln_w": "rwkv_ln_w",
                               "ln_b": "rwkv_ln_b", "post_g": "post_norm_g", "a_norm": "a_norm_2",
                               "q_norm": "a_q_norm_2", "kv_norm": "a_kv_norm_2", "b_norm": "b_norm_2",
                               "bq_gain": "b_q_gain_2", "bk_gain": "b_k_gain_2", "subln": "b_subln_2"}[name]
                        v = d[src]
                        v = v[0, :, :].rearrange("h n -> (h n)") if name == "r_k" else v[0, :]
                        parts = [(0, 0, v.rearrange("(r c) -> r c", c=P))]
                    for r, cc, src in parts:
                        m, w = src.shape
                        sp.dma_start(rows[at + r:at + r + m, b, cc:cc + w], src).then_inc(r_in, 16)
                        nrow.append(1)
                    at += n
            sp.dma_start(X[:, 0:2, :], d["x"][0, 0:2 * P, :].rearrange("(b p) n -> p b n", p=P)).then_inc(x_in, 16)
            sp.dma_start(X[:, 2:4, :], d["x"][0, 2 * P:T, :].rearrange("(b p) n -> p b n", p=P)).then_inc(x_in2, 16)

        @block.gpsimd
        def _(pool):
            nc.gpsimd.memset(rows, 0.0).then_inc(rz, 1)
            pool.sem_inc(k.w_split, 2)
            pool.sem_inc(k.tile_done, 2)
            pool.sem_inc(k.bank_free, 2)
            pool.sem_inc(k.stored[0], 16)
            pool.sem_inc(k.stored[1], 16)

        @block.tensor
        def _(pe):
            pe.wait_ge(c_in, 16)
            pe.wait_ge(r_in, 16 * len(nrow))
            for b in range(2):
                last = nc.tensor.transpose(k.PSB[7][:, b * P:(b + 1) * P], rows[:, b, :], k.c("ident"))
            last.then_inc(r_t, 1)
            pe.wait_ge(x_in, 16)
            pe.wait_ge(x_in2, 16)
            for c in range(KT):
                if c >= 4:
                    pe.wait_ge(x_c, c - 3)
                for b in range(TB):
                    last = nc.tensor.transpose(k.PSB[c % 4][:, b * P:(b + 1) * P], X[:, b, c * P:(c + 1) * P], k.c("ident"))
                last.then_inc(x_t, 1)

        @block.vector
        def _(dve):
            dve.wait_ge(r_t, 1)
            nc.vector.tensor_copy(k.PRM[:, :], k.PSB[7][:, 0:2 * P]).then_inc(r_c, 1)

        @block.scalar
        def _(act):
            for c in range(KT):
                act.wait_ge(x_t, c + 1)
                nc.scalar.activation(k.RES[:, c, :], k.PSB[c % 4][:, :], ACT.Copy).then_inc(x_c, 1)


def norm(k, tag, n, gain, src=None, dst=0, add=False):
    nc = k.nc
    Y = k.AR[:, 0:n * T].rearrange("p (c t) -> p c t", t=T) if src is not None else k.RES
    _, sq0, sq1, t0, t1, rs, r1 = k.arena(KT * T, T, T, T, T, T, T)
    SQ, TM = (sq0, sq1), (t0, t1)
    bank = k.PSB[6]
    y_in, sq_in, sq_used = k.sem(tag + "_y_in"), k.sem(tag + "_squares"), k.sem(tag + "_summed")
    st = k.sem(tag + "_mean")
    sr = k.sem(tag + "_root")
    ri = k.sem(tag + "_rsqrt")
    tn, th, tl = k.sem(tag + "_normed"), k.sem(tag + "_hi"), k.sem(tag + "_lo")

    with nc.Block() as block:
        if src is not None:
            @block.sync
            def _(sp):
                sp.dma_start(Y, k.PROJ[src:src + n, :, :].rearrange("c p t -> p c t")).then_inc(y_in, 16)

        @block.scalar
        def _(act):
            if src is not None:
                act.wait_ge(y_in, 16)
            for c in range(n):
                if c >= 2:
                    act.wait_ge(sq_used, c - 1)
                nc.scalar.activation(SQ[c % 2], Y[:, c, :], ACT.Square).then_inc(sq_in, 1)
            act.wait_ge(st, 1)
            nc.scalar.activation(rs, r1, ACT.Sqrt).then_inc(sr, 1)
            if not add:
                for c in range(n):
                    act.wait_ge(tn, c + 1)
                    nc.scalar.activation(k.XH[:, dst + c, :], TM[c % 2], ACT.Copy).then_inc(th, 1)

        @block.tensor
        def _(pe):
            for c in range(n):
                pe.wait_ge(sq_in, c + 1)
                nc.tensor.matmul(bank[:, :], k.c("ones"), SQ[c % 2], start=(c == 0), stop=(c == n - 1)).then_inc(sq_used, 1)

        @block.vector
        def _(dve):
            dve.wait_ge(sq_used, n)
            nc.vector.tensor_scalar(r1, bank[:, :], 1.0 / (n * P), EPS, ALU.mult, ALU.add).then_inc(st, 1)
            dve.wait_ge(sr, 1)
            nc.vector.reciprocal(rs, rs).then_inc(ri, 1)
            dve.wait_ge(ri, 1)
            for c in range(n):
                g = k.prm(gain, c)
                if add:
                    nc.vector.scalar_tensor_tensor(out=TM[c % 2], in0=Y[:, c, :], scalar=g, in1=rs, op0=ALU.mult, op1=ALU.mult).then_inc(tn, 1)
                    dve.wait_ge(tn, c + 1)
                    nc.vector.tensor_tensor(k.RES[:, c, :], k.RES[:, c, :], TM[c % 2], ALU.add).then_inc(tl, 1)
                    if c < n - 1:
                        dve.wait_ge(tl, c + 1)
                    continue
                if c >= 2:
                    dve.wait_ge(tl, c - 1)
                nc.vector.scalar_tensor_tensor(out=TM[c % 2], in0=Y[:, c, :], scalar=g, in1=rs, op0=ALU.mult, op1=ALU.mult).then_inc(tn, 1)
                if c >= 1:
                    b = c - 1
                    dve.wait_ge(th, b + 1)
                    nc.vector.tensor_tensor(k.XL[:, dst + b, :], TM[b % 2], f32(k.XH[:, dst + b, :]), ALU.subtract).then_inc(tl, 1)
            if not add:
                dve.wait_ge(th, n)
                nc.vector.tensor_tensor(k.XL[:, dst + n - 1, :], TM[(n - 1) % 2], f32(k.XH[:, dst + n - 1, :]), ALU.subtract).then_inc(tl, 1)


def project(k, segments, kt, rhs0=0, add=False):
    nc = k.nc
    plan = []
    nt, ns, ng = k.nt, k.ns, k.ng
    for n, out, load, width, func in segments:
        plan.append((n, out, load, width, nt, ns, func, ng))
        ng += n if func else 0
        nt += n
        if not add:
            ns += n
    k.nt, k.ns, k.ng = nt, ns, ng

    with nc.Block() as block:
        @block.sync
        def _(sp):
            for n, out, load, width, b, s, func, ng0 in plan:
                def step(i, par):
                    j = (b + par) % 2
                    sp.wait_ge(k.w_split, i + (b + 1))
                    for dst, src in load(k.WRAW[j], i):
                        sp.dma_start(dst, src).then_inc(k.w_loaded[j], 16)
                loop(sp, n, step)
            if not add:
                for j in range(2):
                    done = sum(1 for x in range(ns) if x % 2 == j)
                    sp.wait_ge(k.stored[j], 16 * done + 16)

        @block.scalar
        def _(act):
            flat = [(p, i) for p in plan for i in range(p[0])]

            def hi(i, par, p):
                b = p[4]
                j = (b + par) % 2
                act.wait_ge(k.w_loaded[j], (i - par) * 16 + 32 * ((b + par) // 2 + 1))
                act.wait_ge(k.tile_done, i + (b + 1))
                nc.scalar.activation(k.WH[j][:, 0:kt, 0:p[3]], k.WRAW[j][:, 0:kt, 0:p[3]], ACT.Copy).then_inc(k.w_hi, 1)

            def sigmoid(i, par, p):
                act.wait_ge(k.tile_done, i + (p[4] + 3))
                j = (p[4] + par) % 2
                nc.scalar.activation(k.SG[j][0:p[3], :], k.PSB[j][0:p[3], :], ACT.Sigmoid).then_inc(k.sig_done, 1)

            def store(i, par, p):
                if p[6]:
                    sigmoid(i, par, p)
                act.wait_ge(k.bank_free, i + (p[4] + 3))
                act.dma_start(k.PROJ[p[1] + i, 0:p[3], :], k.STG[0:p[3], (p[5] + par) % 2, :]).then_inc(k.stored[(p[5] + par) % 2], 16)

            hi(0, 0, plan[0])
            for x, p in enumerate(plan):
                def step(i, par):
                    hi(i + 1, 1 - par if par == 0 else 2, p)
                    if not add:
                        store(i, par, p)
                loop(act, p[0] - 1, step)
                last = p[0] - 1
                if x + 1 < len(plan):
                    hi(0, 0, plan[x + 1])
                if not add:
                    store(last, last % 2, p)

        @block.vector
        def _(dve):
            def lo(i, par, p):
                j = (p[4] + par) % 2
                dve.wait_ge(k.w_hi, i + (p[4] + 1))
                nc.vector.tensor_tensor(k.WL[j][:, 0:kt, 0:p[3]], k.WRAW[j][:, 0:kt, 0:p[3]], f32(k.WH[j][:, 0:kt, 0:p[3]]), ALU.subtract).then_inc(k.w_split, 1)

            def evac(i, par, p):
                bank = k.PSB[(p[4] + par) % 2]
                dve.wait_ge(k.tile_done, i + (p[4] + 3))
                if add:
                    nc.vector.tensor_tensor(k.RES[:, i, :], bank[:, :], k.RES[:, i, :], ALU.add).then_inc(k.bank_free, 1)
                else:
                    s = (p[5] + par) % 2
                    dve.wait_ge(k.stored[s], (i - par) * 8 + 16 * ((p[5] + par) // 2 + 1))
                    sg = k.SG[(p[4] + par) % 2][0:p[3], :]
                    if p[6]:
                        dve.wait_ge(k.sig_done, i + (p[7] + 1))
                    if p[6] == "silu":
                        nc.vector.tensor_tensor(k.STG[0:p[3], s, :], bank[0:p[3], :], sg, ALU.mult).then_inc(k.bank_free, 1)
                    elif p[6] == "sigmoid":
                        nc.vector.tensor_copy(k.STG[0:p[3], s, :], sg).then_inc(k.bank_free, 1)
                    else:
                        nc.vector.tensor_copy(k.STG[0:p[3], s, :], bank[0:p[3], :]).then_inc(k.bank_free, 1)

            lo(0, 0, plan[0])
            for x, p in enumerate(plan):
                def step(i, par):
                    lo(i + 1, 1 - par if par == 0 else 2, p)
                    evac(i, par, p)
                loop(dve, p[0] - 1, step)
                last = p[0] - 1
                if x + 1 < len(plan):
                    lo(0, 0, plan[x + 1])
                evac(last, last % 2, p)

        @block.tensor
        def _(pe):
            for n, out, load, width, b, s, func, ng0 in plan:
                def step(i, par):
                    j = (b + par) % 2
                    pe.wait_ge(k.w_split, i + (b + 3))
                    pe.wait_ge(k.bank_free, i + (b + 1))
                    bank = k.PSB[j]
                    for c in range(kt):
                        wh, wl = k.WH[j][:, c, 0:width], k.WL[j][:, c, 0:width]
                        xh, xl = k.XH[:, rhs0 + c, :], k.XL[:, rhs0 + c, :]
                        nc.tensor.matmul(bank[0:width, :], wh, xh, start=(c == 0), stop=False)
                        nc.tensor.matmul(bank[0:width, :], wh, xl, start=False, stop=False)
                        last = nc.tensor.matmul(bank[0:width, :], wl, xh, start=False, stop=(c == kt - 1))
                    last.then_inc(k.tile_done, 1)
                loop(pe, n, step)


def columns(w, c0, step=P, width=P):
    half = w.shape[0] // P // 2

    def load(dst, i):
        src = w[:, bass.ds(i * step + c0, width)].rearrange("(k p) n -> p k n", p=P)
        return [(dst[:, a:a + half, 0:width], src[:, a:a + half, :]) for a in (0, half)]
    return load


def rope_columns(w):
    def load(dst, i):
        return [(dst[:, 0:w.shape[0] // P, 64 * e:64 * e + 64],
                 w[:, bass.ds(i * 384 + (192 * e + 128), 64)].rearrange("(k p) n -> p k n", p=P)) for e in (0, 1)]
    return load


def nsa_setup(k):
    nc, d = k.nc, k.d
    A = nsa_arena(k)
    E, BC, KCT, VC, G, VT = A["E"], A["BC"], A["KCT"], A["VC"], A["G"], A["VT"]
    OH, W1, W2, KV, CST, SIGM, HB, VIN, FB, TAB = (A[x] for x in ("OH", "W1", "W2", "KV", "CST", "SIGM", "HB", "VIN", "FB", "TAB"))
    NC2 = NKV * NCMP
    tab0, tab_in, oh_in = k.sem("table_padded"), k.sem("table_in"), k.sem("onehot_in")
    fb_mm, fb_c, fb_out, e_in = k.sem("bias_row"), k.sem("bias_row_copied"), k.sem("bias_row_out"), k.sem("bias_in")
    bc_mm, bc_c = k.sem("cmp_bias"), k.sem("cmp_bias_copied")
    w1_in, kv_in = k.sem("cmp_w_in"), k.sem("cmp_kv_in")
    h_mm, c_c, s_s, hb, o_mm, o_c = (k.sem("cmp_" + x) for x in ("hidden", "const", "sigmoid", "silu", "out", "copied"))
    v_in, v_t, v_c = k.sem("nsa_v_in"), k.sem("nsa_v_turned"), k.sem("nsa_v_copied")
    z0 = k.sem("cmp_zeroed")
    e_mm, e_c = k.sem("bias_flipped"), k.sem("bias_copied")
    W1F = W1.rearrange("p l e -> p (l e)").rearrange("p (h m) -> p h m", m=T)
    VTILES = [KS0 + 2, KS0 + 3, KW0 + 2, KW0 + 3, G0]

    with nc.Block() as block:
        @block.sync
        def _(sp):
            sp.dma_start(OH, d["onehot"]).then_inc(oh_in, 16)
            sp.wait_ge(tab0, 1)
            sp.dma_start(TAB[0:NBUCKET, :], d["rel_bias_table"]).then_inc(tab_in, 16)
            for n, (c0, w1, w2) in enumerate(((KC0, "cmp_k_w1", "cmp_k_w2"), (VC0, "cmp_v_w1", "cmp_v_w2"))):
                if n:
                    sp.wait_ge(o_mm, 1)
                for a in range(0, CMP, 16):
                    sp.dma_start(W1[:, a:a + 16, :], d[w1][0, a * P:(a + 16) * P, :].rearrange("(l p) e -> p l e", p=P)).then_inc(w1_in, 16)
                sp.dma_start(W2, d[w2][0, :, :]).then_inc(w1_in, 16)
                sp.dma_start(KV, k.PROJ[c0:c0 + 2, :, :].rearrange("g p t -> p g t")).then_inc(kv_in, 16)
            sp.wait_ge(fb_c, 2)
            sp.dma_start(k.FBIAS, FB[0:NH, :]).then_inc(fb_out, 16)
            sp.wait_ge(fb_out, 16)
            sp.wait_ge(o_mm, 2)
            sp.dma_start(W1F, bass.AP(k.FBIAS.tensor, 0, [[1, P], [T + P, NH], [1, T]])).then_inc(e_in, 16)

        @block.gpsimd
        def _(pool):
            nc.gpsimd.memset(TAB, -BIG).then_inc(tab0, 1)
            nc.gpsimd.memset(VC, 0.0).then_inc(z0, 1)
            for n, c in enumerate(VTILES):
                if n >= 2:
                    pool.wait_ge(v_t, n - 1)
                rows = NGATE if c == G0 else P
                pool.dma_start(VIN[0:rows, n % 2, :], k.PROJ[c, 0:rows, :]).then_inc(v_in, 16)
                pool.wait_ge(v_in, 16 * n + 16)

        @block.tensor
        def _(pe):
            pe.wait_ge(tab_in, 16)
            pe.wait_ge(oh_in, 16)
            nc.tensor.matmul(k.PSB[0][0:NH, :], TAB, OH[:, 0:T], start=True, stop=True).then_inc(fb_mm, 1)
            nc.tensor.matmul(k.PSB[1][0:NH, 0:P], TAB, OH[:, T:T + P], start=True, stop=True).then_inc(fb_mm, 1)
            for tb in range(TB):
                if tb >= 2:
                    pe.wait_ge(bc_c, tb - 1)
                for i in range(NCMP):
                    c = T + P + (T - 1) + tb * P - (STRIDE * i + CMP - 1)
                    last = nc.tensor.matmul(k.PSB[2 + tb % 2][:, i * NH:(i + 1) * NH], OH[:, c:c + P], TAB, start=True, stop=True)
                last.then_inc(bc_mm, 1)
            for n in range(2):
                pe.wait_ge(w1_in, 48 * (n + 1))
                pe.wait_ge(kv_in, 16 * (n + 1))
                if n:
                    pe.wait_ge(hb, 1)
                for l in range(CMP):
                    nc.tensor.matmul(k.PSB[4][:, 0:NC2].rearrange("p (g i) -> p g i", i=NCMP), W1[:, l, :], KV[:, :, l:l + STRIDE * (NCMP - 1) + 1:STRIDE], start=(l == 0), stop=(l == CMP - 1))
                for l in range(CMP):
                    last = nc.tensor.matmul(k.PSB[5][:, 0:1], W1[:, l, :], k.prm(("pos_k", "pos_v")[n], l), start=(l == 0), stop=(l == CMP - 1))
                last.then_inc(h_mm, 1)
                pe.wait_ge(hb, n + 1)
                if n == 0:
                    nc.tensor.matmul(k.PSB[6][:, 0:NC2], W2, HB, start=True, stop=True).then_inc(o_mm, 1)
                else:
                    pe.wait_ge(o_c, 1)
                    for g in range(NKV):
                        last = nc.tensor.matmul(k.PSB[6][0:NCMP, g * HD:(g + 1) * HD], HB[:, g * NCMP:(g + 1) * NCMP], W2, start=True, stop=True)
                    last.then_inc(o_mm, 1)
            for n, c in enumerate(VTILES):
                pe.wait_ge(v_in, 16 * (n + 1))
                if n >= 2:
                    pe.wait_ge(v_c, n - 1)
                rows = NGATE if c == G0 else P
                for tb in range(TB):
                    last = nc.tensor.transpose(k.PSB[n % 2][:, tb * P:tb * P + rows], VIN[0:rows, n % 2, tb * P:(tb + 1) * P], k.c("ident")[0:rows, 0:rows])
                last.then_inc(v_t, 1)
            pe.wait_ge(e_in, 16)
            pe.wait_ge(bc_c, TB)
            for h in range(NH):
                if h >= 2:
                    pe.wait_ge(e_c, h - 1)
                nc.tensor.matmul(k.PSB[2 + h % 2][:, :], k.c("flip"), W1F[:, h, :], start=True, stop=True).then_inc(e_mm, 1)

        @block.vector
        def _(dve):
            dve.wait_ge(fb_mm, 2)
            nc.vector.tensor_copy(FB[0:NH, 0:T], k.PSB[0][0:NH, :]).then_inc(fb_c, 1)
            nc.vector.tensor_copy(FB[0:NH, T:T + P], k.PSB[1][0:NH, 0:P]).then_inc(fb_c, 1)
            for tb in range(TB):
                dve.wait_ge(bc_mm, tb + 1)
                nc.vector.tensor_copy(BC[:, tb, :], k.PSB[2 + tb % 2][:, 0:NCMP * NH]).then_inc(bc_c, 1)
            for n in range(2):
                dve.wait_ge(h_mm, n + 1)
                if n:
                    dve.wait_ge(s_s, 1)
                nc.vector.tensor_copy(CST, k.PSB[5][:, 0:1]).then_inc(c_c, 1)
                dve.wait_ge(s_s, n + 1)
                if n:
                    dve.wait_ge(o_mm, 1)
                nc.vector.scalar_tensor_tensor(out=HB, in0=k.PSB[4][:, 0:NC2], scalar=CST, in1=SIGM, op0=ALU.add, op1=ALU.mult).then_inc(hb, 1)
                dve.wait_ge(o_mm, n + 1)
                if n == 0:
                    nc.vector.tensor_copy(KCT, k.PSB[6][:, 0:NC2]).then_inc(o_c, 1)
                else:
                    dve.wait_ge(z0, 1)
                    nc.vector.tensor_copy(VC[0:NCMP, :], k.PSB[6][0:NCMP, 0:NKV * HD]).then_inc(o_c, 1)
            for n, c in enumerate(VTILES):
                dve.wait_ge(v_t, n + 1)
                src = k.PSB[n % 2][:, :].rearrange("p (b c) -> p b c", c=P)
                if c == G0:
                    nc.vector.tensor_copy(G, src[:, :, 0:NGATE]).then_inc(v_c, 1)
                else:
                    nc.vector.tensor_copy(VT[:, n // 2, n % 2, :, :], src).then_inc(v_c, 1)
            for h in range(NH):
                dve.wait_ge(e_mm, h + 1)
                nc.vector.tensor_copy(E[:, h, :], k.PSB[2 + h % 2][:, :]).then_inc(e_c, 1)

        @block.scalar
        def _(act):
            for n in range(2):
                act.wait_ge(c_c, n + 1)
                if n:
                    act.wait_ge(hb, 1)
                nc.scalar.activation(SIGM, k.PSB[4][:, 0:NC2], ACT.Sigmoid, bias=CST).then_inc(s_s, 1)


def nsa_arena(k):
    parts = dict(E=NH * T, BC=TB * NCMP * NH, KCT=64, VC=NKV * HD, G=TB * NGATE, VT=4 * TB * HD)
    at = dict(zip(parts, k.arena(*parts.values())))
    used = sum(parts.values())
    free = k.AR[:, used:ARENA]

    def lay(sizes):
        o, out = 0, {}
        for n, w in sizes.items():
            out[n] = free[:, o:o + w]
            o += w
        assert o <= ARENA - used, (o, ARENA - used)
        return out

    s = lay(dict(W1=CMP * P, W2=P, KV=NKV * T, CST=1, SIGM=NKV * NCMP, HB=NKV * NCMP, TAB=NH, FB=T + P))
    OHW = T + P + 2 * T - 1
    h = lay(dict(KK=4 * T, S=2 * T, PT=4 * T, PTC=T, MX=24, Z=T, TM=T))
    A = dict(E=at["E"].rearrange("p (h m) -> p h m", m=T), BC=at["BC"].rearrange("p (b n) -> p b n", n=NCMP * NH),
             KCT=at["KCT"][:, 0:NKV * NCMP], VC=at["VC"], G=at["G"].rearrange("p (b n) -> p b n", n=NGATE),
             VT=at["VT"].rearrange("p (r g b d) -> p r g b d", r=2, g=NKV, b=TB),
             )
    A.update(W1=s["W1"].rearrange("p (l e) -> p l e", e=P), W2=s["W2"], KV=s["KV"].rearrange("p (g t) -> p g t", t=T),
             CST=s["CST"], SIGM=s["SIGM"], HB=s["HB"], TAB=s["TAB"][0:NBUCKET + 1, :], FB=s["FB"])
    A["OH"] = at["E"][0:NBUCKET + 1, 0:OHW]
    A["VIN"] = k.STG
    A["KK"] = h["KK"].rearrange("p (r g t) -> p r g t", r=2, g=NKV)
    A["S"] = h["S"].rearrange("p (j t) -> p j t", t=T)
    A["PT"] = h["PT"].rearrange("p (b t) -> p b t", t=T)
    A["PTC"], A["MX"], A["Z"], A["TM"] = h["PTC"], h["MX"], h["Z"], h["TM"]
    A["Q"] = k.STG
    return A


def nsa_heads(k):
    nc, d = k.nc, k.d
    A = nsa_arena(k)
    E, BC, KCT, VC, G, VT = A["E"], A["BC"], A["KCT"], A["VC"], A["G"], A["VT"]
    KK, S, PT, PTC, MX, Z, TM, Q = (A[x] for x in ("KK", "S", "PT", "PTC", "MX", "Z", "TM", "Q"))
    SCALE = HD ** -0.5
    BR = [(br, tb) for br in range(2) for tb in range(TB)] + [(2, tb) for tb in range(TB)]
    NI = len(BR)
    HG = NH // NKV
    kk_in = k.sem("nsa_k_in")
    q_in = [k.sem(f"nsa_q_in{j}") for j in range(2)]
    z_in = k.sem("nsa_z_in")
    s_mm, s_b, s_max, s_exp = (k.sem("nsa_" + x) for x in ("scores", "biased", "max", "probs"))
    s_sum, s_rec, s_gate, s_p = (k.sem("nsa_" + x) for x in ("sum", "recip", "factor", "scaled"))
    s_red = k.sem("nsa_reduced")
    s_tr, s_pt = k.sem("nsa_turned"), k.sem("nsa_pt")
    s_pv = k.sem("nsa_pv")
    s_out, s_xh, s_xl = k.sem("nsa_out"), k.sem("nsa_hi"), k.sem("nsa_lo")
    s_z0 = k.sem("nsa_ptc_zero")

    def wid(br, tb):
        return NCMP if br == 2 else (tb + 1) * P

    with nc.Block() as block:
        @block.sync
        def _(sp):
            for r, c0 in ((0, KS0), (1, KW0)):
                sp.dma_start(KK[:, r, :, :], k.PROJ[c0:c0 + 2, :, :].rearrange("g p t -> p g t")).then_inc(kk_in, 16)

            def step(h, par):
                sp.wait_ge(s_mm, h * NI + 1)
                sp.dma_start(Q[:, par, :], k.PROJ[Q0 + h, :, :]).then_inc(q_in[par], 16)
                sp.wait_ge(s_out, h + 1)
                sp.dma_start(Z, k.PROJ[ZA0 + h, :, :]).then_inc(z_in, 16)
            loop(sp, NH, step)

        @block.tensor
        def _(pe):
            pe.sem_inc(s_mm, NI + 1)
            pe.sem_inc(s_pv, 1)
            pe.wait_ge(kk_in, 32)

            def head(h, par, g):
                b = h * NI
                O = k.PSB[4 + par]

                def scores(n):
                    br, tb = BR[n]
                    pe.wait_ge(s_b, b + (n + 1))
                    if n == 0:
                        pe.wait_ge(q_in[par], (h - par) * 8 + 16)
                    q = Q[:, par, tb * P:(tb + 1) * P]
                    rhs = KCT[:, g * NCMP:(g + 1) * NCMP] if br == 2 else KK[:, br, g, 0:wid(br, tb)]
                    nc.tensor.matmul(k.PSB[n % 2][:, 0:wid(br, tb)], q, rhs, start=True, stop=True).then_inc(s_mm, 1)

                def turn(n):
                    br, tb = BR[n]
                    pe.wait_ge(s_p, b + (n + 1))
                    pe.wait_ge(s_pt, b + (n + 1))
                    for kb in range(1 if br == 2 else tb + 1):
                        w = NCMP if br == 2 else P
                        last = nc.tensor.transpose(k.PSB[2 + n % 2][0:w, kb * P:(kb + 1) * P], S[:, n % 2, kb * P:kb * P + w], k.c("ident"))
                    last.then_inc(s_tr, 1)

                def values(br):
                    pe.wait_ge(s_pt, b + (4 * br + 4 + 2))
                    if br == 0:
                        pe.wait_ge(s_out, h + 1)
                    if br < 2:
                        for kb in range(TB):
                            last = nc.tensor.matmul(O[:, kb * P:T], VT[:, br, g, kb, :], PT[:, kb, kb * P:T], start=(br == 0 and kb == 0), stop=False)
                    else:
                        last = nc.tensor.matmul(O[:, :], VC[:, g * HD:(g + 1) * HD], PTC, start=False, stop=True)
                    last.then_inc(s_pv, 1)

                scores(0)
                for n in range(NI):
                    if n + 1 < NI:
                        scores(n + 1)
                    turn(n)
                    if n % 4 == 3:
                        values(n // 4)
            for g in range(NKV):
                if g == 0:
                    loop(pe, HG, lambda i, par: head(i, par, 0))
                else:
                    loop(pe, HG, lambda i, par: head(i + HG, par, 1))

        @block.vector
        def _(dve):
            dve.sem_inc(s_b, 2)
            dve.sem_inc(s_out, 1)
            nc.vector.memset(PTC, 0.0).then_inc(s_z0, 1)

            def head(h, par):
                b = h * NI

                def bias(n):
                    br, tb = BR[n]
                    w = wid(br, tb)
                    dve.wait_ge(s_mm, b + (n + NI + 2))
                    dve.wait_ge(s_tr, b + (n + 1))
                    bb = BC[:, tb, :].rearrange("p (i h) -> p h i", h=NH)[:, h, :] if br == 2 else E[:, h, (TB - 1 - tb) * P:T]
                    nc.vector.scalar_tensor_tensor(out=S[:, n % 2, 0:w], in0=k.PSB[n % 2][:, 0:w], scalar=SCALE, in1=bb, op0=ALU.mult, op1=ALU.add).then_inc(s_b, 1)
                    dve.wait_ge(s_b, b + (n + 3))
                    nc.vector.tensor_reduce(MX[:, n % 2:n % 2 + 1], S[:, n % 2, 0:w], AX, ALU.max, negate=True).then_inc(s_red, 1)
                    dve.wait_ge(s_red, b + (n + 1))
                    nc.vector.tensor_scalar(MX[:, 4 + n % 2:5 + n % 2], MX[:, n % 2:n % 2 + 1], MAX_FLOOR, None, ALU.min).then_inc(s_max, 1)

                def scale(n):
                    br, tb = BR[n]
                    w = wid(br, tb)
                    j = n % 2
                    dve.wait_ge(s_exp, b + (n + 1))
                    nc.vector.tensor_scalar(MX[:, 12 + j:13 + j], MX[:, 8 + j:9 + j], 1e-30, None, ALU.max).then_inc(s_sum, 1)
                    dve.wait_ge(s_sum, b + (n + 1))
                    nc.vector.reciprocal(MX[:, 16 + j:17 + j], MX[:, 12 + j:13 + j]).then_inc(s_rec, 1)
                    dve.wait_ge(s_rec, b + (n + 1))
                    gc = {0: 1, 1: 2, 2: 0}[br] * NH
                    nc.vector.tensor_tensor(MX[:, 20 + j:21 + j], MX[:, 16 + j:17 + j], G[:, tb, bass.ds(h + gc, 1)], ALU.mult).then_inc(s_gate, 1)
                    dve.wait_ge(s_gate, b + (n + 1))
                    nc.vector.tensor_scalar(S[:, j, 0:w], S[:, j, 0:w], MX[:, 20 + j:21 + j], None, ALU.mult).then_inc(s_p, 1)

                bias(0)
                for n in range(NI):
                    if n + 1 < NI:
                        bias(n + 1)
                    scale(n)
                dve.wait_ge(s_pv, h * 3 + 4)
                dve.wait_ge(z_in, h * 16 + 16)
                dve.wait_ge(s_xl, h + 1)
                nc.vector.tensor_tensor(TM, k.PSB[4 + par][:, :], Z, ALU.mult).then_inc(s_out, 1)
                dve.wait_ge(s_xh, h + 1)
                nc.vector.tensor_tensor(k.XL[:, h, :], TM, f32(k.XH[:, h, :]), ALU.subtract).then_inc(s_xl, 1)
            loop(dve, NH, head)

        @block.scalar
        def _(act):
            act.sem_inc(s_pt, 2)
            act.sem_inc(s_tr, 2)
            act.sem_inc(s_xl, 1)
            act.wait_ge(s_z0, 1)

            def head(h, par):
                b = h * NI

                def exps(n):
                    br, tb = BR[n]
                    w = wid(br, tb)
                    j = n % 2
                    act.wait_ge(s_max, b + (n + 1))
                    nc.scalar.activation(S[:, j, 0:w], S[:, j, 0:w], ACT.Exp, bias=MX[:, 4 + j:5 + j], accum_out=MX[:, 8 + j:9 + j]).then_inc(s_exp, 1)

                def copy(n):
                    br, tb = BR[n]
                    act.wait_ge(s_tr, b + (n + 3))
                    if n % 4 == 0:
                        act.wait_ge(s_pv, h * 3 + (2 if br == 1 else 1))
                    if br == 2:
                        nc.scalar.activation(PTC[0:NCMP, tb * P:(tb + 1) * P], k.PSB[2 + n % 2][0:NCMP, 0:P], ACT.Copy).then_inc(s_pt, 1)
                    else:
                        nc.scalar.activation(PT[:, 0:tb + 1, tb * P:(tb + 1) * P], k.PSB[2 + n % 2][:, 0:(tb + 1) * P].rearrange("p (b t) -> p b t", t=P), ACT.Copy).then_inc(s_pt, 1)

                exps(0)
                for n in range(NI):
                    if n + 1 < NI:
                        exps(n + 1)
                    copy(n)
                act.wait_ge(s_out, h + 2)
                nc.scalar.activation(k.XH[:, h, :], TM, ACT.Copy).then_inc(s_xh, 1)
            loop(act, NH, head)


class Steps:

    def __init__(self, k, tag, **order):
        self.order = {e: {n: j for j, n in enumerate(names)} for e, names in order.items()}
        self.sem = {e: k.sem(f"{tag}_{e}") for e in order}
        self.n = {e: len(names) for e, names in order.items()}
        for e, names in order.items():
            assert len(set(names)) == len(names)
        self.next = dict.fromkeys(order, 0)

    def begin(self, eng, e):
        eng.sem_inc(self.sem[e], 1)

    def turn(self, eng, i, *engines):
        for e in engines:
            eng.wait_ge(self.sem[e], i * self.n[e] + 1)

    def wait(self, eng, i, *steps):
        for s in steps:
            e, name = s.split(".")
            eng.wait_ge(self.sem[e], i * self.n[e] + (self.order[e][name] + 2))

    def did(self, instruction, e, name):
        assert self.order[e][name] == self.next[e] % self.n[e], (e, name, self.next[e] % self.n[e])
        self.next[e] += 1
        instruction.then_inc(self.sem[e], 1)


def rwkv(k):
    nc, d = k.nc, k.d
    o = [0]

    def take(n):
        o[0] += n
        assert o[0] <= ARENA, o[0]
        return k.AR[:, o[0] - n:o[0]]

    AR = take(2 * T).rearrange("p (j t) -> p j t", t=T)
    BZ = take(2 * T).rearrange("p (e t) -> p e t", t=T)
    KZ = take(2 * T).rearrange("p (e t) -> p e t", t=T)
    TOK = take(4 * T).rearrange("p (n b f) -> p n b f", n=4, f=P)
    BON = take(T)
    WC = take(NCH)
    TW = take(T)
    W2 = take(P)
    GTI = take(NCH * P).rearrange("p (c f) -> p c f", f=P)
    HB = take(NCH * P).rearrange("p (c f) -> p c f", f=P)
    ST = take(NCH * P).rearrange("p (c f) -> p c f", f=P)
    base = o[0]
    IN = take(3 * (T + 1)).rearrange("p (n t) -> p n t", t=T + 1)
    M = take(3 * T).rearrange("p (n t) -> p n t", t=T)
    DT, F1, F2, F3, F4 = (take(T) for _ in range(5))
    end_a = o[0]
    flat = k.AR[:, base:base + 3 * (T + 1)]
    EW, EWI, EWP = (flat[:, n * T:(n + 1) * T] for n in range(3))
    o[0] = base
    GB = take(TB * T).rearrange("p (b n) -> p b n", n=T)
    LOT = [take(T).rearrange("p (b n) -> p b n", n=P) for _ in range(2)]
    T_, TT, X, BTZ = (take(T).rearrange("p (b n) -> p b n", n=P) for _ in range(4))
    UVA, P1TA, P1Z, VZ = X, T_, LOT[0], LOT[1]
    gbf = GB.rearrange("p b n -> p (b n)")
    SQ, VE, Z = gbf[:, 0:T], gbf[:, T:2 * T], gbf[:, 2 * T:3 * T]
    QT, Y = k.STG[:, 0, :], k.STG[:, 1, :]
    LW, AS, KK, SQN = F1, F2, F3, F4
    L = DT
    NL = len(LEVELS)
    C = k.c
    B = k.PSB

    heads = range(2)
    dve = ["z0"] + [f"{x}{n}" for n in "rkv" for x in ("d", "m")] + ["kk", "lw", "scan", "lp", "nmax", "nrec", "kn", "am", "kp", "at", "ba", "bt", "kt", "bz0", "bz1", "kz0", "kz1", "rt", "wc", "bo", "bon", "tokA", "tokB"]
    for e in heads:
        dve += [f"gb{e}{b}" for b in range(TB)] + [f"t0a{e}", f"t0b{e}", f"tt0a{e}", f"tt0b{e}"]
        for l in range(1, NL):
            dve += ([f"ta{e}{l}"] if l < NL - 1 else []) + [f"tta{e}{l}"]
        dve += [f"gti{e}", f"hb{e}"]
    dve += ["st0", "st1", "qt", "yv"] + [f"su{c}" for c in range(1, NCH - 1)] + ["yy", "yc", "ve", "vrec", "yn", "yb", "yz", "xl"]
    act = ["sgw", "sga", "sqk", "sqrt", "ew", "ewi", "ewp", "tokK", "tokV"]
    for e in heads:
        act += [f"xc{e}{l}" for l in range(1, NL)] + [f"uvc{e}", f"ptc{e}"]
    act += ["sqy", "vsqrt", "xh"]
    pe_ = ["zw", "za", "ss", "bs", "tA", "tB", "tK", "tV"]
    for e in heads:
        pe_ += [f"g{e}{b}" for b in range(TB)] + [f"lm{e}"]
        for l in range(1, NL):
            pe_ += [f"x{e}{l}"] + ([f"tx{e}{l}"] if l < NL - 1 else []) + [f"xt{e}{l}"]
        pe_ += [f"uv{e}", f"pt{e}", f"q{e}", f"y{e}", f"gt{e}", f"h{e}"]
    pe_ += [f"s{c}" for c in range(1, NCH - 1)] + ["yf", "mean", "var"]
    pool_ = []
    for e in heads:
        pool_ += [f"lot{e}{l}" for l in range(1, NL)] + [f"btz{e}", f"uva{e}", f"vz{e}", f"p1z{e}"]
    S = Steps(k, "rwkv", dve=dve, act=act, pe=pe_, pool=pool_)
    w_in, w_m, w_t, zeroed = k.sem("rwkv_lora_in"), k.sem("rwkv_lora_mixed"), k.sem("rwkv_lora_tanh"), k.sem("rwkv_zeroed")
    ld, z_in, col_zero = k.sem("rwkv_in"), k.sem("rwkv_z_in"), k.sem("rwkv_col_zero")

    def blk(b):
        return slice(b * P, (b + 1) * P)

    def rows(e):
        return slice(64 * e, 64 * e + 64)

    def lev(n):
        return C("lev", n * P, (n + 1) * P).unsqueeze(1).broadcast_to([P, TB, P])

    def ident4():
        return C("ident").unsqueeze(1).broadcast_to([P, TB, P])

    with nc.Block() as block:
        @block.sync
        def _(sp):
            sp.dma_start(IN[:, 0, 1:T + 1], k.PROJ[WA0, :, :]).then_inc(w_in, 16)
            sp.wait_ge(w_m, 2)

            def pair(i, par):
                S.turn(sp, i, "dve", "act", "pe", "pool")
                for n, c0 in enumerate((R0, K0, V0)):
                    sp.dma_start(IN[:, n, 1:T + 1], k.PROJ[c0 + i, :, :]).then_inc(ld, 16)
                for e, w in ((0, "rwkv_w2"), (1, "rwkv_a2")):
                    sp.dma_start(W2[rows(e), :], d[w][0, :, bass.ds(i * P, P)]).then_inc(ld, 16)
                S.wait(sp, i, "pe.y1")
                sp.dma_start(Z, k.PROJ[ZB0 + i, :, :]).then_inc(z_in, 16)
            loop(sp, NPAIR, pair)

        @block.gpsimd
        def _(pool):
            for buf in (BZ, KZ, GTI, HB):
                nc.gpsimd.memset(buf, 0.0).then_inc(zeroed, 1)
            S.begin(pool, "pool")

            def mask(out, in_, e, name):
                src = in_.unsqueeze(2).broadcast_to([P, TB, 2, 64])
                m = C("cmask").unsqueeze(1).unsqueeze(3).broadcast_to([P, TB, 2, 64])
                S.did(nc.gpsimd.tensor_tensor(out.rearrange("p b (c f) -> p b c f", c=2), src, m, ALU.mult), "pool", name)

            def pair(i, par):
                S.turn(pool, i, "dve", "act", "pe")
                for e in heads:
                    for l in range(1, NL):
                        if l == 1:
                            S.wait(pool, i, f"dve.gb{e}{TB - 1}")
                            if e:
                                S.wait(pool, i, "pe.h0")
                        if l >= 3:
                            S.wait(pool, i, f"pe.x{e}{l - 2}")
                        S.did(nc.gpsimd.tensor_tensor(LOT[l % 2], GB[:, :, 0:P], lev(l + 1), ALU.mult), "pool", f"lot{e}{l}")
                    S.wait(pool, i, f"pe.xt{e}{NL - 1}")
                    mask(BTZ, TOK[:, 1, :, rows(e)], e, f"btz{e}")
                    S.did(nc.gpsimd.tensor_copy(UVA[:, :, 64:P], TOK[:, 0, :, rows(e)]), "pool", f"uva{e}")
                    mask(VZ, TOK[:, 3, :, rows(e)], e, f"vz{e}")
                    S.wait(pool, i, f"act.ptc{e}")
                    mask(P1Z, P1TA[:, :, 0:64], e, f"p1z{e}")
            loop(pool, NPAIR, pair)

        @block.tensor
        def _(pe):
            mm = nc.tensor.matmul
            S.begin(pe, "pe")
            pe.wait_ge(w_t, 1)
            pe.wait_ge(zeroed, 4)

            def pair(i, par):
                S.turn(pe, i, "dve", "act", "pool")
                pe.wait_ge(ld, i * 80 + 80)
                S.did(mm(B[0][:, :], W2[rows(0), :], TW[rows(0), :], start=True, stop=True), "pe", "zw")
                S.did(mm(B[1][:, :], W2[rows(1), :], TW[rows(1), :], start=True, stop=True), "pe", "za")
                S.wait(pe, i, "act.sqk")
                S.did(mm(B[2][:, :], C("bones"), SQN, start=True, stop=True), "pe", "ss")
                S.wait(pe, i, "dve.bo")
                S.did(mm(B[3][:, :], C("bones"), EWP, start=True, stop=True), "pe", "bs")
                for n, (x, src) in enumerate((("A", AR[:, 0, :]), ("B", SQN), ("K", LW), ("V", M[:, 2, :]))):
                    for b in range(TB):
                        last = nc.tensor.transpose(B[4 + n][:, blk(b)], src[:, blk(b)], C("ident"))
                    S.did(last, "pe", "t" + x)
                for e in heads:
                    for b in range(TB):
                        if b >= 2:
                            S.wait(pe, i, f"dve.gb{e}{b - 2}")
                        mm(B[b % 2][:, 0:2 * P], BZ[:, e, blk(b)], AR[:, :, blk(b)], start=True, stop=True)
                        S.did(mm(B[b % 2][:, 2 * P:T], KZ[:, e, blk(b)], AR[:, :, blk(b)], start=True, stop=True), "pe", f"g{e}{b}")
                    for b in range(TB):
                        last = mm(B[2][:, blk(b)], AR[:, 0, blk(b)], BZ[:, e, blk(b)], start=True, stop=True)
                    S.did(last, "pe", f"lm{e}")
                    S.wait(pe, i, f"dve.tt0b{e}")
                    if e == 0:
                        S.wait(pe, i, "dve.tokB", "act.tokV", "dve.bon")
                    for l in range(1, NL):
                        S.wait(pe, i, f"pool.lot{e}{l}")
                        if l > 1:
                            S.wait(pe, i, f"dve.tta{e}{l - 1}")
                        for b in range(TB):
                            last = mm(B[3][:, blk(b)], LOT[l % 2][:, b, :], T_[:, b, :], start=True, stop=True)
                        S.did(last, "pe", f"x{e}{l}")
                        S.wait(pe, i, f"act.xc{e}{l}")
                        if l < NL - 1:
                            for b in range(TB):
                                last = mm(B[4][:, blk(b)], TT[:, b, :], X[:, b, :], start=True, stop=True)
                            S.did(last, "pe", f"tx{e}{l}")
                        for b in range(TB):
                            last = mm(B[5][:, blk(b)], X[:, b, :], TT[:, b, :], start=True, stop=True)
                        S.did(last, "pe", f"xt{e}{l}")
                    S.wait(pe, i, f"dve.tta{e}{NL - 1}")
                    for b in range(TB):
                        last = mm(B[3][:, b * 64:b * 64 + 64], GB[:, b, 2 * P:3 * P], TOK[:, 3, b, rows(e)], start=True, stop=True)
                    S.did(last, "pe", f"uv{e}")
                    S.wait(pe, i, f"act.uvc{e}", f"pool.uva{e}")
                    for b in range(TB):
                        last = mm(B[4][:, blk(b)], TT[:, b, :], UVA[:, b, :], start=True, stop=True)
                    S.did(last, "pe", f"pt{e}")
                    S.wait(pe, i, f"act.ptc{e}")
                    for b in range(TB):
                        last = mm(B[6][rows(e), blk(b)], P1TA[:, b, 64:P], GB[:, b, P:2 * P], start=True, stop=True)
                    S.did(last, "pe", f"q{e}")
                    for b in range(TB):
                        mm(B[7][rows(e), blk(b)], P1TA[:, b, 0:64], GB[:, b, P:2 * P], start=True, stop=False)
                        last = mm(B[7][rows(e), blk(b)], TOK[:, 3, b, rows(e)], GB[:, b, 3 * P:T], start=False, stop=True)
                    S.did(last, "pe", f"y{e}")
                    S.wait(pe, i, f"pool.btz{e}")
                    for b in range(TB):
                        last = mm(B[3][rows(e), blk(b)], P1TA[:, b, 64:P], BTZ[:, b, :], start=True, stop=True)
                    S.did(last, "pe", f"gt{e}")
                    S.wait(pe, i, f"pool.p1z{e}")
                    for b in range(TB):
                        mm(B[5][rows(e), blk(b)], TOK[:, 1, b, rows(e)], P1Z[:, b, :], start=True, stop=False)
                        last = mm(B[5][rows(e), blk(b)], TOK[:, 2, b, rows(e)], VZ[:, b, :], start=False, stop=True)
                    S.did(last, "pe", f"h{e}")
                S.wait(pe, i, "dve.hb1")
                for c in range(1, NCH - 1):
                    S.wait(pe, i, "dve.st1" if c == 1 else f"dve.su{c - 1}")
                    S.did(mm(B[c % 2][:, 0:P], GTI[:, c, :], ST[:, c, :], start=True, stop=True), "pe", f"s{c}")
                S.wait(pe, i, "dve.qt", f"dve.su{NCH - 2}")
                for c in range(NCH):
                    last = mm(B[2][:, c * CH:(c + 1) * CH], ST[:, c, :], QT[:, c * CH:(c + 1) * CH], start=True, stop=True)
                S.did(last, "pe", "yf")
                S.wait(pe, i, "dve.yy")
                S.did(mm(B[0][:, :], C("bones"), Y, start=True, stop=True), "pe", "mean")
                S.wait(pe, i, "act.sqy")
                S.did(mm(B[1][:, :], C("bones"), SQ, start=True, stop=True), "pe", "var")
            loop(pe, NPAIR, pair)

        @block.scalar
        def _(act):
            A = nc.scalar.activation
            S.begin(act, "act")
            act.wait_ge(w_m, 2)
            A(TW[0:64, :], TW[0:64, :], ACT.Tanh).then_inc(w_t, 1)

            def pair(i, par):
                S.turn(act, i, "dve", "pe", "pool")

                def did(name, ins):
                    S.did(ins, "act", name)
                S.wait(act, i, "pe.zw")
                did("sgw", A(LW, B[0][:, :], ACT.Sigmoid, bias=k.prm("w0", i)))
                S.wait(act, i, "pe.za")
                did("sga", A(AS, B[1][:, :], ACT.Sigmoid, bias=k.prm("a0", i)))
                S.wait(act, i, "dve.kk")
                did("sqk", A(SQN, KK, ACT.Square))
                S.wait(act, i, "pe.ss")
                did("sqrt", A(SQN, B[2][:, :], ACT.Sqrt))
                S.wait(act, i, "dve.mv", "dve.lp")
                did("ew", A(EW, L, ACT.Exp))
                did("ewi", A(EWI, L, ACT.Exp, scale=-1.0))
                did("ewp", A(EWP, EWP, ACT.Exp))
                for n, x in ((2, "K"), (3, "V")):
                    S.wait(act, i, "pe.t" + x)
                    did("tok" + x, A(TOK[:, n, :, :], B[4 + n][:, :].rearrange("p (b f) -> p b f", f=P), ACT.Copy))
                for e in heads:
                    for l in range(1, NL):
                        S.wait(act, i, f"pe.x{e}{l}")
                        did(f"xc{e}{l}", A(X, B[3][:, :].rearrange("p (b f) -> p b f", f=P), ACT.Copy))
                    S.wait(act, i, f"pe.uv{e}")
                    did(f"uvc{e}", A(UVA[:, :, 0:64], B[3][:, 0:2 * P].rearrange("p (b f) -> p b f", f=64), ACT.Copy))
                    S.wait(act, i, f"pe.pt{e}")
                    did(f"ptc{e}", A(P1TA, B[4][:, :].rearrange("p (b f) -> p b f", f=P), ACT.Copy))
                S.wait(act, i, "dve.yc")
                did("sqy", A(SQ, Y, ACT.Square))
                S.wait(act, i, "dve.ve")
                did("vsqrt", A(VE, VE, ACT.Sqrt))
                S.wait(act, i, "dve.yz")
                did("xh", A(k.XH[:, i + NPAIR, :], Y, ACT.Copy))
            loop(act, NPAIR, pair)

        @block.vector
        def _(dve):
            V = nc.vector
            S.begin(dve, "dve")
            TTn, STT, TS = V.tensor_tensor, V.scalar_tensor_tensor, V.tensor_scalar
            V.memset(IN[:, 0, 0:1], 0.0).then_inc(col_zero, 1)
            dve.wait_ge(w_in, 16)
            dve.wait_ge(zeroed, 4)
            dve.wait_ge(col_zero, 1)
            TTn(M[:, 0, :], IN[:, 0, 0:T], IN[:, 0, 1:T + 1], ALU.subtract).then_inc(w_m, 1)
            dve.wait_ge(w_m, 1)
            STT(out=TW, in0=M[:, 0, :], scalar=k.prm("mu", 24), in1=IN[:, 0, 1:T + 1], op0=ALU.mult, op1=ALU.add).then_inc(w_m, 1)

            def pair(i, par):
                S.turn(dve, i, "act", "pe", "pool")

                def do(name, ins):
                    S.did(ins, "dve", name)

                def after(*names):
                    S.wait(dve, i, *names)
                do("z0", V.memset(IN[:, :, 0:1], 0.0))
                dve.wait_ge(ld, i * 80 + 80)
                after("dve.z0")
                for n, (x, mu) in enumerate((("r", 0), ("k", 8), ("v", 16))):
                    if n:
                        after("dve.m" + "rkv"[n - 1])
                    do("d" + x, TTn(DT, IN[:, n, 0:T], IN[:, n, 1:T + 1], ALU.subtract))
                    after("dve.d" + x)
                    do("m" + x, STT(out=M[:, n, :], in0=DT, scalar=k.prm("mu", i + mu), in1=IN[:, n, 1:T + 1], op0=ALU.mult, op1=ALU.add))
                do("kk", TS(KK, M[:, 1, :], k.prm("k_k", i), None, ALU.mult))
                after("act.sgw")
                do("lw", TS(LW, LW, -float(np.exp(-0.5)), None, ALU.mult))
                after("dve.lw", "dve.mv")
                do("scan", V.tensor_tensor_scan(L, C("rst"), LW, 0.0, ALU.mult, ALU.add))
                after("dve.scan")
                do("lp", TTn(EWP, L, LW, ALU.subtract))
                after("act.sqrt")
                do("nmax", TS(SQN, SQN, 1e-12, None, ALU.max))
                after("dve.nmax")
                do("nrec", V.reciprocal(SQN, SQN))
                after("dve.nrec")
                do("kn", TTn(KK, KK, SQN, ALU.mult))
                after("act.ewp")
                do("am", TS(L, AS, -1.0, k.prm("k_a", i), ALU.add, ALU.mult))
                after("dve.am")
                do("kp", STT(out=M[:, 1, :], in0=L, scalar=1.0, in1=M[:, 1, :], op0=ALU.add, op1=ALU.mult))
                after("dve.kn")
                do("at", STT(out=AR[:, 0, :], in0=KK, scalar=-1.0, in1=EWP, op0=ALU.mult, op1=ALU.mult))
                do("ba", TTn(SQN, KK, AS, ALU.mult))
                after("dve.ba")
                do("bt", TTn(SQN, SQN, EWI, ALU.mult))
                after("dve.kp")
                do("kt", TTn(LW, M[:, 1, :], EWI, ALU.mult))
                after("dve.bt")
                for e in heads:
                    do(f"bz{e}", V.tensor_copy(BZ[rows(e), e, :], SQN[rows(e), :]))
                after("dve.kt")
                for e in heads:
                    do(f"kz{e}", V.tensor_copy(KZ[rows(e), e, :], LW[rows(e), :]))
                do("rt", TTn(AR[:, 1, :], M[:, 0, :], EW, ALU.mult))
                do("wc", V.tensor_copy(WC, EW[:, CH - 1::CH]))
                do("bo", STT(out=EWP, in0=M[:, 0, :], scalar=k.prm("r_k", i), in1=M[:, 1, :], op0=ALU.mult, op1=ALU.mult))
                after("pe.bs")
                do("bon", TTn(BON, B[3][:, :], M[:, 2, :], ALU.mult))
                for n, x in ((0, "A"), (1, "B")):
                    after("pe.t" + x)
                    do("tok" + x, V.tensor_copy(TOK[:, n, :, :], B[4 + n][:, :].rearrange("p (b f) -> p b f", f=P)))
                after("pe.tV")
                for e in heads:
                    for b in range(TB):
                        after(f"pe.g{e}{b}")
                        do(f"gb{e}{b}", TTn(GB[:, b, :], B[b % 2][:, :], C("mt"), ALU.mult))
                    after(f"pe.lm{e}")
                    do(f"t0a{e}", TTn(T_, B[2][:, :].rearrange("p (b f) -> p b f", f=P), lev(0), ALU.mult))
                    after(f"dve.t0a{e}")
                    do(f"t0b{e}", TTn(T_, T_, ident4(), ALU.add))
                    do(f"tt0a{e}", TTn(TT, GB[:, :, 0:P], lev(1), ALU.mult))
                    after(f"dve.tt0a{e}")
                    do(f"tt0b{e}", TTn(TT, TT, ident4(), ALU.add))
                    for l in range(1, NL):
                        if l < NL - 1:
                            after(f"pe.tx{e}{l}")
                            do(f"ta{e}{l}", TTn(T_, T_, B[4][:, :].rearrange("p (b f) -> p b f", f=P), ALU.add))
                        after(f"pe.xt{e}{l}")
                        do(f"tta{e}{l}", TTn(TT, TT, B[5][:, :].rearrange("p (b f) -> p b f", f=P), ALU.add))
                    after(f"pe.gt{e}")
                    do(f"gti{e}", TTn(GTI[rows(e), :, rows(e)], B[3][rows(e), :].rearrange("p (c f) -> p c f", f=64),
                                      C("ident")[rows(e), rows(e)].unsqueeze(1).broadcast_to([64, NCH, 64]), ALU.add))
                    after(f"pe.h{e}")
                    do(f"hb{e}", TTn(HB[rows(e), :, rows(e)], B[5][rows(e), :].rearrange("p (c f) -> p c f", f=64),
                                     WC[rows(e), :].unsqueeze(2).broadcast_to([64, NCH, 64]), ALU.mult))
                do("st0", V.memset(ST[:, 0, :], 0.0))
                after("dve.hb1")
                do("st1", V.tensor_copy(ST[:, 1, :], HB[:, 0, :]))
                do("qt", TTn(QT, B[6][:, :], AR[:, 1, :], ALU.add))
                do("yv", V.tensor_copy(Y, B[7][:, :]))
                for c in range(1, NCH - 1):
                    after(f"pe.s{c}")
                    do(f"su{c}", STT(out=ST[:, c + 1, :], in0=B[c % 2][:, 0:P], scalar=WC[:, c:c + 1], in1=HB[:, c, :], op0=ALU.mult, op1=ALU.add))
                after("pe.yf", "dve.yv")
                do("yy", TTn(Y, B[2][:, :], Y, ALU.add))
                after("pe.mean")
                do("yc", STT(out=Y, in0=B[0][:, :], scalar=-1.0 / 64, in1=Y, op0=ALU.mult, op1=ALU.add))
                after("pe.var")
                do("ve", TS(VE, B[1][:, :], 1.0 / 64, GN_EPS, ALU.mult, ALU.add))
                after("act.vsqrt")
                do("vrec", V.reciprocal(VE, VE))
                after("dve.vrec")
                do("yn", STT(out=Y, in0=Y, scalar=k.prm("ln_w", i), in1=VE, op0=ALU.mult, op1=ALU.mult))
                after("dve.yn")
                do("yb", STT(out=Y, in0=Y, scalar=k.prm("ln_b", i), in1=BON, op0=ALU.add, op1=ALU.add))
                after("dve.yb")
                dve.wait_ge(z_in, i * 16 + 16)
                do("yz", TTn(Y, Y, Z, ALU.mult))
                after("act.xh")
                do("xl", TTn(k.XL[:, i + NPAIR, :], Y, f32(k.XH[:, i + NPAIR, :]), ALU.subtract))
            loop(dve, NPAIR, pair)


def positions(k, tag, rope):
    nc, d = k.nc, k.d
    A = mla_arena(k)
    PI, CI, PF, CF, ANG, KI, KF = (A[x] for x in ("PI", "CI", "PF", "CF", "ANG", "KI", "KF"))
    DM, COS, SIN = A["DM"], A["COS"], A["SIN"]
    PQI, PQF, CQI, CQF = A["PQI"], A["PQF"], A["CQI"], A["CQF"]
    pi, st, si = k.sem(tag + "pos_in"), k.sem(tag + "pos_step"), k.sem(tag + "pos_trig")
    n = [0]
    TWO_PI = float(2 * np.pi)
    c1 = 6.28125
    c2 = float(np.float32(np.floor((TWO_PI - c1) * 2 ** 21) / 2 ** 21))
    c3 = float(TWO_PI - c1 - c2)
    with nc.Block() as block:
        @block.sync
        def _(sp):
            p = d["positions_2"]
            sp.dma_start(PI, p[0:1, :].broadcast_to([P, T])).then_inc(pi, 16)
            with nc.allow_non_contiguous_dma(reason="512 positions, one a partition"):
                sp.dma_start(PQI, p[0, :].rearrange("(b p) -> p b", p=P)).then_inc(pi, 16)

        @block.vector
        def _(dve):
            V = nc.vector

            def do(ins):
                n[0] += 1
                ins.then_inc(st, 1)
                dve.wait_ge(st, n[0])
            dve.wait_ge(pi, 32)
            do(V.tensor_copy(PF, PI))
            do(V.tensor_copy(PQF, PQI))
            do(V.tensor_scalar(CI, PI, 6, None, ALU.arith_shift_right))
            do(V.tensor_scalar(CQI, PQI, 6, None, ALU.arith_shift_right))
            do(V.tensor_copy(CF, CI))
            do(V.tensor_copy(CQF, CQI))
            for tb in range(TB):
                if rope:
                    do(V.tensor_scalar(DM[:, tb, :], CF, CQF[:, tb:tb + 1], -BIG, ALU.is_gt, ALU.mult))
                    continue
                do(V.tensor_scalar(DM[:, tb, :], PF, PQF[:, tb:tb + 1], None, ALU.subtract))
                do(V.tensor_scalar(ANG, DM[:, tb, :], -1.0, None, ALU.mult))
                do(V.tensor_tensor(DM[:, tb, :], DM[:, tb, :], ANG, ALU.max))
                do(V.tensor_scalar(ANG, CF, CQF[:, tb:tb + 1], BIG, ALU.is_gt, ALU.mult))
                do(V.tensor_tensor(DM[:, tb, :], DM[:, tb, :], ANG, ALU.add))
            for out, shift in ((SIN, 0.0), (COS, 0.25)) if rope else ():
                do(V.tensor_scalar(ANG, PF, k.c("freq"), None, ALU.mult))
                do(V.tensor_scalar(KF, ANG, 1.0 / TWO_PI, shift, ALU.mult, ALU.add))
                do(V.tensor_copy(KI, KF))
                do(V.tensor_copy(KF, KI))
                for c in (c1, c2, c3):
                    do(V.scalar_tensor_tensor(out=ANG, in0=KF, scalar=-c, in1=ANG, op0=ALU.mult, op1=ALU.add))
                if shift:
                    do(V.tensor_scalar(ANG, ANG, float(np.pi / 2), None, ALU.add))
                do(V.tensor_scalar(KF, ANG, float(np.pi), -TWO_PI, ALU.is_gt, ALU.mult))
                do(V.tensor_tensor(ANG, ANG, KF, ALU.add))
                do(V.tensor_scalar(KF, ANG, -float(np.pi), TWO_PI, ALU.is_lt, ALU.mult))
                do(V.tensor_tensor(ANG, ANG, KF, ALU.add))
                do(V.tensor_scalar(out, ANG, 3.1415925, -3.1415925, ALU.min, ALU.max))

        if not rope:
            return

        @block.scalar
        def _(act):
            act.wait_ge(st, n[0])
            nc.scalar.activation(SIN, SIN, ACT.Sin).then_inc(si, 1)
            nc.scalar.activation(COS, COS, ACT.Sin).then_inc(si, 1)


def mla_arena(k):
    o = [0]

    def take(n):
        o[0] += n
        assert o[0] <= ARENA, o[0]
        return k.AR[:, o[0] - n:o[0]]
    o[0] = ARENA - TB * T
    DM = take(TB * T)
    o[0] = 0
    A = dict(COS=take(T), SIN=take(T), KPR=take(T), KPS=take(T))
    A["DM"] = DM.rearrange("p (b t) -> p b t", t=T)
    b = o[0]
    for x in ("PF", "CF", "ANG", "KF"):
        A[x] = take(T)
    for x in ("PI", "CI", "KI"):
        A[x] = take(T).bitcast(I32)
    A["PQF"], A["CQF"] = take(TB), take(TB)
    A["PQI"], A["CQI"] = take(TB).bitcast(I32), take(TB).bitcast(I32)
    o[0] = b
    A["KRZ"] = take(2 * T).rearrange("p (e t) -> p e t", t=T)
    A["QR"], A["QRS"], A["QRG"], A["SWS"] = take(T), take(T), take(T), take(T)
    A["QN"], A["QNS"], A["KN"], A["KNS"], A["VV"], A["VT"], A["RK"] = (take(T) for _ in range(7))
    A["S"] = take(2 * T).rearrange("p (j t) -> p j t", t=T)
    A["PT"] = take(TB * T).rearrange("p (b t) -> p b t", t=T)
    A["Z"], A["TM"] = take(T), take(T)
    A["RQ"] = take(2 * TB)
    A["MX"] = take(16)
    assert o[0] <= ARENA - TB * T, o[0]
    return A


def mla(k):
    nc, d = k.nc, k.d
    A = mla_arena(k)
    DM, COS, SIN, KPR, KPS, KRZ = (A[x] for x in ("DM", "COS", "SIN", "KPR", "KPS", "KRZ"))
    QR, QRS, QRG, SWS, QN, QNS, KN, KNS, VV, VT, RK = (A[x] for x in ("QR", "QRS", "QRG", "SWS", "QN", "QNS", "KN", "KNS", "VV", "VT", "RK"))
    S_, PT, Z, TM, RQ, MX = (A[x] for x in ("S", "PT", "Z", "TM", "RQ", "MX"))
    B, C = k.PSB, k.c
    QK = 192
    NP = AH // 2
    heads = range(2)
    pe_ = ["qswap"]
    act = ["qrs"]
    dve = ["qrg", "qrc", "qrsn", "qrr"]
    for e in heads:
        act += [f"qns{e}", f"kns{e}", f"rqs{e}", f"rks{e}", f"vt{e}"]
        dve += [f"qg{e}", f"rqm{e}", f"rqr{e}", f"rqx{e}", f"rkm{e}", f"rkr{e}", f"kg{e}", f"krz{e}"]
        pe_ += [f"rq{e}", f"rk{e}", f"v{e}", f"sc{e}0"]
        dve += [f"bias{e}0", f"max{e}0"]
        act += [f"exp{e}0"]
        for n in range(TB):
            if n + 1 < TB:
                pe_ += [f"sc{e}{n + 1}"]
                dve += [f"bias{e}{n + 1}", f"max{e}{n + 1}"]
                act += [f"exp{e}{n + 1}"]
            pe_ += [f"tr{e}{n}"]
            dve += [f"rec{e}{n}", f"p{e}{n}"]
            act += [f"pt{e}{n}"]
        pe_ += [f"pv{e}"]
        dve += [f"o{e}", f"xl{e}"]
        act += [f"xh{e}"]
    S = Steps(k, "mla", pe=pe_, act=act, dve=dve)
    kp_in, kp_s, kp_m = k.sem("kpe_in"), k.sem("kpe_step"), k.sem("kpe_swap")
    kp_q = k.sem("kpe_square")
    q_in, h_in = k.sem("mla_pair_in"), k.sem("mla_head_in")
    z0 = k.sem("krz_zeroed")

    def rows(e):
        return slice(64 * e, 64 * e + 64)

    def blk(b):
        return slice(b * P, (b + 1) * P)

    with nc.Block() as block:
        @block.gpsimd
        def _(pool):
            nc.gpsimd.memset(KRZ, 0.0).then_inc(z0, 1)

        @block.sync
        def _(sp):
            for e in heads:
                sp.dma_start(KPR[rows(e), :], k.PROJ[KPE0, 0:64, :]).then_inc(kp_in, 16)

            def pair(i, par):
                S.turn(sp, i, "pe", "act", "dve")
                sp.dma_start(QR, k.PROJ[QR0 + i, :, :]).then_inc(q_in, 16)
                for e in heads:
                    if e:
                        S.wait(sp, i, "dve.o0")
                    sp.dma_start(QN, k.PROJ[i * 2 + (QN0 + e), :, :]).then_inc(h_in, 16)
                    sp.dma_start(KN, k.PROJ[i * 4 + (KV0 + 2 * e), :, :]).then_inc(h_in, 16)
                    sp.dma_start(VV, k.PROJ[i * 4 + (KV0 + 2 * e + 1), :, :]).then_inc(h_in, 16)
                    sp.dma_start(Z, k.PROJ[i * 2 + (AG0 + e), :, :]).then_inc(h_in, 16)
            loop(sp, NP, pair)

        @block.tensor
        def _(pe):
            mm = nc.tensor.matmul
            S.begin(pe, "pe")
            pe.wait_ge(kp_s, 1)
            mm(B[0][:, :], C("swap"), KPR, start=True, stop=True).then_inc(kp_m, 1)
            pe.wait_ge(kp_s, 4)
            pe.wait_ge(z0, 1)

            def pair(i, par):
                S.turn(pe, i, "dve", "act")
                S.wait(pe, i, "dve.qrg")
                S.did(mm(B[6][:, :], C("swap"), QRG, start=True, stop=True), "pe", "qswap")
                for e in heads:
                    S.wait(pe, i, f"act.kns{e}", "act.qrs")
                    for tb in range(TB):
                        mm(B[7][:, tb:tb + 1], QNS[:, blk(tb)], C("ones", 0, 1), start=True, stop=False)
                        last = mm(B[7][:, tb:tb + 1], QRS[:, blk(tb)], C(f"hone{e}", 0, 1), start=False, stop=True)
                    S.did(last, "pe", f"rq{e}")
                    mm(B[5][:, :], C("ones"), KNS, start=True, stop=False)
                    S.did(mm(B[5][:, :], C("hone0"), KPS, start=False, stop=True), "pe", f"rk{e}")
                    pe.wait_ge(h_in, (i * 2 + (e + 1)) * 64)
                    for b in range(TB):
                        last = nc.tensor.transpose(B[3][:, blk(b)], VV[:, blk(b)], C("ident"))
                    S.did(last, "pe", f"v{e}")

                    def scores(n):
                        if n == 0:
                            S.wait(pe, i, f"dve.krz{e}", f"dve.qrr")
                        if n >= 2:
                            S.wait(pe, i, f"dve.bias{e}{n - 2}")
                        mm(B[n % 2][:, :], QN[:, blk(n)], KN, start=True, stop=False)
                        S.did(mm(B[n % 2][:, :], QRG[:, blk(n)], KRZ[:, e, :], start=False, stop=True), "pe", f"sc{e}{n}")

                    scores(0)
                    for n in range(TB):
                        if n + 1 < TB:
                            scores(n + 1)
                        S.wait(pe, i, f"dve.p{e}{n}")
                        if n == 0:
                            S.wait(pe, i, f"act.vt{e}")
                        if n >= 2:
                            S.wait(pe, i, f"act.pt{e}{n - 2}")
                        for b in range(TB):
                            last = nc.tensor.transpose(B[2 + n % 2][:, blk(b)], S_[:, n % 2, blk(b)], C("ident"))
                        S.did(last, "pe", f"tr{e}{n}")
                    S.wait(pe, i, f"act.pt{e}{TB - 1}")
                    for b in range(TB):
                        last = mm(B[4][:, :], VT[:, blk(b)], PT[:, b, :], start=(b == 0), stop=(b == TB - 1))
                    S.did(last, "pe", f"pv{e}")
            loop(pe, NP, pair)

        @block.scalar
        def _(act):
            Ac = nc.scalar.activation
            S.begin(act, "act")
            act.wait_ge(kp_in, 32)
            Ac(KPS, KPR, ACT.Square).then_inc(kp_q, 1)

            def pair(i, par):
                def did(name, ins):
                    S.did(ins, "act", name)

                def after(*names):
                    S.wait(act, i, *names)
                S.turn(act, i, "dve", "pe")
                act.wait_ge(q_in, i * 16 + 16)
                did("qrs", Ac(QRS, QR, ACT.Square))
                for e in heads:
                    act.wait_ge(h_in, (i * 2 + (e + 1)) * 64)
                    did(f"qns{e}", Ac(QNS, QN, ACT.Square))
                    did(f"kns{e}", Ac(KNS, KN, ACT.Square))
                    after(f"dve.rqm{e}")
                    did(f"rqs{e}", Ac(RQ[:, TB:2 * TB], RQ[:, 0:TB], ACT.Sqrt))
                    after(f"dve.rkm{e}")
                    did(f"rks{e}", Ac(RK, RK, ACT.Sqrt))
                    after(f"pe.v{e}")
                    did(f"vt{e}", Ac(VT, B[3][:, :], ACT.Copy))

                    def exps(n):
                        j = n % 2
                        after(f"dve.max{e}{n}")
                        did(f"exp{e}{n}", Ac(S_[:, j, :], S_[:, j, :], ACT.Exp, bias=MX[:, j:j + 1], accum_out=MX[:, 4 + j:5 + j]))
                    exps(0)
                    for n in range(TB):
                        if n + 1 < TB:
                            exps(n + 1)
                        after(f"pe.tr{e}{n}")
                        if e and n == 0:
                            after("pe.pv0")
                        did(f"pt{e}{n}", Ac(PT[:, :, blk(n)], B[2 + n % 2][:, :].rearrange("p (b t) -> p b t", t=P), ACT.Copy))
                    after(f"dve.o{e}")
                    did(f"xh{e}", Ac(k.XH[:, i * 2 + e, :], TM, ACT.Copy))
            loop(act, NP, pair)

        @block.vector
        def _(dve):
            V = nc.vector
            TTn, STT, TS = V.tensor_tensor, V.scalar_tensor_tensor, V.tensor_scalar
            S.begin(dve, "dve")
            dve.wait_ge(kp_q, 1)
            TS(KPR, KPR, k.prm("k_gain", 1), None, ALU.mult).then_inc(kp_s, 1)
            dve.wait_ge(kp_m, 1)
            TTn(TM, B[0][:, :], SIN, ALU.mult).then_inc(kp_s, 1)
            TTn(KPR, KPR, COS, ALU.mult).then_inc(kp_s, 1)
            dve.wait_ge(kp_s, 3)
            TTn(KPR, KPR, TM, ALU.add).then_inc(kp_s, 1)
            dve.wait_ge(kp_s, 4)
            dve.wait_ge(z0, 1)

            def pair(i, par):
                def do(name, ins):
                    S.did(ins, "dve", name)

                def after(*names):
                    S.wait(dve, i, *names)
                S.turn(dve, i, "act", "pe")
                after("act.qrs")
                do("qrg", TS(QRG, QR, k.prm("q_gain", 1), None, ALU.mult))
                after("pe.qswap")
                do("qrc", TTn(SWS, B[6][:, :], SIN, ALU.mult))
                do("qrsn", TTn(QRG, QRG, COS, ALU.mult))
                after("dve.qrsn")
                do("qrr", TTn(QRG, QRG, SWS, ALU.add))
                for e in heads:
                    after(f"act.qns{e}")
                    do(f"qg{e}", TS(QN, QN, k.prm("q_gain", 0), None, ALU.mult))
                    after(f"pe.rq{e}")
                    do(f"rqm{e}", TS(RQ[:, 0:TB], B[7][:, 0:TB], 1.0 / QK, EPS, ALU.mult, ALU.add))
                    after(f"act.rqs{e}")
                    do(f"rqr{e}", V.reciprocal(RQ[:, 0:TB], RQ[:, TB:2 * TB]))
                    after(f"dve.rqr{e}")
                    do(f"rqx{e}", TS(RQ[:, 0:TB], RQ[:, 0:TB], QK ** -0.5, None, ALU.mult))
                    after(f"pe.rk{e}")
                    do(f"rkm{e}", TS(RK, B[5][:, :], 1.0 / QK, EPS, ALU.mult, ALU.add))
                    after(f"act.rks{e}")
                    do(f"rkr{e}", V.reciprocal(RK, RK))
                    after(f"dve.rkr{e}")
                    do(f"kg{e}", STT(out=KN, in0=KN, scalar=k.prm("k_gain", 0), in1=RK, op0=ALU.mult, op1=ALU.mult))
                    do(f"krz{e}", TTn(KRZ[rows(e), e, :], KPR[rows(e), :], RK[rows(e), :], ALU.mult))

                    def bias(n):
                        j = n % 2
                        after(f"pe.sc{e}{n}")
                        if n >= 2:
                            after(f"pe.tr{e}{n - 2}")
                        do(f"bias{e}{n}", STT(out=S_[:, j, :], in0=B[j][:, :], scalar=RQ[:, n:n + 1], in1=DM[:, n, :], op0=ALU.mult, op1=ALU.add))
                        after(f"dve.bias{e}{n}")
                        do(f"max{e}{n}", V.tensor_reduce(MX[:, j:j + 1], S_[:, j, :], AX, ALU.max, negate=True))
                    bias(0)
                    for n in range(TB):
                        j = n % 2
                        if n + 1 < TB:
                            bias(n + 1)
                        after(f"act.exp{e}{n}")
                        do(f"rec{e}{n}", V.reciprocal(MX[:, 8 + j:9 + j], MX[:, 4 + j:5 + j]))
                        after(f"dve.rec{e}{n}")
                        do(f"p{e}{n}", TS(S_[:, j, :], S_[:, j, :], MX[:, 8 + j:9 + j], None, ALU.mult))
                    after(f"pe.pv{e}")
                    do(f"o{e}", TTn(TM, B[4][:, :], Z, ALU.mult))
                    after(f"act.xh{e}")
                    do(f"xl{e}", TTn(k.XL[:, i * 2 + e, :], TM, f32(k.XH[:, i * 2 + e, :]), ALU.subtract))
            loop(dve, NP, pair)


def diff(k):
    nc, d = k.nc, k.d
    DM = mla_arena(k)["DM"]
    o = [0]

    def take(n, shape=None):
        o[0] += n
        assert o[0] <= ARENA - TB * T, o[0]
        v = k.AR[:, o[0] - n:o[0]]
        return v.rearrange("p (a t) -> p a t", t=T) if shape else v
    BM, PT = take(TB * T, 1), take(TB * T, 1)
    QN, KN, QS, KS, VV, VT, Z = (take(2 * T, 1) for _ in range(7))
    S_ = take(4 * T).rearrange("p (j c t) -> p j c t", c=2, t=T)
    RQ, MX, LM = take(16), take(32), take(8)
    TM, RK, OS, RS = VV, KS, QS, KS[:, 0, :]
    B, C = k.PSB, k.c
    HALF = range(2)
    pe_ = ["rq", "rk0", "rk1", "v"] + ["sc00", "sc01"]
    act = ["qs0", "qs1", "ks0", "ks1", "rqs", "rks0", "rks1", "vt0", "vt1", "exp00", "exp01"]
    dve = ["bm", "qg0", "qg1", "rqm", "rqr", "rqx", "rkm0", "rkm1", "rkr0", "rkr1", "kg0", "kg1", "bias00", "max00", "bias01", "max01"]
    for n in range(TB):
        if n + 1 < TB:
            pe_ += [f"sc{n + 1}0", f"sc{n + 1}1"]
            act += [f"exp{n + 1}0", f"exp{n + 1}1"]
            dve += [f"bias{n + 1}0", f"max{n + 1}0", f"bias{n + 1}1", f"max{n + 1}1"]
        pe_ += [f"tr{n}"]
        act += [f"pt{n}"]
        dve += [f"rec{n}0", f"rec{n}1", f"rl{n}", f"pa{n}", f"pb{n}"]
    pe_ += ["pv0", "pv1", "os"]
    act += ["os0", "os1", "osq", "xh0", "xh1"]
    dve += ["osm", "osr", "o0", "o1", "oz0", "oz1", "xl0", "xl1"]
    S = Steps(k, "diff", pe=pe_, act=act, dve=dve)
    h_in = k.sem("diff_head_in")
    lp, lm, le = k.sem("lambda_products"), k.sem("lambda_sums"), k.sem("lambda_exps")

    def blk(b):
        return slice(b * P, (b + 1) * P)

    with nc.Block() as block:
        @block.sync
        def _(sp):
            def head(h, par):
                S.turn(sp, h, "pe", "act", "dve")
                for buf, c0 in ((QN, BQ0), (KN, BK0), (VV, BV0), (Z, BG0)):
                    sp.dma_start(buf, k.PROJ[bass.ds(h * 2 + c0, 2), :, :].rearrange("c p t -> p c t")).then_inc(h_in, 16)
            loop(sp, BH, head)

        @block.tensor
        def _(pe):
            mm = nc.tensor.matmul
            S.begin(pe, "pe")
            pe.wait_ge(lp, 2)
            mm(B[7][:, 0:2], C("ones"), LM[:, 0:2], start=True, stop=True).then_inc(lm, 1)

            def head(h, par):
                S.turn(pe, h, "dve", "act")

                def after(*names):
                    S.wait(pe, h, *names)
                if par == 0:
                    pe.wait_ge(le, 3)
                after("act.qs1")
                for c in HALF:
                    for tb in range(TB):
                        last = mm(B[7][:, c * TB + tb:c * TB + tb + 1], QS[:, c, blk(tb)], C("ones", 0, 1), start=True, stop=True)
                S.did(last, "pe", "rq")
                for c in HALF:
                    after(f"act.ks{c}")
                    S.did(mm(B[5 + c][:, :], C("ones"), KS[:, c, :], start=True, stop=True), "pe", f"rk{c}")
                for j in HALF:
                    for b in range(TB):
                        last = nc.tensor.transpose(B[2 + j][:, blk(b)], VV[:, j, blk(b)], C("ident"))
                S.did(last, "pe", "v")

                def scores(n):
                    for c in HALF:
                        after(f"dve.kg{c}" if n == 0 else f"dve.bias{n - 1}{c}")
                        S.did(mm(B[c][:, :], QN[:, c, blk(n)], KN[:, c, :], start=True, stop=True), "pe", f"sc{n}{c}")
                scores(0)
                for n in range(TB):
                    if n + 1 < TB:
                        scores(n + 1)
                    after(f"dve.pb{n}")
                    after("act.vt1" if n < 2 else f"act.pt{n - 2}")
                    for b in range(TB):
                        last = nc.tensor.transpose(B[2 + n % 2][:, blk(b)], S_[:, n % 2, 0, blk(b)], C("ident"))
                    S.did(last, "pe", f"tr{n}")
                after(f"act.pt{TB - 1}")
                for j in HALF:
                    for b in range(TB):
                        last = mm(B[4 + j][:, :], VT[:, j, blk(b)], PT[:, b, :], start=(b == 0), stop=(b == TB - 1))
                    S.did(last, "pe", f"pv{j}")
                after("act.os1")
                for j in HALF:
                    last = mm(B[6][:, :], C("ones"), OS[:, j, :], start=(j == 0), stop=(j == 1))
                S.did(last, "pe", "os")
            loop(pe, BH, head)

        @block.scalar
        def _(act):
            Ac = nc.scalar.activation
            S.begin(act, "act")
            act.wait_ge(lm, 1)
            Ac(LM[:, 2:4], B[7][:, 0:2], ACT.Exp).then_inc(le, 1)

            def head(h, par):
                def did(name, ins):
                    S.did(ins, "act", name)

                def after(*names):
                    S.wait(act, h, *names)
                S.turn(act, h, "dve", "pe")
                act.wait_ge(h_in, h * 64 + 64)
                for c in HALF:
                    did(f"qs{c}", Ac(QS[:, c, :], QN[:, c, :], ACT.Square))
                for c in HALF:
                    did(f"ks{c}", Ac(KS[:, c, :], KN[:, c, :], ACT.Square))
                after("dve.rqm")
                did("rqs", Ac(RQ[:, 8:16], RQ[:, 0:8], ACT.Sqrt))
                for c in HALF:
                    after(f"dve.rkm{c}")
                    did(f"rks{c}", Ac(RK[:, c, :], RK[:, c, :], ACT.Sqrt))
                after("pe.v")
                for j in HALF:
                    did(f"vt{j}", Ac(VT[:, j, :], B[2 + j][:, :], ACT.Copy))

                def exps(n):
                    for c in HALF:
                        j = 2 * (n % 2) + c
                        after(f"dve.max{n}{c}")
                        did(f"exp{n}{c}", Ac(S_[:, n % 2, c, :], S_[:, n % 2, c, :], ACT.Exp, bias=MX[:, j:j + 1], accum_out=MX[:, 8 + j:9 + j]))
                exps(0)
                for n in range(TB):
                    if n + 1 < TB:
                        exps(n + 1)
                    after(f"pe.tr{n}")
                    did(f"pt{n}", Ac(PT[:, :, blk(n)], B[2 + n % 2][:, :].rearrange("p (b t) -> p b t", t=P), ACT.Copy))
                for j in HALF:
                    after(f"pe.pv{j}")
                    did(f"os{j}", Ac(OS[:, j, :], B[4 + j][:, :], ACT.Square))
                after("dve.osm")
                did("osq", Ac(RS, RS, ACT.Sqrt))
                for j in HALF:
                    after(f"dve.oz{j}")
                    did(f"xh{j}", Ac(k.XH[:, h * 2 + j, :], TM[:, j, :], ACT.Copy))
            loop(act, BH, head)

        @block.vector
        def _(dve):
            V = nc.vector
            TTn, STT, TS = V.tensor_tensor, V.scalar_tensor_tensor, V.tensor_scalar
            S.begin(dve, "dve")
            for j in HALF:
                TTn(LM[:, j:j + 1], k.prm("lam", 2 * j), k.prm("lam", 2 * j + 1), ALU.mult).then_inc(lp, 1)
            dve.wait_ge(le, 1)
            TTn(LM[:, 4:5], LM[:, 3:4], LM[:, 2:3], ALU.subtract).then_inc(le, 1)
            dve.wait_ge(le, 2)
            TS(LM[:, 5:6], LM[:, 4:5], -LAM_INIT, None, ALU.add).then_inc(le, 1)
            dve.wait_ge(le, 3)

            def head(h, par):
                def do(name, ins):
                    S.did(ins, "dve", name)

                def after(*names):
                    S.wait(dve, h, *names)
                S.turn(dve, h, "act", "pe")
                do("bm", TS(BM, DM, C("nslope")[:, bass.ds(h, 1)], None, ALU.mult))
                for c in HALF:
                    after(f"act.qs{c}")
                    do(f"qg{c}", TS(QN[:, c, :], QN[:, c, :], k.prm("bq_gain"), None, ALU.mult))
                after("pe.rq")
                do("rqm", TS(RQ[:, 0:8], B[7][:, 0:8], 1.0 / HD, EPS, ALU.mult, ALU.add))
                after("act.rqs")
                do("rqr", V.reciprocal(RQ[:, 0:8], RQ[:, 8:16]))
                after("dve.rqr")
                do("rqx", TS(RQ[:, 0:8], RQ[:, 0:8], HD ** -0.5, None, ALU.mult))
                for c in HALF:
                    after(f"pe.rk{c}")
                    do(f"rkm{c}", TS(RK[:, c, :], B[5 + c][:, :], 1.0 / HD, EPS, ALU.mult, ALU.add))
                for c in HALF:
                    after(f"act.rks{c}")
                    do(f"rkr{c}", V.reciprocal(RK[:, c, :], RK[:, c, :]))
                for c in HALF:
                    after(f"dve.rkr{c}")
                    do(f"kg{c}", STT(out=KN[:, c, :], in0=KN[:, c, :], scalar=k.prm("bk_gain"), in1=RK[:, c, :], op0=ALU.mult, op1=ALU.mult))

                def bias(n):
                    for c in HALF:
                        j = 2 * (n % 2) + c
                        after(f"pe.sc{n}{c}")
                        if n >= 2:
                            after(f"pe.tr{n - 2}")
                        do(f"bias{n}{c}", STT(out=S_[:, n % 2, c, :], in0=B[c][:, :], scalar=RQ[:, c * TB + n:c * TB + n + 1], in1=BM[:, n, :], op0=ALU.mult, op1=ALU.add))
                        after(f"dve.bias{n}{c}")
                        do(f"max{n}{c}", V.tensor_reduce(MX[:, j:j + 1], S_[:, n % 2, c, :], AX, ALU.max, negate=True))
                bias(0)
                for n in range(TB):
                    q = n % 2
                    if n + 1 < TB:
                        bias(n + 1)
                    for c in HALF:
                        j = 2 * q + c
                        after(f"act.exp{n}{c}")
                        do(f"rec{n}{c}", V.reciprocal(MX[:, 16 + j:17 + j], MX[:, 8 + j:9 + j]))
                    after(f"dve.rec{n}1")
                    do(f"rl{n}", TTn(MX[:, 24 + q:25 + q], MX[:, 17 + 2 * q:18 + 2 * q], LM[:, 5:6], ALU.mult))
                    do(f"pa{n}", TS(S_[:, q, 0, :], S_[:, q, 0, :], MX[:, 16 + 2 * q:17 + 2 * q], None, ALU.mult))
                    after(f"dve.pa{n}")
                    do(f"pb{n}", STT(out=S_[:, q, 0, :], in0=S_[:, q, 1, :], scalar=MX[:, 24 + q:25 + q], in1=S_[:, q, 0, :], op0=ALU.mult, op1=ALU.add))
                after("pe.os")
                do("osm", TS(RS, B[6][:, :], 1.0 / (2 * HD), EPS, ALU.mult, ALU.add))
                after("act.osq")
                do("osr", V.reciprocal(RS, RS))
                after("dve.osr")
                for j in HALF:
                    do(f"o{j}", STT(out=TM[:, j, :], in0=B[4 + j][:, :], scalar=k.prm("subln", j), in1=RS, op0=ALU.mult, op1=ALU.mult))
                for j in HALF:
                    after(f"dve.o{j}")
                    do(f"oz{j}", STT(out=TM[:, j, :], in0=TM[:, j, :], scalar=1.0 - LAM_INIT, in1=Z[:, j, :], op0=ALU.mult, op1=ALU.mult))
                for j in HALF:
                    after(f"act.xh{j}")
                    do(f"xl{j}", TTn(k.XL[:, h * 2 + j, :], TM[:, j, :], f32(k.XH[:, h * 2 + j, :]), ALU.subtract))
            loop(dve, BH, head)


def write_out(k):
    nc = k.nc
    O = k.AR[:, 0:2 * D].rearrange("p (j n) -> p j n", n=D)
    t, c_, out = k.sem("out_turned"), k.sem("out_copied"), [k.sem(f"out_stored{j}") for j in range(2)]
    NG = KT // 4
    with nc.Block() as block:
        @block.tensor
        def _(pe):
            for tb in range(TB):
                for g in range(NG):
                    n = tb * NG + g
                    if n >= 4:
                        pe.wait_ge(c_, n - 3)
                    for c in range(4):
                        last = nc.tensor.transpose(k.PSB[n % 4][:, c * P:(c + 1) * P], k.RES[:, 4 * g + c, tb * P:(tb + 1) * P], k.c("ident"))
                    last.then_inc(t, 1)

        @block.scalar
        def _(act):
            for tb in range(TB):
                if tb >= 2:
                    act.wait_ge(out[tb % 2], 16)
                for g in range(NG):
                    n = tb * NG + g
                    act.wait_ge(t, n + 1)
                    nc.scalar.activation(O[:, tb % 2, g * T:(g + 1) * T], k.PSB[n % 4][:, :], ACT.Copy).then_inc(c_, 1)

        @block.sync
        def _(sp):
            for tb in range(TB):
                sp.wait_ge(c_, (tb + 1) * NG)
                sp.dma_start(k.d["out"][0, tb * P:(tb + 1) * P, :], O[:, tb % 2, :]).then_inc(out[tb % 2], 16)
            sp.wait_ge(out[0], 32)
            sp.wait_ge(out[1], 32)


def build(nc, dram, stop=None):
    with ExitStack() as ctx:
        k = Kernel(nc, ctx, dram)
        setup(k)
        norm(k, "pre", KT, "pre_g")
        w = dram["w_in"][0, :, :]
        c_gate, c_za, c_b = 2560, 2584, 3608
        project(k, [(20, Q0, columns(w, 0), P, None),
                    (1, G0, columns(w, c_gate, width=NGATE), NGATE, "sigmoid"),
                    (8, ZA0, columns(w, c_za), P, "silu"),
                    (25, R0, columns(w, c_b), P, None),
                    (8, ZB0, columns(w, c_b + 3200), P, "silu")], KT)
        if stop == "proj1":
            return dump(k)
        nsa_setup(k)
        nsa_heads(k)
        if stop == "nsa":
            return dump(k)
        rwkv(k)
        if stop == "rwkv":
            return dump(k)
        project(k, [(KT, 0, columns(dram["w_out"][0, :, :], 0), P, None)], KT)
        norm(k, "post", KT, "post_g", src=0, add=True)
        if stop == "l1":
            k.dump_res = True
            return dump(k)
        norm(k, "a", KT, "a_norm")
        w = dram["a_w_in_2"][0, :, :]
        project(k, [(8, CQ0, columns(w, 0), P, None), (1, KPE0, columns(w, 1024, width=64), 64, None),
                    (KT, AG0, columns(w, 1088), P, "silu")], KT)
        norm(k, "q", 4, "q_norm", src=CQ0)
        norm(k, "kv", 4, "kv_norm", src=CKV0, dst=4)
        wq, wkv = dram["a_w_q_up_2"][0, :, :], dram["a_w_kv_up_2"][0, :, :]
        project(k, [(AH, QN0, columns(wq, 0, step=192), P, None), (AH // 2, QR0, rope_columns(wq), P, None)], 4)
        project(k, [(2 * AH, KV0, columns(wkv, 0), P, None)], 4, rhs0=4)
        positions(k, "a_", rope=True)
        mla(k)
        if stop == "mla":
            return dump(k)
        project(k, [(KT, 0, columns(dram["a_w_out_2"][0, :, :], 0), P, None)], KT, add=True)
        if stop == "l2":
            k.dump_res = True
            return dump(k)
        norm(k, "b", KT, "b_norm")
        w = dram["b_w_in_2"][0, :, :]
        project(k, [(48, 0, columns(w, 0), P, None), (KT, BG0, columns(w, 48 * P), P, "silu")], KT)
        positions(k, "b_", rope=False)
        diff(k)
        project(k, [(KT, 0, columns(dram["b_w_out_2"][0, :, :], 0), P, None)], KT, add=True)
        write_out(k)


def dump(k):
    nc = k.nc
    o = k.sem("dumped")
    with nc.Block() as block:
        @block.sync
        def _(sp):
            sp.dma_start(k.d["out"][0, :, :].rearrange("(a b) n -> a (b n)", a=P), (k.RES if k.dump_res else f32(k.XH[:, :, :]))[:, :, :].rearrange("p k t -> p (k t)")).then_inc(o, 16)
            sp.wait_ge(o, 16)


def kernel(**inputs):
    import concourse.bacc as bacc
    from concourse.bass_utils import run_bass_kernel_spmd

    consts, onehot = constants()
    arrays = {n: np.ascontiguousarray(a) for n, a in inputs.items()}
    arrays["consts"], arrays["onehot"] = consts, onehot
    nc = bacc.Bacc("TRN2", target_bir_lowering=False, num_devices=1)
    dram = {n: nc.dram_tensor(n, a.shape, mybir.dt.from_np(a.dtype), kind="ExternalInput").ap() for n, a in arrays.items()}
    dram["out"] = nc.dram_tensor("out", (1, T, D), F32, kind="ExternalOutput").ap()
    build(nc, dram)
    result = run_bass_kernel_spmd(nc, [arrays], core_ids=[0])
    return result.results[0]["out"]
```

```python
from contextlib import ExitStack, contextmanager

import numpy as np

import concourse.bass as bass
from concourse import mybir

F32 = mybir.dt.float32
F32R = mybir.dt.float32r
I32 = mybir.dt.int32
ALU = mybir.AluOpType
ACT = mybir.ActivationFunctionType
AX = mybir.AxisListType.X

P = 128
T = 512
TB = T // P
D = 2048
KT = D // P
BIG = 1e30
MAX_FLOOR = 1e20
EPS = 1e-6

NH, NKV, HD = 8, 2, 128
CMP, STRIDE = 32, 16
NCMP = (T - CMP) // STRIDE + 1
RW = 1024
NPAIR = RW // P
CH = 64
NCH = T // CH
LEVELS = [1, 2, 4, 8, 16, 32]
GN_EPS = 64e-5
NBUCKET, MAXDIST = 32, 1024
Q0, KC0, VC0, KS0, VS0, KW0, VW0, G0 = 0, 8, 10, 12, 14, 16, 18, 20
ZA0 = 21
R0, K0, V0, WA0 = 29, 37, 45, 53
ZB0 = 54
NGATE = 24
AH, AV = 16, 128
CQ0, CKV0, KPE0, AG0 = 0, 4, 8, 9
QN0, QR0, KV0 = 25, 41, 49
BH = 8
BQ0, BK0, BV0, BG0 = 0, 16, 32, 48
LAM_INIT = 0.8 - 0.6 * float(np.exp(-0.3))
NPROJ = 81
ARENA = 16032
ARENA2 = 4 * D

CONST = dict(ident=128, ones=128, bones=128, hone0=128, hone1=128, swap=128, flip=128, mt=512,
             lev=(1 + len(LEVELS)) * 128, cmask=2, rst=512, freq=1, nslope=8)


def const_cols():
    at, out = 0, {}
    for k, n in CONST.items():
        out[k] = (at, n)
        at += n
    return out, at


def constants():
    cols, n = const_cols()
    c = np.zeros((P, n), np.float32)
    i = np.arange(P)

    def put(name, a):
        at, w = cols[name]
        c[:, at:at + w] = a

    put("ident", np.eye(P))
    put("ones", 1.0)
    put("flip", np.eye(P)[::-1])
    put("bones", (i[:, None] // 64 == i[None, :] // 64))
    put("hone0", np.repeat((i < 64)[:, None], P, 1))
    put("hone1", np.repeat((i >= 64)[:, None], P, 1))
    swap = np.zeros((P, P))
    for m in range(P):
        if m % 64 < 32:
            swap[m + 32, m] = -1.0
        else:
            swap[m - 32, m] = 1.0
    put("swap", swap)
    same = i[:, None] // CH == i[None, :] // CH
    strict = same & (i[:, None] < i[None, :])
    incl = same & (i[:, None] <= i[None, :])
    put("mt", np.concatenate([strict, incl, strict, incl], 1))
    put("cmask", (i[:, None] // CH == np.arange(2)[None]))
    lev = []
    for m in LEVELS:
        low = (i[:, None] // (2 * m) == i[None, :] // (2 * m)) & (i[:, None] % (2 * m) >= m) & (i[None, :] % (2 * m) < m)
        lev += [low, low.T] if m == 1 else [low.T]
    put("lev", np.concatenate(lev, 1))
    put("rst", np.repeat((np.arange(T) % CH != 0)[None], P, 0))
    freq = np.float32(10000.0) ** (-np.arange(0, 64, 2, dtype=np.float32) / np.float32(64))
    put("freq", freq[i % 32][:, None])
    put("nslope", np.repeat(-(2.0 ** -(np.arange(1, BH + 1) * 8.0 / BH))[None], P, 0))
    dist = np.arange(-(T - 1), T)
    nd = np.maximum(dist, 0)
    nf = np.maximum(nd, 1).astype(np.float32)
    half = NBUCKET // 2
    large = half + (np.log(nf / np.float32(half)) / np.float32(np.log(MAXDIST / half)) * np.float32(half)).astype(np.int32)
    b = np.where(nd < half, nd, np.minimum(large, NBUCKET - 1))
    b = np.where(dist < 0, NBUCKET, b)
    oh = (np.arange(NBUCKET + 1)[:, None] == b[None]).astype(np.float32)
    return c, np.ascontiguousarray(oh[:, ::-1][:, :T + P])


ROWS0 = [("pre_g", 16), ("mu", 25), ("w0", 8), ("a0", 8), ("k_k", 8), ("k_a", 8), ("r_k", 8), ("ln_w", 8),
         ("ln_b", 8), ("post_g", 16)]
ROWS1 = [("a_norm", 16), ("q_norm", 4), ("kv_norm", 4), ("q_gain", 2), ("k_gain", 2), ("b_norm", 16),
         ("bq_gain", 1), ("bk_gain", 1), ("subln", 2), ("lam", 4), ("pos_k", 32), ("pos_v", 32)]


def param_cols():
    out = {}
    for base, rows in ((0, ROWS0), (P, ROWS1)):
        at = base
        for name, n in rows:
            out[name] = at
            at += n
        assert at - base <= P
    return out


PC = param_cols()


def loop(eng, n, body):
    turns = n // 2
    if turns >= 2:
        with eng.Fori(0, turns) as it:
            body(it * 2, 0)
            body(it * 2 + 1, 1)
    else:
        turns = 0
    for i in range(2 * turns, n):
        body(i, i % 2)


class Kernel:

    def __init__(self, nc, ctx, dram):
        self.nc, self.ctx, self.d = nc, ctx, dram
        cc, nconst = const_cols()
        self.RES = self.sb("RES", [P, KT, T])
        self.XH = self.sb("XH", [P, KT, T], F32R)
        self.XL = self.sb("XL", [P, KT, T], F32R)
        self.C = self.sb("C", [P, nconst])
        self.PRM = self.sb("PRM", [P, 2 * P])
        self.STG = self.sb("STG", [P, 2, T])
        self.AR = self.sb("AR", [P, ARENA])
        self.PSB = [ctx.enter_context(nc.psum_tensor(f"PS{i}", [P, T], F32)) for i in range(8)]
        self.PROJ = nc.dram_tensor("proj_scratch", [NPROJ, P, T], F32).ap()
        self.FBIAS = nc.dram_tensor("bias_scratch", [NH, T + P], F32).ap()
        w = KT * P
        self.nw = 0
        self.WRAW = [self.AR[:, j * w:(j + 1) * w].rearrange("p (k n) -> p k n", n=P) for j in range(2)]
        self.SG = [self.AR[:, 2 * w + j * T:2 * w + (j + 1) * T] for j in range(2)]
        self.cc = cc
        self.dump_res = False
        self.nt = 0
        self.ng = 0
        self.ns = 0
        s = self.sem
        self.w_loaded = [s(f"w_loaded{j}") for j in range(2)]
        self.w_hi = s("w_hi")
        self.w_split = s("w_split")
        self.tile_done = s("tile_done")
        self.bank_free = s("bank_free")
        self.sig_done = s("sig_done")
        self.stored = [s(f"stored{j}") for j in range(2)]
        self.norm_sems = [s("norm_" + x) for x in ("y_in", "squares", "summed", "mean", "root", "rsqrt", "normed", "hi", "lo", "lo_pool")]
        self.norm_counts = [0] * 10

    @contextmanager
    def weights(self):
        self.nw += 1
        with self.nc.sbuf_tensor(f"WHT{self.nw}", [P, 2, KT, P], F32R) as WHT, self.nc.sbuf_tensor(f"WLT{self.nw}", [P, 2, KT, P], F32R) as WLT:
            self.WH = [WHT[:, j, :, :] for j in range(2)]
            self.WL = [WLT[:, j, :, :] for j in range(2)]
            yield

    @contextmanager
    def more(self):
        self.nw += 1
        with self.nc.sbuf_tensor(f"AR{self.nw}", [P, ARENA2], F32) as AR2:
            self.AR2 = AR2
            yield

    def sb(self, name, shape, dt=F32):
        return self.ctx.enter_context(self.nc.sbuf_tensor(name, shape, dt))

    def sem(self, name):
        return self.ctx.enter_context(self.nc.semaphore(name))

    def c(self, name, a=0, b=None):
        at, n = self.cc[name]
        return self.C[:, at + a:at + (n if b is None else b)]

    def prm(self, name, i=0):
        return self.PRM[:, bass.ds(i + PC[name], 1)]

    def arena(self, *sizes):
        at, out = 0, []
        for n in sizes:
            out.append(self.AR[:, at:at + n])
            at += n
        assert at <= ARENA, at
        return out


def r32(ap):
    return ap.bitcast(F32R)


def f32(ap):
    return ap.bitcast(F32)


def setup(k):
    nc, d = k.nc, k.d
    X = k.AR[:, 0:TB * D].rearrange("p (b n) -> p b n", n=D)
    rows = k.AR[:, TB * D:TB * D + 2 * P].rearrange("p (b n) -> p b n", n=P)
    c_in, r_in, x_in, x_in2 = k.sem("consts_in"), k.sem("rows_in"), k.sem("x_in"), k.sem("x_in2")
    r_t, r_c = k.sem("rows_turned"), k.sem("rows_copied")
    x_t, x_c = k.sem("x_turned"), k.sem("x_copied")
    rz = k.sem("rows_zeroed")
    nrow = []

    with nc.Block() as block:
        @block.sync
        def _(sp):
            sp.dma_start(k.C[:, :], d["consts"]).then_inc(c_in, 16)
            sp.dma_start(X[:, 0:2, :], d["x"][0, 0:2 * P, :].rearrange("(b p) n -> p b n", p=P)).then_inc(x_in, 16)
            sp.dma_start(X[:, 2:4, :], d["x"][0, 2 * P:T, :].rearrange("(b p) n -> p b n", p=P)).then_inc(x_in2, 16)
            sp.wait_ge(rz, 1)
            for b, table in ((0, ROWS0), (1, ROWS1)):
                at = 0
                for name, n in table:
                    if name in ("q_gain", "k_gain"):
                        src = d[f"a_{name}_2"]
                        parts = [(0, 0, src[0:1, 0:P]), (1, 0, src[0:1, P:192]), (1, 64, src[0:1, P:192])]
                    elif name == "lam":
                        parts = [(i, 0, d[x][0:1, :]) for i, x in enumerate(
                            ("b_lambda_q1_2", "b_lambda_k1_2", "b_lambda_q2_2", "b_lambda_k2_2"))]
                    elif name in ("pos_k", "pos_v"):
                        parts = [(0, 0, d["cmp_" + name][0, :, :])]
                    else:
                        src = {"pre_g": "pre_norm_g", "mu": "rwkv_mu", "w0": "rwkv_w0", "a0": "rwkv_a0",
                               "k_k": "rwkv_k_k", "k_a": "rwkv_k_a", "r_k": "rwkv_r_k", "ln_w": "rwkv_ln_w",
                               "ln_b": "rwkv_ln_b", "post_g": "post_norm_g", "a_norm": "a_norm_2",
                               "q_norm": "a_q_norm_2", "kv_norm": "a_kv_norm_2", "b_norm": "b_norm_2",
                               "bq_gain": "b_q_gain_2", "bk_gain": "b_k_gain_2", "subln": "b_subln_2"}[name]
                        v = d[src]
                        v = v[0, :, :].rearrange("h n -> (h n)") if name == "r_k" else v[0, :]
                        parts = [(0, 0, v.rearrange("(r c) -> r c", c=P))]
                    for r, cc, src in parts:
                        m, w = src.shape
                        sp.dma_start(rows[at + r:at + r + m, b, cc:cc + w], src).then_inc(r_in, 16)
                        nrow.append(1)
                    at += n

        @block.gpsimd
        def _(pool):
            nc.gpsimd.memset(rows, 0.0).then_inc(rz, 1)
            pool.sem_inc(k.w_split, 2)
            pool.sem_inc(k.tile_done, 2)
            pool.sem_inc(k.bank_free, 2)
            pool.sem_inc(k.stored[0], 16)
            pool.sem_inc(k.stored[1], 16)

        @block.tensor
        def _(pe):
            pe.wait_ge(c_in, 16)
            pe.wait_ge(x_in, 16)
            pe.wait_ge(x_in2, 16)
            for c in range(KT):
                if c >= 4:
                    pe.wait_ge(x_c, c - 3)
                for b in range(TB):
                    last = nc.tensor.transpose(k.PSB[c % 4][:, b * P:(b + 1) * P], X[:, b, c * P:(c + 1) * P], k.c("ident"))
                last.then_inc(x_t, 1)
            pe.wait_ge(r_in, 16 * len(nrow))
            for b in range(2):
                last = nc.tensor.transpose(k.PSB[7][:, b * P:(b + 1) * P], rows[:, b, :], k.c("ident"))
            last.then_inc(r_t, 1)

        @block.vector
        def _(dve):
            dve.wait_ge(r_t, 1)
            nc.vector.tensor_copy(k.PRM[:, :], k.PSB[7][:, 0:2 * P]).then_inc(r_c, 1)

        @block.scalar
        def _(act):
            for c in range(KT):
                act.wait_ge(x_t, c + 1)
                nc.scalar.activation(k.RES[:, c, :], k.PSB[c % 4][:, :], ACT.Copy).then_inc(x_c, 1)


def norm(k, n, gain, src=None, dst=0, add=False, ahead=None):
    nc = k.nc
    Y = k.AR[:, 0:n * T].rearrange("p (c t) -> p c t", t=T) if src is not None else k.RES
    _, sq0, sq1, rs, r1, *TM = k.arena(KT * T, *[T] * 8)
    SQ = (sq0, sq1)
    bank = k.PSB[6]
    y_in, sq_in, sq_used, st, sr, ri, tn, th, tl, tp = k.norm_sems
    at = dict(zip(k.norm_sems, k.norm_counts))

    with nc.Block() as block:
        if src is not None:
            @block.sync
            def _(sp):
                sp.dma_start(Y, k.PROJ[src:src + n, :, :].rearrange("c p t -> p c t")).then_inc(y_in, 16)

        @block.scalar
        def _(act):
            if src is not None:
                act.wait_ge(y_in, at[y_in] + 16)
            for c in range(n):
                if c >= 2:
                    act.wait_ge(sq_used, at[sq_used] + c - 1)
                nc.scalar.activation(SQ[c % 2], Y[:, c, :], ACT.Square).then_inc(sq_in, 1)
            act.wait_ge(st, at[st] + 1)
            nc.scalar.activation(rs, r1, ACT.Sqrt).then_inc(sr, 1)
            if not add:
                for c in range(n):
                    act.wait_ge(tn, at[tn] + c + 1)
                    nc.scalar.activation(k.XH[:, dst + c, :], TM[c % 4], ACT.Copy).then_inc(th, 1)

        if ahead is not None:
            @block.sync
            def _(sp):
                for i in range(2):
                    j = (k.nt + i) % 2
                    sp.wait_ge(k.w_split, k.nt + i + 1)
                    for to, frm in ahead(k.WRAW[j], i):
                        sp.dma_start(to, frm).then_inc(k.w_loaded[j], 16)

        def low(engine, c, done):
            engine.tensor_tensor(k.XL[:, dst + c, :], TM[c % 4], f32(k.XH[:, dst + c, :]), ALU.subtract).then_inc(done, 1)

        if not add:
            @block.gpsimd
            def _(pool):
                for c in range(0, n, 2):
                    pool.wait_ge(th, at[th] + c + 1)
                    low(nc.gpsimd, c, tp)

        @block.tensor
        def _(pe):
            for c in range(n):
                pe.wait_ge(sq_in, at[sq_in] + c + 1)
                nc.tensor.matmul(bank[:, :], k.c("ones"), SQ[c % 2], start=(c == 0), stop=(c == n - 1)).then_inc(sq_used, 1)

        @block.vector
        def _(dve):
            dve.wait_ge(sq_used, at[sq_used] + n)
            nc.vector.tensor_scalar(r1, bank[:, :], 1.0 / (n * P), EPS, ALU.mult, ALU.add).then_inc(st, 1)
            dve.wait_ge(sr, at[sr] + 1)
            nc.vector.reciprocal(rs, rs).then_inc(ri, 1)
            dve.wait_ge(ri, at[ri] + 1)
            for c in range(n):
                g = k.prm(gain, c)
                if add:
                    nc.vector.scalar_tensor_tensor(out=TM[c % 2], in0=Y[:, c, :], scalar=g, in1=rs, op0=ALU.mult, op1=ALU.mult).then_inc(tn, 1)
                    dve.wait_ge(tn, at[tn] + c + 1)
                    nc.vector.tensor_tensor(k.RES[:, c, :], k.RES[:, c, :], TM[c % 2], ALU.add).then_inc(tl, 1)
                    if c < n - 1:
                        dve.wait_ge(tl, at[tl] + c + 1)
                    continue
                if c >= 4:
                    if c % 2:
                        dve.wait_ge(tl, at[tl] + (c - 4) // 2 + 1)
                    else:
                        dve.wait_ge(tp, at[tp] + (c - 4) // 2 + 1)
                nc.vector.scalar_tensor_tensor(out=TM[c % 4], in0=Y[:, c, :], scalar=g, in1=rs, op0=ALU.mult, op1=ALU.mult).then_inc(tn, 1)
                if c >= 2 and c % 2 == 0:
                    dve.wait_ge(th, at[th] + c)
                    low(nc.vector, c - 1, tl)
            if not add:
                dve.wait_ge(th, at[th] + n)
                low(nc.vector, n - 1, tl)
    done = (16 if src is not None else 0, n, n, 1, 1, 1, n, 0 if add else n, n if add else n // 2, 0 if add else n // 2)
    k.norm_counts = [a + b for a, b in zip(k.norm_counts, done)]


def project(k, segments, kt, rhs0=0, add=False, ahead=False):
    nc = k.nc
    plan = []
    nt, ns, ng = k.nt, k.ns, k.ng
    for n, out, load, width, func in segments:
        plan.append((n, out, load, width, nt, ns, func, ng))
        ng += n if func else 0
        nt += n
        if not add:
            ns += n
    k.nt, k.ns, k.ng = nt, ns, ng

    with nc.Block() as block:
        @block.sync
        def _(sp):
            for n, out, load, width, b, s, func, ng0 in plan:
                def step(i, par):
                    j = (b + par) % 2
                    sp.wait_ge(k.w_split, i + (b + 1))
                    for dst, src in load(k.WRAW[j], i):
                        sp.dma_start(dst, src).then_inc(k.w_loaded[j], 16)
                if ahead and b == plan[0][4]:
                    loop(sp, n - 2, lambda i, par: step(i + 2, par))
                else:
                    loop(sp, n, step)
            if not add:
                for j in range(2):
                    done = sum(1 for x in range(ns) if x % 2 == j)
                    sp.wait_ge(k.stored[j], 16 * done + 16)

        @block.scalar
        def _(act):
            flat = [(p, i) for p in plan for i in range(p[0])]

            def hi(i, par, p):
                b = p[4]
                j = (b + par) % 2
                act.wait_ge(k.w_loaded[j], (i - par) * 16 + 32 * ((b + par) // 2 + 1))
                act.wait_ge(k.tile_done, i + (b + 1))
                nc.scalar.activation(k.WH[j][:, 0:kt, 0:p[3]], k.WRAW[j][:, 0:kt, 0:p[3]], ACT.Copy).then_inc(k.w_hi, 1)

            def sigmoid(i, par, p):
                act.wait_ge(k.tile_done, i + (p[4] + 3))
                j = (p[4] + par) % 2
                nc.scalar.activation(k.SG[j][0:p[3], :], k.PSB[j][0:p[3], :], ACT.Sigmoid).then_inc(k.sig_done, 1)

            def store(i, par, p):
                if p[6]:
                    sigmoid(i, par, p)
                act.wait_ge(k.bank_free, i + (p[4] + 3))
                act.dma_start(k.PROJ[p[1] + i, 0:p[3], :], k.STG[0:p[3], (p[5] + par) % 2, :]).then_inc(k.stored[(p[5] + par) % 2], 16)

            hi(0, 0, plan[0])
            for x, p in enumerate(plan):
                def step(i, par):
                    hi(i + 1, 1 - par if par == 0 else 2, p)
                    if not add:
                        store(i, par, p)
                loop(act, p[0] - 1, step)
                last = p[0] - 1
                if x + 1 < len(plan):
                    hi(0, 0, plan[x + 1])
                if not add:
                    store(last, last % 2, p)

        @block.vector
        def _(dve):
            def lo(i, par, p):
                j = (p[4] + par) % 2
                dve.wait_ge(k.w_hi, i + (p[4] + 1))
                nc.vector.tensor_tensor(k.WL[j][:, 0:kt, 0:p[3]], k.WRAW[j][:, 0:kt, 0:p[3]], f32(k.WH[j][:, 0:kt, 0:p[3]]), ALU.subtract).then_inc(k.w_split, 1)

            def evac(i, par, p):
                bank = k.PSB[(p[4] + par) % 2]
                dve.wait_ge(k.tile_done, i + (p[4] + 3))
                if add:
                    nc.vector.tensor_tensor(k.RES[:, i, :], bank[:, :], k.RES[:, i, :], ALU.add).then_inc(k.bank_free, 1)
                else:
                    s = (p[5] + par) % 2
                    dve.wait_ge(k.stored[s], (i - par) * 8 + 16 * ((p[5] + par) // 2 + 1))
                    sg = k.SG[(p[4] + par) % 2][0:p[3], :]
                    if p[6]:
                        dve.wait_ge(k.sig_done, i + (p[7] + 1))
                    if p[6] == "silu":
                        nc.vector.tensor_tensor(k.STG[0:p[3], s, :], bank[0:p[3], :], sg, ALU.mult).then_inc(k.bank_free, 1)
                    elif p[6] == "sigmoid":
                        nc.vector.tensor_copy(k.STG[0:p[3], s, :], sg).then_inc(k.bank_free, 1)
                    else:
                        nc.vector.tensor_copy(k.STG[0:p[3], s, :], bank[0:p[3], :]).then_inc(k.bank_free, 1)

            lo(0, 0, plan[0])
            for x, p in enumerate(plan):
                def step(i, par):
                    lo(i + 1, 1 - par if par == 0 else 2, p)
                    evac(i, par, p)
                loop(dve, p[0] - 1, step)
                last = p[0] - 1
                if x + 1 < len(plan):
                    lo(0, 0, plan[x + 1])
                evac(last, last % 2, p)

        @block.tensor
        def _(pe):
            for n, out, load, width, b, s, func, ng0 in plan:
                def step(i, par):
                    j = (b + par) % 2
                    pe.wait_ge(k.w_split, i + (b + 3))
                    pe.wait_ge(k.bank_free, i + (b + 1))
                    bank = k.PSB[j]
                    for c in range(kt):
                        wh, wl = k.WH[j][:, c, 0:width], k.WL[j][:, c, 0:width]
                        xh, xl = k.XH[:, rhs0 + c, :], k.XL[:, rhs0 + c, :]
                        nc.tensor.matmul(bank[0:width, :], wh, xh, start=(c == 0), stop=False)
                        nc.tensor.matmul(bank[0:width, :], wh, xl, start=False, stop=False)
                        last = nc.tensor.matmul(bank[0:width, :], wl, xh, start=False, stop=(c == kt - 1))
                    last.then_inc(k.tile_done, 1)
                loop(pe, n, step)


def columns(w, c0, step=P, width=P):
    half = w.shape[0] // P // 2

    def load(dst, i):
        src = w[:, bass.ds(i * step + c0, width)].rearrange("(k p) n -> p k n", p=P)
        return [(dst[:, a:a + half, 0:width], src[:, a:a + half, :]) for a in (0, half)]
    return load


def rope_columns(w):
    def load(dst, i):
        return [(dst[:, 0:w.shape[0] // P, 64 * e:64 * e + 64],
                 w[:, bass.ds(i * 384 + (192 * e + 128), 64)].rearrange("(k p) n -> p k n", p=P)) for e in (0, 1)]
    return load


def nsa_setup(k):
    nc, d = k.nc, k.d
    A = nsa_arena(k)
    E, KCT, VC, G, VT = A["E"], A["KCT"], A["VC"], A["G"], A["VT"]
    OH, W1, W1F, W2, KV, CST, SIGM, HB, VIN, FB, TAB = (A[x] for x in ("OH", "W1", "W1F", "W2", "KV", "CST", "SIGM", "HB", "VIN", "FB", "TAB"))
    NC2 = NKV * NCMP
    tab0, tab_in, oh_in = k.sem("table_padded"), k.sem("table_in"), k.sem("onehot_in")
    fb_mm, fb_c, fb_out, e_in = k.sem("bias_row"), k.sem("bias_row_copied"), k.sem("bias_row_out"), k.sem("bias_in")
    w1_in = [k.sem(f"cmp_{x}_in") for x in "kv"]
    h_mm, c_c, s_s, hb, o_mm, o_c = (k.sem("cmp_" + x) for x in ("hidden", "const", "sigmoid", "silu", "out", "copied"))
    v_in, v_t, v_c = k.sem("nsa_v_in"), k.sem("nsa_v_turned"), k.sem("nsa_v_copied")
    g_in = k.sem("nsa_gates_in")
    z0 = k.sem("cmp_zeroed")
    e_mm, e_c = k.sem("bias_flipped"), k.sem("bias_copied")
    VTILES = [KS0 + 2, KS0 + 3, KW0 + 2, KW0 + 3, G0]

    with nc.Block() as block:
        @block.sync
        def _(sp):
            sp.wait_ge(tab0, 1)
            sp.dma_start(TAB[0:NBUCKET, :], d["rel_bias_table"]).then_inc(tab_in, 16)
            sp.dma_start(OH, d["onehot"]).then_inc(oh_in, 16)
            for n, (c0, w1, w2) in enumerate(((KC0, "cmp_k_w1", "cmp_k_w2"), (VC0, "cmp_v_w1", "cmp_v_w2"))):
                for a in range(0, CMP, 16):
                    sp.dma_start(W1[n][:, a:a + 16, :], d[w1][0, a * P:(a + 16) * P, :].rearrange("(l p) e -> p l e", p=P)).then_inc(w1_in[n], 16)
                sp.dma_start(W2[n], d[w2][0, :, :]).then_inc(w1_in[n], 16)
                sp.dma_start(KV[n], k.PROJ[c0:c0 + 2, :, :].rearrange("g p t -> p g t")).then_inc(w1_in[n], 16)
                if n == 0:
                    sp.wait_ge(fb_c, 2)
                    sp.dma_start(k.FBIAS, FB[0:NH, :]).then_inc(fb_out, 16)
            sp.dma_start(VIN[:, 0:2, :], k.PROJ[KS0 + 2:KS0 + 4, :, :].rearrange("g p t -> p g t")).then_inc(v_in, 16)
            sp.dma_start(VIN[:, 2:4, :], k.PROJ[KW0 + 2:KW0 + 4, :, :].rearrange("g p t -> p g t")).then_inc(v_in, 16)
            sp.dma_start(k.STG[0:NGATE, 0, :], k.PROJ[G0, 0:NGATE, :]).then_inc(g_in, 16)
            sp.wait_ge(fb_out, 16)
            sp.dma_start(W1F, bass.AP(k.FBIAS.tensor, 0, [[1, P], [T + P, NH], [1, T]])).then_inc(e_in, 16)

        @block.gpsimd
        def _(pool):
            nc.gpsimd.memset(TAB, -BIG).then_inc(tab0, 1)
            nc.gpsimd.memset(VC, 0.0).then_inc(z0, 1)

        @block.tensor
        def _(pe):
            pe.wait_ge(tab_in, 16)
            pe.wait_ge(oh_in, 16)
            nc.tensor.matmul(k.PSB[0][0:NH, :], TAB, OH[:, 0:T], start=True, stop=True).then_inc(fb_mm, 1)
            nc.tensor.matmul(k.PSB[1][0:NH, 0:P], TAB, OH[:, T:T + P], start=True, stop=True).then_inc(fb_mm, 1)
            for n in range(2):
                pe.wait_ge(w1_in[n], 64)
                if n:
                    pe.wait_ge(hb, 1)
                for l in range(CMP):
                    nc.tensor.matmul(k.PSB[4][:, 0:NC2].rearrange("p (g i) -> p g i", i=NCMP), W1[n][:, l, :], KV[n][:, :, l:l + STRIDE * (NCMP - 1) + 1:STRIDE], start=(l == 0), stop=(l == CMP - 1))
                for l in range(CMP):
                    last = nc.tensor.matmul(k.PSB[5][:, 0:1], W1[n][:, l, :], k.prm(("pos_k", "pos_v")[n], l), start=(l == 0), stop=(l == CMP - 1))
                last.then_inc(h_mm, 1)
                pe.wait_ge(hb, n + 1)
                if n == 0:
                    nc.tensor.matmul(k.PSB[6][:, 0:NC2], W2[n], HB, start=True, stop=True).then_inc(o_mm, 1)
                else:
                    pe.wait_ge(o_c, 1)
                    for g in range(NKV):
                        last = nc.tensor.matmul(k.PSB[6][0:NCMP, g * HD:(g + 1) * HD], HB[:, g * NCMP:(g + 1) * NCMP], W2[n], start=True, stop=True)
                    last.then_inc(o_mm, 1)
            for n, c in enumerate(VTILES):
                if n == 0:
                    pe.wait_ge(v_in, 32)
                if c == G0:
                    pe.wait_ge(g_in, 16)
                if n >= 2:
                    pe.wait_ge(v_c, n - 1)
                src = k.STG[:, 0, :] if c == G0 else VIN[:, n, :]
                rows = NGATE if c == G0 else P
                for tb in range(TB):
                    last = nc.tensor.transpose(k.PSB[n % 2][:, tb * P:tb * P + rows], src[0:rows, tb * P:(tb + 1) * P], k.c("ident")[0:rows, 0:rows])
                last.then_inc(v_t, 1)
            pe.wait_ge(e_in, 16)
            for h in range(NH):
                if h >= 2:
                    pe.wait_ge(e_c, h - 1)
                nc.tensor.matmul(k.PSB[2 + h % 2][:, :], k.c("flip"), W1F[:, h, :], start=True, stop=True).then_inc(e_mm, 1)

        @block.vector
        def _(dve):
            dve.wait_ge(fb_mm, 2)
            nc.vector.tensor_copy(FB[0:NH, 0:T], k.PSB[0][0:NH, :]).then_inc(fb_c, 1)
            nc.vector.tensor_copy(FB[0:NH, T:T + P], k.PSB[1][0:NH, 0:P]).then_inc(fb_c, 1)
            for n in range(2):
                dve.wait_ge(h_mm, n + 1)
                if n:
                    dve.wait_ge(s_s, 1)
                nc.vector.tensor_copy(CST, k.PSB[5][:, 0:1]).then_inc(c_c, 1)
                dve.wait_ge(s_s, n + 1)
                if n:
                    dve.wait_ge(o_mm, 1)
                nc.vector.scalar_tensor_tensor(out=HB, in0=k.PSB[4][:, 0:NC2], scalar=CST, in1=SIGM, op0=ALU.add, op1=ALU.mult).then_inc(hb, 1)
                dve.wait_ge(o_mm, n + 1)
                if n == 0:
                    nc.vector.tensor_copy(KCT, k.PSB[6][:, 0:NC2]).then_inc(o_c, 1)
                else:
                    dve.wait_ge(z0, 1)
                    nc.vector.tensor_copy(VC[0:NCMP, :], k.PSB[6][0:NCMP, 0:NKV * HD]).then_inc(o_c, 1)
            for n, c in enumerate(VTILES):
                dve.wait_ge(v_t, n + 1)
                src = k.PSB[n % 2][:, :].rearrange("p (b c) -> p b c", c=P)
                if c == G0:
                    nc.vector.tensor_copy(G, src[:, :, 0:NGATE]).then_inc(v_c, 1)
                else:
                    nc.vector.tensor_copy(VT[:, n // 2, n % 2, :, :], src).then_inc(v_c, 1)
            for h in range(NH):
                dve.wait_ge(e_mm, h + 1)
                nc.vector.tensor_copy(E[:, h, :], k.PSB[2 + h % 2][:, :]).then_inc(e_c, 1)

        @block.scalar
        def _(act):
            for n in range(2):
                act.wait_ge(c_c, n + 1)
                if n:
                    act.wait_ge(hb, 1)
                nc.scalar.activation(SIGM, k.PSB[4][:, 0:NC2], ACT.Sigmoid, bias=CST).then_inc(s_s, 1)


def nsa_arena(k):
    parts = dict(E=NH * T, KCT=64, VC=NKV * HD, G=TB * NGATE, VT=4 * TB * HD)
    at = dict(zip(parts, k.arena(*parts.values())))
    used = sum(parts.values())
    free = k.AR[:, used:ARENA]

    def lay(sizes):
        o, out = 0, {}
        for n, w in sizes.items():
            out[n] = free[:, o:o + w]
            o += w
        assert o <= ARENA - used, (o, ARENA - used)
        return out

    s = lay(dict(W1=CMP * P, W2=2 * P, KV=2 * NKV * T, CST=1, SIGM=NKV * NCMP, HB=NKV * NCMP, TAB=NH, FB=T + P, VIN=4 * T))
    OHW = T + P
    h = lay(dict(KK=4 * T, S=3 * T, PTC=T, MX=24, TM=T))
    A = dict(E=at["E"].rearrange("p (h m) -> p h m", m=T), KCT=at["KCT"][:, 0:NKV * NCMP], VC=at["VC"], G=at["G"].rearrange("p (b n) -> p b n", n=NGATE),
             VT=at["VT"].rearrange("p (r g b d) -> p r g b d", r=2, g=NKV, b=TB),
             )
    A.update(W1=[x.rearrange("p (l e) -> p l e", e=P) for x in (s["W1"], k.AR2[:, 0:CMP * P])],
             W1F=k.AR2[:, CMP * P:CMP * P + NH * T].rearrange("p (h m) -> p h m", m=T),
             W2=[s["W2"][:, 0:P], s["W2"][:, P:2 * P]],
             KV=[s["KV"][:, n * NKV * T:(n + 1) * NKV * T].rearrange("p (g t) -> p g t", t=T) for n in range(2)],
             CST=s["CST"], SIGM=s["SIGM"], HB=s["HB"], TAB=s["TAB"][0:NBUCKET + 1, :], FB=s["FB"])
    A["OH"] = at["E"][0:NBUCKET + 1, 0:OHW]
    A["VIN"] = s["VIN"].rearrange("p (n t) -> p n t", t=T)
    A["KK"] = h["KK"].rearrange("p (r g t) -> p r g t", r=2, g=NKV)
    A["S"] = h["S"].rearrange("p (j t) -> p j t", t=T)
    A["PT"] = [k.AR2[:, j * 4 * T:(j + 1) * 4 * T].rearrange("p (b t) -> p b t", t=T) for j in range(2)]
    A["Z"] = [k.AR2[:, (8 + j) * T:(9 + j) * T] for j in range(2)]
    A["PTC"], A["MX"], A["TM"] = h["PTC"], h["MX"], h["TM"]
    A["Q"] = k.STG
    return A


def nsa_heads(k):
    nc, d = k.nc, k.d
    A = nsa_arena(k)
    E, KCT, VC, G, VT = A["E"], A["KCT"], A["VC"], A["G"], A["VT"]
    KK, S, PT, PTC, MX, Z, TM, Q = (A[x] for x in ("KK", "S", "PT", "PTC", "MX", "Z", "TM", "Q"))
    SCALE = HD ** -0.5
    BR = [(br, tb) for br in range(2) for tb in range(TB)] + [(2, tb) for tb in range(TB)]
    NI = len(BR)
    ITEMS = [(par, br, tb) for par in range(2) for br, tb in BR]
    HG = NH // NKV
    kk_in = k.sem("nsa_k_in")
    q_in = [k.sem(f"nsa_q_in{j}") for j in range(2)]
    z_in = [k.sem(f"nsa_z_in{j}") for j in range(2)]
    s_mm, s_b, s_max, s_exp = (k.sem("nsa_" + x) for x in ("scores", "biased", "max", "probs"))
    s_sum, s_rec, s_gate, s_p = (k.sem("nsa_" + x) for x in ("sum", "recip", "factor", "scaled"))
    s_red = k.sem("nsa_reduced")
    s_tr, s_pt = k.sem("nsa_turned"), k.sem("nsa_pt")
    s_pv = k.sem("nsa_pv")
    s_out, s_xh, s_xl = k.sem("nsa_out"), k.sem("nsa_hi"), k.sem("nsa_lo")
    s_z0 = k.sem("nsa_ptc_zero")

    def wid(br, tb):
        return ((tb + 1) * P - CMP) // STRIDE + 1 if br == 2 else (tb + 1) * P

    def bias_of(h, br, tb):
        m = (TB - 1 - tb) * P
        if br == 2:
            m += CMP - 1
            return E[:, h, m:m + STRIDE * (wid(2, tb) - 1) + 1:STRIDE]
        return E[:, h, m:T]

    with nc.Block() as block:
        @block.sync
        def _(sp):
            for r, c0 in ((0, KS0), (1, KW0)):
                sp.dma_start(KK[:, r, :, :], k.PROJ[c0:c0 + 2, :, :].rearrange("g p t -> p g t")).then_inc(kk_in, 16)

            def step(h, par):
                sp.wait_ge(s_mm, h * NI + 1)
                sp.dma_start(Q[:, par, :], k.PROJ[Q0 + h, :, :]).then_inc(q_in[par], 16)
                sp.wait_ge(s_out, h + 1)
                sp.dma_start(Z[par], k.PROJ[ZA0 + h, :, :]).then_inc(z_in[par], 16)
            loop(sp, NH, step)

        @block.tensor
        def _(pe):
            pe.sem_inc(s_mm, NI + 1)
            pe.sem_inc(s_pv, 3)
            pe.wait_ge(kk_in, 32)

            def pair(i, g):
                b = i * (2 * NI)

                def scores(n):
                    par, br, tb = ITEMS[n]
                    pe.wait_ge(s_b, b + (n + 1))
                    if n % NI == 0:
                        pe.wait_ge(q_in[par], i * 16 + 16)
                    q = Q[:, par, tb * P:(tb + 1) * P]
                    rhs = KCT[:, g * NCMP:g * NCMP + wid(2, tb)] if br == 2 else KK[:, br, g, 0:wid(br, tb)]
                    nc.tensor.matmul(k.PSB[n % 2][:, 0:wid(br, tb)], q, rhs, start=True, stop=True).then_inc(s_mm, 1)

                def turn(n):
                    par, br, tb = ITEMS[n]
                    pe.wait_ge(s_p, b + (n + 1))
                    pe.wait_ge(s_pt, b + (n + 1))
                    for kb in range(1 if br == 2 else tb + 1):
                        w = wid(2, tb) if br == 2 else P
                        last = nc.tensor.transpose(k.PSB[2 + n % 2][0:w, kb * P:(kb + 1) * P], S[:, n % 3, kb * P:kb * P + w], k.c("ident"))
                    last.then_inc(s_tr, 1)

                def values(v):
                    par, br = v // 3, v % 3
                    O = k.PSB[4 + par]
                    pe.wait_ge(s_pt, b + (4 * v + 4 + 2))
                    if br == 0:
                        pe.wait_ge(s_out, i * 2 + (par + 1))
                    if br < 2:
                        for kb in range(TB):
                            last = nc.tensor.matmul(O[:, kb * P:T], VT[:, br, g, kb, :], PT[br][:, kb, kb * P:T], start=(br == 0 and kb == 0), stop=False)
                    else:
                        last = nc.tensor.matmul(O[:, :], VC[:, g * HD:(g + 1) * HD], PTC, start=False, stop=True)
                    last.then_inc(s_pv, 1)

                scores(0)
                scores(1)
                scores(2)
                for n in range(2 * NI):
                    if n + 3 < 2 * NI:
                        scores(n + 3)
                    turn(n)
                    if n % 4 == 0 and n:
                        values(n // 4 - 1)
                values(5)
            for g in range(NKV):
                with pe.Fori(0, HG // 2) as it:
                    pair(it + g * (HG // 2), g)

        @block.vector
        def _(dve):
            dve.sem_inc(s_b, 2)
            dve.sem_inc(s_out, 2)
            nc.vector.memset(PTC, 0.0).then_inc(s_z0, 1)

            def bias(i, n):
                b = i * (2 * NI)
                par, br, tb = ITEMS[n]
                w = wid(br, tb)
                j = n % 3
                dve.wait_ge(s_mm, b + (n + NI + 2))
                dve.wait_ge(s_tr, b + (n + 1))
                h = i * 2 + par
                bb = bias_of(h, br, tb)
                nc.vector.scalar_tensor_tensor(out=S[:, j, 0:w], in0=k.PSB[n % 2][:, 0:w], scalar=SCALE, in1=bb, op0=ALU.mult, op1=ALU.add).then_inc(s_b, 1)
                dve.wait_ge(s_b, b + (n + 3))
                nc.vector.tensor_reduce(MX[:, j:j + 1], S[:, j, 0:w], AX, ALU.max, negate=True).then_inc(s_red, 1)
                dve.wait_ge(s_red, b + (n + 1))
                nc.vector.tensor_scalar(MX[:, 4 + j:5 + j], MX[:, j:j + 1], MAX_FLOOR, None, ALU.min).then_inc(s_max, 1)

            def scale(i, n):
                b = i * (2 * NI)
                par, br, tb = ITEMS[n]
                w = wid(br, tb)
                j = n % 3
                dve.wait_ge(s_exp, b + (n + 1))
                nc.vector.tensor_scalar(MX[:, 12 + j:13 + j], MX[:, 8 + j:9 + j], 1e-30, None, ALU.max).then_inc(s_sum, 1)
                dve.wait_ge(s_sum, b + (n + 1))
                nc.vector.reciprocal(MX[:, 16 + j:17 + j], MX[:, 12 + j:13 + j]).then_inc(s_rec, 1)
                dve.wait_ge(s_rec, b + (n + 1))
                gc = {0: 1, 1: 2, 2: 0}[br] * NH
                nc.vector.tensor_tensor(MX[:, 20 + j:21 + j], MX[:, 16 + j:17 + j], G[:, tb, bass.ds(i * 2 + (par + gc), 1)], ALU.mult).then_inc(s_gate, 1)
                dve.wait_ge(s_gate, b + (n + 1))
                nc.vector.tensor_scalar(S[:, j, 0:w], S[:, j, 0:w], MX[:, 20 + j:21 + j], None, ALU.mult).then_inc(s_p, 1)

            def output(i, par):
                dve.wait_ge(s_pv, i * 6 + (3 * par + 6))
                dve.wait_ge(z_in[par], i * 16 + 16)
                dve.wait_ge(s_xl, i * 2 + (par + 1))
                nc.vector.tensor_tensor(TM, k.PSB[4 + par][:, :], Z[par], ALU.mult).then_inc(s_out, 1)

            def low(i, par):
                dve.wait_ge(s_xh, i * 2 + (par + 1))
                nc.vector.tensor_tensor(k.XL[:, i * 2 + par, :], TM, f32(k.XH[:, i * 2 + par, :]), ALU.subtract).then_inc(s_xl, 1)

            def pair(i):
                bias(i, 0)
                bias(i, 1)
                for n in range(2 * NI):
                    if n + 2 < 2 * NI:
                        bias(i, n + 2)
                    scale(i, n)
                    if n == NI + 2:
                        output(i, 0)
                    if n == NI + 4:
                        low(i, 0)
                output(i, 1)
                low(i, 1)
            with dve.Fori(0, NH // 2) as it:
                pair(it)

        @block.scalar
        def _(act):
            act.sem_inc(s_pt, 2)
            act.sem_inc(s_tr, 3)
            act.sem_inc(s_xl, 1)
            act.wait_ge(s_z0, 1)

            def exps(i, n):
                par, br, tb = ITEMS[n]
                w = wid(br, tb)
                j = n % 3
                act.wait_ge(s_max, i * (2 * NI) + (n + 1))
                nc.scalar.activation(S[:, j, 0:w], S[:, j, 0:w], ACT.Exp, bias=MX[:, 4 + j:5 + j], accum_out=MX[:, 8 + j:9 + j]).then_inc(s_exp, 1)

            def copy(i, n):
                par, br, tb = ITEMS[n]
                act.wait_ge(s_tr, i * (2 * NI) + (n + 4))
                if n % 4 == 0:
                    act.wait_ge(s_pv, i * 6 + (n // 4 + 1))
                w = wid(br, tb)
                if br == 2:
                    nc.scalar.activation(PTC[0:w, tb * P:(tb + 1) * P], k.PSB[2 + n % 2][0:w, 0:P], ACT.Copy).then_inc(s_pt, 1)
                else:
                    nc.scalar.activation(PT[br][:, 0:tb + 1, tb * P:(tb + 1) * P], k.PSB[2 + n % 2][:, 0:(tb + 1) * P].rearrange("p (b t) -> p b t", t=P), ACT.Copy).then_inc(s_pt, 1)

            def high(i, par):
                act.wait_ge(s_out, i * 2 + (par + 3))
                nc.scalar.activation(k.XH[:, i * 2 + par, :], TM, ACT.Copy).then_inc(s_xh, 1)

            def pair(i):
                exps(i, 0)
                exps(i, 1)
                for n in range(2 * NI):
                    if n + 2 < 2 * NI:
                        exps(i, n + 2)
                    copy(i, n)
                    if n == NI + 3:
                        high(i, 0)
                high(i, 1)
            with act.Fori(0, NH // 2) as it:
                pair(it)


class Steps:

    def __init__(self, k, tag, **order):
        self.order = {e: {n: j for j, n in enumerate(names)} for e, names in order.items()}
        self.sem = {e: k.sem(f"{tag}_{e}") for e in order}
        self.n = {e: len(names) for e, names in order.items()}
        for e, names in order.items():
            assert len(set(names)) == len(names)
        self.next = dict.fromkeys(order, 0)

    def begin(self, eng, e):
        eng.sem_inc(self.sem[e], self.n[e] + 1)

    def turn(self, eng, i, *engines):
        for e in engines:
            eng.wait_ge(self.sem[e], i * self.n[e] + (self.n[e] + 1))

    def wait(self, eng, i, *steps):
        for s in steps:
            e, name = s.split(".")
            eng.wait_ge(self.sem[e], i * self.n[e] + (self.n[e] + self.order[e][name] + 2))

    def before(self, eng, i, *steps):
        for s in steps:
            e, name = s.split(".")
            eng.wait_ge(self.sem[e], i * self.n[e] + (self.order[e][name] + 2))

    def did(self, instruction, e, name):
        assert self.order[e][name] == self.next[e] % self.n[e], (e, name, self.next[e] % self.n[e])
        self.next[e] += 1
        instruction.then_inc(self.sem[e], 1)


def rwkv(k):
    nc, d = k.nc, k.d
    o = [0, 0]

    def take(n, w=0):
        o[w] += n
        assert o[w] <= (ARENA, ARENA2)[w], o
        return (k.AR, k.AR2)[w][:, o[w] - n:o[w]]

    def take4(w=0):
        return take(T, w).rearrange("p (b n) -> p b n", n=P)

    AR = take(2 * T).rearrange("p (j t) -> p j t", t=T)
    BZ = take(2 * T).rearrange("p (e t) -> p e t", t=T)
    KZ = take(2 * T).rearrange("p (e t) -> p e t", t=T)
    TOK = take(4 * T).rearrange("p (n b f) -> p n b f", n=4, f=P)
    BON2 = [take(T) for _ in range(2)]
    WC2 = [take(NCH) for _ in range(2)]
    TW = take(T)
    W2 = take(P)
    GTI = take(NCH * P).rearrange("p (c f) -> p c f", f=P)
    HB = take(NCH * P).rearrange("p (c f) -> p c f", f=P)
    ST = take(NCH * P).rearrange("p (c f) -> p c f", f=P)
    flat = take(3 * (T + 1))
    IN = flat.rearrange("p (n t) -> p n t", t=T + 1)
    M = take(3 * T).rearrange("p (n t) -> p n t", t=T)
    LW, AS, KK, SQN = (take(T) for _ in range(4))
    L = take(T, 1)
    DT = SQN
    EW, EWI, EWP = (flat[:, n * T:(n + 1) * T] for n in range(3))
    gb = [take(TB * T, 1) for _ in range(2)]
    GB = [x.rearrange("p (b n) -> p b n", n=T) for x in gb]
    T_, TT, X = ([take4(1), take4(1)] for _ in range(3))
    LOT = [take4(0), take4(0)]
    BTZ = take4(1)
    UVA, P1TA, P1Z, VZ = X, T_, LOT, X
    SQ, VE, Z = (gb[0][:, n * T:(n + 1) * T] for n in range(3))
    QT, Y = k.STG[:, 0, :], k.STG[:, 1, :]
    NL = len(LEVELS)
    C = k.c
    B = k.PSB
    XB, TXB, XTB = (3, 0), (4, 1), (5, 2)

    heads = range(2)
    levels = range(1, NL)
    N = Steps(k, "rwkvp",
              pe=["zw", "za", "ss", "tA", "tB", "tK", "tV", "bs"],
              act=["sgw", "sga", "sqk", "ew", "ewi", "ewp", "sqrt", "tokK", "tokV"],
              dve=["z0", "dr", "mr", "dk", "mk", "kk", "dv", "mv", "lw", "scan", "lp", "am", "kp", "kt", "nmax", "nrec", "kn",
                   "ba", "bt", "at", "rt", "bz0", "bz1", "kz0", "kz1", "bo", "wc", "tokA", "tokB", "bon"])
    dve = []
    for e in heads:
        dve += [f"gb{e}{b}" for b in range(TB)] + [f"t0a{e}", f"t0b{e}", f"tt0a{e}", f"tt0b{e}"]
    for l in levels:
        for e in heads:
            dve += ([f"ta{e}{l}"] if l < NL - 1 else []) + [f"tta{e}{l}"]
    dve += ["gti0", "hb0", "gti1", "hb1", "st1", "qt", "yv"] + [f"su{c}" for c in range(1, NCH - 1)]
    dve += ["yy", "yc", "ve", "vrec", "yn", "yb", "yz", "xl"]
    act = [f"xc{e}{l}" for l in levels for e in heads] + ["uvc0", "uvc1", "ptc0", "ptc1", "sqy", "vsqrt", "xh"]
    pe_ = [f"{x}{e}{b}" for e in heads for x, b in [("g", b) for b in range(TB)] + [("lm", "")]]
    for l in levels:
        pe_ += [f"x{e}{l}" for e in heads]
        for e in heads:
            pe_ += ([f"tx{e}{l}"] if l < NL - 1 else []) + [f"xt{e}{l}"]
    pe_ += ["uv0", "uv1", "pt0", "pt1", "q0", "y0", "q1", "y1", "gt0", "gt1", "h0", "h1"]
    pe_ += [f"s{c}" for c in range(1, NCH - 1)] + ["yf", "mean", "var"]
    pool_ = [f"lot{e}{l}" for l in levels for e in heads] + ["btz0", "uva0", "uva1", "btz1", "p1z0", "p1z1", "vz0", "vz1"]
    S = Steps(k, "rwkv", dve=dve, act=act, pe=pe_, pool=pool_)
    w_in, w_m, w_t, zeroed = k.sem("rwkv_lora_in"), k.sem("rwkv_lora_mixed"), k.sem("rwkv_lora_tanh"), k.sem("rwkv_zeroed")
    ld, z_in, col_zero = k.sem("rwkv_in"), k.sem("rwkv_z_in"), k.sem("rwkv_col_zero")

    def blk(b):
        return slice(b * P, (b + 1) * P)

    def rows(e):
        return slice(64 * e, 64 * e + 64)

    def lev(n):
        return C("lev", n * P, (n + 1) * P).unsqueeze(1).broadcast_to([P, TB, P])

    def ident4():
        return C("ident").unsqueeze(1).broadcast_to([P, TB, P])

    def four(ap):
        return ap.rearrange("p (b f) -> p b f", f=P)

    def pairs(eng, turn):
        loop(eng, NPAIR - 1, lambda i, par: turn(i, par, True))
        turn(NPAIR - 1, (NPAIR - 1) % 2, False)

    with nc.Block() as block:
        @block.sync
        def _(sp):
            sp.dma_start(IN[:, 0, 1:T + 1], k.PROJ[WA0, :, :]).then_inc(w_in, 16)
            sp.wait_ge(w_m, 2)

            def load(i):
                for n, c0 in enumerate((R0, K0, V0)):
                    sp.dma_start(IN[:, n, 1:T + 1], k.PROJ[c0 + i, :, :]).then_inc(ld, 16)
                for e, w in ((0, "rwkv_w2"), (1, "rwkv_a2")):
                    sp.dma_start(W2[rows(e), :], d[w][0, :, bass.ds(i * P, P)]).then_inc(ld, 16)

            def turn(i, par, more):
                if more:
                    N.wait(sp, i, "pe.bs", "dve.wc")
                    load(i + 1)
                S.wait(sp, i, "pe.y1")
                sp.dma_start(Z, k.PROJ[ZB0 + i, :, :]).then_inc(z_in, 16)
            load(0)
            pairs(sp, turn)

        @block.gpsimd
        def _(pool):
            for buf in (BZ, KZ, GTI, HB, ST):
                nc.gpsimd.memset(buf, 0.0).then_inc(zeroed, 1)
            S.begin(pool, "pool")

            def mask(out, in_, name):
                src = in_.unsqueeze(2).broadcast_to([P, TB, 2, 64])
                m = C("cmask").unsqueeze(1).unsqueeze(3).broadcast_to([P, TB, 2, 64])
                S.did(nc.gpsimd.tensor_tensor(out.rearrange("p b (c f) -> p b c f", c=2), src, m, ALU.mult), "pool", name)

            def turn(i, par, more):
                for l in levels:
                    for e in heads:
                        if l == 1:
                            S.wait(pool, i, f"dve.gb{e}{TB - 1}")
                        else:
                            S.wait(pool, i, f"pe.x{e}{l - 1}")
                        S.did(nc.gpsimd.tensor_tensor(LOT[e], GB[e][:, :, 0:P], lev(l + 1), ALU.mult), "pool", f"lot{e}{l}")
                S.wait(pool, i, f"pe.xt1{NL - 1}")
                mask(BTZ, TOK[:, 1, :, rows(0)], "btz0")
                for e in heads:
                    S.did(nc.gpsimd.tensor_copy(UVA[e][:, :, 64:P], TOK[:, 0, :, rows(e)]), "pool", f"uva{e}")
                S.wait(pool, i, "pe.gt0")
                mask(BTZ, TOK[:, 1, :, rows(1)], "btz1")
                for e in heads:
                    S.wait(pool, i, f"act.ptc{e}")
                    mask(P1Z[e], P1TA[e][:, :, 0:64], f"p1z{e}")
                for e in heads:
                    mask(VZ[e], TOK[:, 3, :, rows(e)], f"vz{e}")
            pairs(pool, turn)

        @block.tensor
        def _(pe):
            mm = nc.tensor.matmul
            S.begin(pe, "pe")
            N.begin(pe, "pe")
            pe.wait_ge(w_t, 1)
            pe.wait_ge(zeroed, 5)

            def decays(i):
                pe.wait_ge(ld, i * 80 + 80)
                N.did(mm(B[6][:, :], W2[rows(0), :], TW[rows(0), :], start=True, stop=True), "pe", "zw")
                N.did(mm(B[7][:, :], W2[rows(1), :], TW[rows(1), :], start=True, stop=True), "pe", "za")

            def key_sums(i):
                N.wait(pe, i, "act.sqk", "act.sgw")
                N.did(mm(B[6][:, :], C("bones"), SQN, start=True, stop=True), "pe", "ss")

            def transposed(i, n, x, src, ready):
                N.wait(pe, i, ready)
                for b in range(TB):
                    last = nc.tensor.transpose(B[4 + n][:, blk(b)], src[:, blk(b)], C("ident"))
                N.did(last, "pe", "t" + x)

            def bonus_sums(i):
                N.wait(pe, i, "dve.bo")
                N.did(mm(B[3][:, :], C("bones"), EWP, start=True, stop=True), "pe", "bs")

            def levels_of(i, l):
                for e in heads:
                    S.wait(pe, i, f"pool.lot{e}{l}")
                    S.wait(pe, i, f"dve.tta{e}{l - 1}" if l > 1 else f"dve.tt0b{e}")
                    for b in range(TB):
                        last = mm(B[XB[e]][:, blk(b)], LOT[e][:, b, :], T_[e][:, b, :], start=True, stop=True)
                    S.did(last, "pe", f"x{e}{l}")
                for e in heads:
                    S.wait(pe, i, f"act.xc{e}{l}")
                    if l < NL - 1:
                        for b in range(TB):
                            last = mm(B[TXB[e]][:, blk(b)], TT[e][:, b, :], X[e][:, b, :], start=True, stop=True)
                        S.did(last, "pe", f"tx{e}{l}")
                    for b in range(TB):
                        last = mm(B[XTB[e]][:, blk(b)], X[e][:, b, :], TT[e][:, b, :], start=True, stop=True)
                    S.did(last, "pe", f"xt{e}{l}")

            def turn(i, par, more):
                N.wait(pe, i, "dve.bon", "act.tokV")
                if more:
                    decays(i + 1)
                S.before(pe, i, "dve.ve")
                for e in heads:
                    for b in range(TB):
                        if b >= 2:
                            S.wait(pe, i, f"dve.gb{e}{b - 2}")
                        elif e:
                            S.wait(pe, i, f"dve.gb0{b + 2}")
                        mm(B[b % 2][:, 0:2 * P], BZ[:, e, blk(b)], AR[:, :, blk(b)], start=True, stop=True)
                        S.did(mm(B[b % 2][:, 2 * P:T], KZ[:, e, blk(b)], AR[:, :, blk(b)], start=True, stop=True), "pe", f"g{e}{b}")
                    if e:
                        S.wait(pe, i, "dve.t0a0")
                    for b in range(TB):
                        last = mm(B[2][:, blk(b)], AR[:, 0, blk(b)], BZ[:, e, blk(b)], start=True, stop=True)
                    S.did(last, "pe", f"lm{e}")
                for l in levels:
                    levels_of(i, l)
                    if l == 4 and more:
                        key_sums(i + 1)
                for e in heads:
                    for b in range(TB):
                        last = mm(B[XB[e]][:, b * 64:b * 64 + 64], GB[e][:, b, 2 * P:3 * P], TOK[:, 3, b, rows(e)], start=True, stop=True)
                    S.did(last, "pe", f"uv{e}")
                for e in heads:
                    S.wait(pe, i, f"act.uvc{e}", f"pool.uva{e}", f"dve.tta{e}{NL - 1}")
                    for b in range(TB):
                        last = mm(B[TXB[e]][:, blk(b)], TT[e][:, b, :], UVA[e][:, b, :], start=True, stop=True)
                    S.did(last, "pe", f"pt{e}")
                for e in heads:
                    S.wait(pe, i, f"act.ptc{e}")
                    for b in range(TB):
                        last = mm(B[6][rows(e), blk(b)], P1TA[e][:, b, 64:P], GB[e][:, b, P:2 * P], start=True, stop=True)
                    S.did(last, "pe", f"q{e}")
                    for b in range(TB):
                        mm(B[7][rows(e), blk(b)], P1TA[e][:, b, 0:64], GB[e][:, b, P:2 * P], start=True, stop=False)
                        last = mm(B[7][rows(e), blk(b)], TOK[:, 3, b, rows(e)], GB[e][:, b, 3 * P:T], start=False, stop=True)
                    S.did(last, "pe", f"y{e}")
                for e in heads:
                    S.wait(pe, i, f"pool.btz{e}")
                    for b in range(TB):
                        last = mm(B[3][rows(e), blk(b)], P1TA[e][:, b, 64:P], BTZ[:, b, :], start=True, stop=True)
                    S.did(last, "pe", f"gt{e}")
                for e in heads:
                    S.wait(pe, i, f"pool.vz{e}")
                    for b in range(TB):
                        mm(B[5][rows(e), blk(b)], TOK[:, 1, b, rows(e)], P1Z[e][:, b, :], start=True, stop=False)
                        last = mm(B[5][rows(e), blk(b)], TOK[:, 2, b, rows(e)], VZ[e][:, b, :], start=False, stop=True)
                    S.did(last, "pe", f"h{e}")
                for c in range(1, NCH - 1):
                    S.wait(pe, i, "dve.st1" if c == 1 else f"dve.su{c - 1}")
                    S.did(mm(B[c % 2][:, 0:P], GTI[:, c, :], ST[:, c, :], start=True, stop=True), "pe", f"s{c}")
                    if more:
                        if c == 2:
                            transposed(i + 1, 0, "A", AR[:, 0, :], "dve.at")
                        if c == 3:
                            transposed(i + 1, 1, "B", SQN, "dve.bt")
                            S.wait(pe, i, "dve.yv")
                        if c == 4:
                            transposed(i + 1, 2, "K", LW, "dve.kt")
                        if c == 5:
                            transposed(i + 1, 3, "V", M[:, 2, :], "dve.mv")
                S.wait(pe, i, "dve.qt", f"dve.su{NCH - 2}")
                for c in range(NCH):
                    last = mm(B[2][:, c * CH:(c + 1) * CH], ST[:, c, :], QT[:, c * CH:(c + 1) * CH], start=True, stop=True)
                S.did(last, "pe", "yf")
                if more:
                    bonus_sums(i + 1)
                S.wait(pe, i, "dve.yy")
                S.did(mm(B[0][:, :], C("bones"), Y, start=True, stop=True), "pe", "mean")
                S.wait(pe, i, "act.sqy")
                S.did(mm(B[1][:, :], C("bones"), SQ, start=True, stop=True), "pe", "var")

            decays(0)
            key_sums(0)
            transposed(0, 0, "A", AR[:, 0, :], "dve.at")
            transposed(0, 1, "B", SQN, "dve.bt")
            transposed(0, 2, "K", LW, "dve.kt")
            transposed(0, 3, "V", M[:, 2, :], "dve.mv")
            bonus_sums(0)
            pairs(pe, turn)

        @block.scalar
        def _(act):
            A = nc.scalar.activation
            S.begin(act, "act")
            N.begin(act, "act")
            act.wait_ge(w_m, 2)
            A(TW[0:64, :], TW[0:64, :], ACT.Tanh).then_inc(w_t, 1)

            def did(name, ins):
                S.did(ins, "act", name)

            def gates(i):
                N.before(act, i, "dve.kz1")
                N.wait(act, i, "pe.zw")
                N.did(A(LW, B[6][:, :], ACT.Sigmoid, bias=k.prm("w0", i)), "act", "sgw")
                N.wait(act, i, "pe.za")
                N.did(A(AS, B[7][:, :], ACT.Sigmoid, bias=k.prm("a0", i)), "act", "sga")

            def squares(i):
                N.wait(act, i, "dve.kk", "dve.mv")
                N.did(A(SQN, KK, ACT.Square), "act", "sqk")

            def exps(i):
                N.wait(act, i, "dve.lp")
                N.did(A(EW, L, ACT.Exp), "act", "ew")
                N.did(A(EWI, L, ACT.Exp, scale=-1.0), "act", "ewi")
                N.did(A(EWP, EWP, ACT.Exp), "act", "ewp")

            def root(i):
                N.wait(act, i, "pe.ss")
                N.did(A(SQN, B[6][:, :], ACT.Sqrt), "act", "sqrt")

            def token_major(i):
                for n, x in ((2, "K"), (3, "V")):
                    N.wait(act, i, "pe.t" + x)
                    N.did(A(TOK[:, n, :, :], four(B[4 + n][:, :]), ACT.Copy), "act", "tok" + x)

            def turn(i, par, more):
                for l in levels:
                    for e in heads:
                        S.wait(act, i, f"pe.x{e}{l}")
                        did(f"xc{e}{l}", A(X[e], four(B[XB[e]][:, :]), ACT.Copy))
                    if more:
                        if l == 1:
                            gates(i + 1)
                        if l == 3:
                            squares(i + 1)
                        if l == 4:
                            exps(i + 1)
                for e in heads:
                    S.wait(act, i, f"pe.uv{e}")
                    S.wait(act, i, f"pe.xt{e}{NL - 1}")
                    did(f"uvc{e}", A(UVA[e][:, :, 0:64], B[XB[e]][:, 0:2 * P].rearrange("p (b f) -> p b f", f=64), ACT.Copy))
                if more:
                    root(i + 1)
                for e in heads:
                    S.wait(act, i, f"pe.pt{e}")
                    did(f"ptc{e}", A(P1TA[e], four(B[TXB[e]][:, :]), ACT.Copy))
                if more:
                    token_major(i + 1)
                S.wait(act, i, "dve.yc")
                did("sqy", A(SQ, Y, ACT.Square))
                S.wait(act, i, "dve.ve")
                did("vsqrt", A(VE, VE, ACT.Sqrt))
                S.wait(act, i, "dve.yz")
                did("xh", A(k.XH[:, i + NPAIR, :], Y, ACT.Copy))
            gates(0)
            squares(0)
            exps(0)
            root(0)
            token_major(0)
            pairs(act, turn)

        @block.vector
        def _(dve):
            V = nc.vector
            S.begin(dve, "dve")
            N.begin(dve, "dve")
            TTn, STT, TS = V.tensor_tensor, V.scalar_tensor_tensor, V.tensor_scalar
            V.memset(IN[:, 0, 0:1], 0.0).then_inc(col_zero, 1)
            dve.wait_ge(w_in, 16)
            dve.wait_ge(zeroed, 5)
            dve.wait_ge(col_zero, 1)
            TTn(M[:, 0, :], IN[:, 0, 0:T], IN[:, 0, 1:T + 1], ALU.subtract).then_inc(w_m, 1)
            dve.wait_ge(w_m, 1)
            STT(out=TW, in0=M[:, 0, :], scalar=k.prm("mu", 24), in1=IN[:, 0, 1:T + 1], op0=ALU.mult, op1=ALU.add).then_inc(w_m, 1)

            def prep(name, ins):
                N.did(ins, "dve", name)

            def mixed(i, n):
                x, mu = (("r", 0), ("k", 8), ("v", 16))[n]
                if n:
                    N.wait(dve, i, ("dve.mr", "dve.kk")[n - 1])
                prep("d" + x, TTn(DT, IN[:, n, 0:T], IN[:, n, 1:T + 1], ALU.subtract))
                N.wait(dve, i, "dve.d" + x)
                prep("m" + x, STT(out=M[:, n, :], in0=DT, scalar=k.prm("mu", i + mu), in1=IN[:, n, 1:T + 1], op0=ALU.mult, op1=ALU.add))

            def mix_rk(i):
                N.wait(dve, i, "pe.za")
                prep("z0", V.memset(IN[:, :, 0:1], 0.0))
                dve.wait_ge(ld, i * 80 + 80)
                N.wait(dve, i, "dve.z0")
                mixed(i, 0)
                mixed(i, 1)

            def mix_v(i):
                N.wait(dve, i, "dve.mk")
                prep("kk", TS(KK, M[:, 1, :], k.prm("k_k", i), None, ALU.mult))
                mixed(i, 2)

            def log_decay(i):
                N.wait(dve, i, "act.sgw")
                prep("lw", TS(LW, LW, -float(np.exp(-0.5)), None, ALU.mult))
                N.wait(dve, i, "dve.lw", "dve.mv")
                prep("scan", V.tensor_tensor_scan(L, C("rst"), LW, 0.0, ALU.mult, ALU.add))
                N.wait(dve, i, "dve.scan")
                prep("lp", TTn(EWP, L, LW, ALU.subtract))

            def keys(i):
                N.wait(dve, i, "act.ewp")
                prep("am", TS(L, AS, -1.0, k.prm("k_a", i), ALU.add, ALU.mult))
                N.wait(dve, i, "dve.am")
                prep("kp", STT(out=M[:, 1, :], in0=L, scalar=1.0, in1=M[:, 1, :], op0=ALU.add, op1=ALU.mult))
                N.wait(dve, i, "dve.kp")
                prep("kt", TTn(LW, M[:, 1, :], EWI, ALU.mult))

            def unit_keys(i):
                N.wait(dve, i, "act.sqrt")
                prep("nmax", TS(SQN, SQN, 1e-12, None, ALU.max))
                N.wait(dve, i, "dve.nmax")
                prep("nrec", V.reciprocal(SQN, SQN))
                N.wait(dve, i, "dve.nrec")
                prep("kn", TTn(KK, KK, SQN, ALU.mult))
                N.wait(dve, i, "dve.kn")
                prep("ba", TTn(SQN, KK, AS, ALU.mult))
                N.wait(dve, i, "dve.ba")
                prep("bt", TTn(SQN, SQN, EWI, ALU.mult))

            def put_a(i, par):
                prep("at", STT(out=AR[:, 0, :], in0=KK, scalar=-1.0, in1=EWP, op0=ALU.mult, op1=ALU.mult))

            def put_r(i, par):
                prep("rt", TTn(AR[:, 1, :], M[:, 0, :], EW, ALU.mult))

            def put_b(i, par):
                N.wait(dve, i, "dve.bt")
                for e in heads:
                    prep(f"bz{e}", V.tensor_copy(BZ[rows(e), e, :], SQN[rows(e), :]))

            def put_k(i, par):
                for e in heads:
                    prep(f"kz{e}", V.tensor_copy(KZ[rows(e), e, :], LW[rows(e), :]))

            def bonus(i, par):
                N.wait(dve, i, "dve.at")
                prep("bo", STT(out=EWP, in0=M[:, 0, :], scalar=k.prm("r_k", i), in1=M[:, 1, :], op0=ALU.mult, op1=ALU.mult))
                prep("wc", V.tensor_copy(WC2[par], EW[:, CH - 1::CH]))

            def token_major(i):
                for n, x in ((0, "A"), (1, "B")):
                    N.wait(dve, i, "pe.t" + x)
                    prep("tok" + x, V.tensor_copy(TOK[:, n, :, :], four(B[4 + n][:, :])))

            def put_bonus(i, par):
                N.wait(dve, i, "pe.bs")
                prep("bon", TTn(BON2[par], B[3][:, :], M[:, 2, :], ALU.mult))

            puts = (put_a, put_r, put_b, put_k, bonus)

            def turn(i, par, more):
                WC, BON = WC2[par], BON2[par]

                def do(name, ins):
                    S.did(ins, "dve", name)

                def after(*names):
                    S.wait(dve, i, *names)
                for e in heads:
                    for b in range(TB):
                        after(f"pe.g{e}{b}")
                        do(f"gb{e}{b}", TTn(GB[e][:, b, :], B[b % 2][:, :], C("mt"), ALU.mult))
                    after(f"pe.lm{e}")
                    do(f"t0a{e}", TTn(T_[e], four(B[2][:, :]), lev(0), ALU.mult))
                    after(f"dve.t0a{e}")
                    do(f"t0b{e}", TTn(T_[e], T_[e], ident4(), ALU.add))
                    do(f"tt0a{e}", TTn(TT[e], GB[e][:, :, 0:P], lev(1), ALU.mult))
                    after(f"dve.tt0a{e}")
                    do(f"tt0b{e}", TTn(TT[e], TT[e], ident4(), ALU.add))
                for l in levels:
                    for e in heads:
                        if l < NL - 1:
                            after(f"pe.tx{e}{l}")
                            do(f"ta{e}{l}", TTn(T_[e], T_[e], four(B[TXB[e]][:, :]), ALU.add))
                        after(f"pe.xt{e}{l}")
                        do(f"tta{e}{l}", TTn(TT[e], TT[e], four(B[XTB[e]][:, :]), ALU.add))
                    if more:
                        if l == 1:
                            mix_rk(i + 1)
                        if l == 2:
                            mix_v(i + 1)
                        if l == 3:
                            log_decay(i + 1)
                        if l == 5:
                            keys(i + 1)
                if more:
                    unit_keys(i + 1)
                after("pe.h1")
                for e in heads:
                    do(f"gti{e}", TTn(GTI[rows(e), :, rows(e)], B[3][rows(e), :].rearrange("p (c f) -> p c f", f=64),
                                      C("ident")[rows(e), rows(e)].unsqueeze(1).broadcast_to([64, NCH, 64]), ALU.add))
                    do(f"hb{e}", TTn(HB[rows(e), :, rows(e)], B[5][rows(e), :].rearrange("p (c f) -> p c f", f=64),
                                     WC[rows(e), :].unsqueeze(2).broadcast_to([64, NCH, 64]), ALU.mult))
                after("dve.hb1")
                do("st1", V.tensor_copy(ST[:, 1, :], HB[:, 0, :]))
                do("qt", TTn(QT, B[6][:, :], AR[:, 1, :], ALU.add))
                do("yv", V.tensor_copy(Y, B[7][:, :]))
                for c in range(1, NCH - 1):
                    after(f"pe.s{c}")
                    do(f"su{c}", STT(out=ST[:, c + 1, :], in0=B[c % 2][:, 0:P], scalar=WC[:, c:c + 1], in1=HB[:, c, :], op0=ALU.mult, op1=ALU.add))
                    if more and c <= len(puts):
                        puts[c - 1](i + 1, 1 - par)
                if more:
                    token_major(i + 1)
                after("pe.yf", "dve.yv")
                do("yy", TTn(Y, B[2][:, :], Y, ALU.add))
                if more:
                    put_bonus(i + 1, 1 - par)
                after("pe.mean")
                do("yc", STT(out=Y, in0=B[0][:, :], scalar=-1.0 / 64, in1=Y, op0=ALU.mult, op1=ALU.add))
                after("pe.var")
                do("ve", TS(VE, B[1][:, :], 1.0 / 64, GN_EPS, ALU.mult, ALU.add))
                after("act.vsqrt")
                do("vrec", V.reciprocal(VE, VE))
                after("dve.vrec")
                do("yn", STT(out=Y, in0=Y, scalar=k.prm("ln_w", i), in1=VE, op0=ALU.mult, op1=ALU.mult))
                after("dve.yn")
                do("yb", STT(out=Y, in0=Y, scalar=k.prm("ln_b", i), in1=BON, op0=ALU.add, op1=ALU.add))
                after("dve.yb")
                dve.wait_ge(z_in, i * 16 + 16)
                do("yz", TTn(Y, Y, Z, ALU.mult))
                after("act.xh")
                do("xl", TTn(k.XL[:, i + NPAIR, :], Y, f32(k.XH[:, i + NPAIR, :]), ALU.subtract))

            mix_rk(0)
            mix_v(0)
            log_decay(0)
            keys(0)
            unit_keys(0)
            for put in puts:
                put(0, 0)
            token_major(0)
            put_bonus(0, 0)
            pairs(dve, turn)


def positions(k, tag, rope):
    nc, d = k.nc, k.d
    A = mla_arena(k)
    PI, CI, PF, CF, ANG, KI, KF = (A[x] for x in ("PI", "CI", "PF", "CF", "ANG", "KI", "KF"))
    DM, COS, SIN = A["DM"], A["COS"], A["SIN"]
    PQI, PQF, CQI, CQF = A["PQI"], A["PQF"], A["CQI"], A["CQF"]
    pi, st, si = k.sem(tag + "pos_in"), k.sem(tag + "pos_step"), k.sem(tag + "pos_trig")
    n = [0]
    TWO_PI = float(2 * np.pi)
    c1 = 6.28125
    c2 = float(np.float32(np.floor((TWO_PI - c1) * 2 ** 21) / 2 ** 21))
    c3 = float(TWO_PI - c1 - c2)
    with nc.Block() as block:
        @block.sync
        def _(sp):
            p = d["positions_2"]
            sp.dma_start(PI, p[0:1, :].broadcast_to([P, T])).then_inc(pi, 16)
            with nc.allow_non_contiguous_dma(reason="512 positions, one a partition"):
                sp.dma_start(PQI, p[0, :].rearrange("(b p) -> p b", p=P)).then_inc(pi, 16)

        @block.vector
        def _(dve):
            V = nc.vector

            def do(ins):
                n[0] += 1
                ins.then_inc(st, 1)
                dve.wait_ge(st, n[0])
            dve.wait_ge(pi, 32)
            do(V.tensor_copy(PF, PI))
            do(V.tensor_copy(PQF, PQI))
            do(V.tensor_scalar(CI, PI, 6, None, ALU.arith_shift_right))
            do(V.tensor_scalar(CQI, PQI, 6, None, ALU.arith_shift_right))
            do(V.tensor_copy(CF, CI))
            do(V.tensor_copy(CQF, CQI))
            for tb in range(TB):
                if rope:
                    do(V.tensor_scalar(DM[:, tb, :], CF, CQF[:, tb:tb + 1], -BIG, ALU.is_gt, ALU.mult))
                    continue
                do(V.tensor_scalar(DM[:, tb, :], PF, PQF[:, tb:tb + 1], None, ALU.subtract))
                do(V.tensor_scalar(ANG, DM[:, tb, :], -1.0, None, ALU.mult))
                do(V.tensor_tensor(DM[:, tb, :], DM[:, tb, :], ANG, ALU.max))
                do(V.tensor_scalar(ANG, CF, CQF[:, tb:tb + 1], BIG, ALU.is_gt, ALU.mult))
                do(V.tensor_tensor(DM[:, tb, :], DM[:, tb, :], ANG, ALU.add))
            for out, shift in ((SIN, 0.0), (COS, 0.25)) if rope else ():
                do(V.tensor_scalar(ANG, PF, k.c("freq"), None, ALU.mult))
                do(V.tensor_scalar(KF, ANG, 1.0 / TWO_PI, shift, ALU.mult, ALU.add))
                do(V.tensor_copy(KI, KF))
                do(V.tensor_copy(KF, KI))
                for c in (c1, c2, c3):
                    do(V.scalar_tensor_tensor(out=ANG, in0=KF, scalar=-c, in1=ANG, op0=ALU.mult, op1=ALU.add))
                if shift:
                    do(V.tensor_scalar(ANG, ANG, float(np.pi / 2), None, ALU.add))
                do(V.tensor_scalar(KF, ANG, float(np.pi), -TWO_PI, ALU.is_gt, ALU.mult))
                do(V.tensor_tensor(ANG, ANG, KF, ALU.add))
                do(V.tensor_scalar(KF, ANG, -float(np.pi), TWO_PI, ALU.is_lt, ALU.mult))
                do(V.tensor_tensor(ANG, ANG, KF, ALU.add))
                do(V.tensor_scalar(out, ANG, 3.1415925, -3.1415925, ALU.min, ALU.max))

        if not rope:
            return

        @block.scalar
        def _(act):
            act.wait_ge(st, n[0])
            nc.scalar.activation(SIN, SIN, ACT.Sin).then_inc(si, 1)
            nc.scalar.activation(COS, COS, ACT.Sin).then_inc(si, 1)


def mla_arena(k, more=False):
    o = [0]

    def take(n):
        o[0] += n
        assert o[0] <= ARENA, o[0]
        return k.AR[:, o[0] - n:o[0]]
    o[0] = ARENA - TB * T
    DM = take(TB * T)
    o[0] = 0
    A = dict(COS=take(T), SIN=take(T), KPR=take(T), KPS=take(T))
    A["DM"] = DM.rearrange("p (b t) -> p b t", t=T)
    b = o[0]
    for x in ("PF", "CF", "ANG", "KF"):
        A[x] = take(T)
    for x in ("PI", "CI", "KI"):
        A[x] = take(T).bitcast(I32)
    A["PQF"], A["CQF"] = take(TB), take(TB)
    A["PQI"], A["CQI"] = take(TB).bitcast(I32), take(TB).bitcast(I32)
    o[0] = b
    A["QN"], A["KN"] = ([[take(T) for _ in range(2)] for _ in range(2)] for _ in range(2))
    A["QRG"] = [take(T) for _ in range(2)]
    A["KRZ"] = [take(2 * T).rearrange("p (e t) -> p e t", t=T) for _ in range(2)]
    for x in ("QR", "QRS", "QNS", "KNS"):
        A[x] = take(T)
    A["RQM"], A["RQ"], A["MX"], A["GK"] = take(8 * TB), [take(2 * TB), take(2 * TB)], take(16), take(1)
    if more:
        two = [k.AR2[:, n * T:(n + 1) * T] for n in range(ARENA2 // T)]
        A["VT"], A["Z"], A["VV"] = [two[0:2], two[2:4]], two[4:6], two[6]
        A["PT"] = [k.AR2[:, 8 * T:12 * T].rearrange("p (b t) -> p b t", t=T), k.AR2[:, 12 * T:16 * T].rearrange("p (b t) -> p b t", t=T)]
        A["RK"] = [two[7], take(T)]
        A["S"] = take(4 * T).rearrange("p (j t) -> p j t", t=T)
    assert o[0] <= ARENA - TB * T, o[0]
    return A


def mla(k):
    nc, d = k.nc, k.d
    A = mla_arena(k, more=True)
    DM, COS, SIN, KPR, KPS, KRZ = (A[x] for x in ("DM", "COS", "SIN", "KPR", "KPS", "KRZ"))
    QR, QRS, QRG, QN, QNS, KN, KNS, VV, VT, RK = (A[x] for x in ("QR", "QRS", "QRG", "QN", "QNS", "KN", "KNS", "VV", "VT", "RK"))
    S_, PT, Z, RQM, RQ, MX, GK = (A[x] for x in ("S", "PT", "Z", "RQM", "RQ", "MX", "GK"))
    SWS = RK[1]
    B, C = k.PSB, k.c
    QK = 192
    NP = AH // 2
    heads = range(2)
    NI = 2 * TB
    N = Steps(k, "mlap",
              pe=["qswap", "sq0", "sq1", "v0", "rk0", "rk1", "v1"],
              act=["qrs", "qns0", "kns0", "qns1", "kns1", "rqs", "vt0", "vt1"],
              dve=["qrg", "qrc", "qrsn", "qrr", "rqm", "rqr", "rqx", "dg0", "dg1", "kg0", "krz0", "kg1", "krz1"])
    s_mm, s_b, s_max, s_exp, s_rec, s_p, s_tr, s_pt, s_pv, s_out, s_xh, s_xl = (k.sem("mla_" + x) for x in (
        "scores", "biased", "max", "exps", "recip", "probs", "turned", "pt", "pv", "out", "hi", "lo"))
    kp_in, kp_s, kp_m = k.sem("kpe_in"), k.sem("kpe_step"), k.sem("kpe_swap")
    kp_q, gk = k.sem("kpe_square"), k.sem("gains_multiplied")
    q_in, h_in, v_in = k.sem("mla_pair_in"), k.sem("mla_head_in"), k.sem("mla_second_value_in")
    z_in = [k.sem(f"mla_z_in{e}") for e in heads]
    z0 = k.sem("krz_zeroed")

    def rows(e):
        return slice(64 * e, 64 * e + 64)

    def blk(b):
        return slice(b * P, (b + 1) * P)

    def pairs(eng, turn):
        turn(0, 0, True, False)
        with eng.Fori(0, NP // 2 - 1) as it:
            turn(it * 2 + 1, 1, False, False)
            turn(it * 2 + 2, 0, False, False)
        turn(NP - 1, 1, False, True)

    def at(i, par, n):
        return (i + n // NI, (par + n // NI) % 2, n % NI // TB, n % TB)

    with nc.Block() as block:
        @block.gpsimd
        def _(pool):
            for x in KRZ:
                nc.gpsimd.memset(x, 0.0).then_inc(z0, 1)

        @block.sync
        def _(sp):
            for e in heads:
                sp.dma_start(KPR[rows(e), :], k.PROJ[KPE0, 0:64, :]).then_inc(kp_in, 16)

            def load(i, par):
                sp.dma_start(QR, k.PROJ[QR0 + i, :, :]).then_inc(q_in, 16)
                for e in heads:
                    sp.dma_start(QN[par][e], k.PROJ[i * 2 + (QN0 + e), :, :]).then_inc(h_in, 16)
                    sp.dma_start(KN[par][e], k.PROJ[i * 4 + (KV0 + 2 * e), :, :]).then_inc(h_in, 16)
                sp.dma_start(VV, k.PROJ[i * 4 + (KV0 + 1), :, :]).then_inc(h_in, 16)

            def second_value(i):
                N.wait(sp, i, "pe.v0")
                sp.dma_start(VV, k.PROJ[i * 4 + (KV0 + 3), :, :]).then_inc(v_in, 16)

            def turn(i, par, first, last):
                if not last:
                    N.wait(sp, i, "pe.v1")
                    sp.wait_ge(s_mm, i * NI + 1)
                    load(i + 1, 1 - par)
                for e in heads:
                    sp.wait_ge(s_xl, i * 2 + (e + 1))
                    sp.dma_start(Z[e], k.PROJ[i * 2 + (AG0 + e), :, :]).then_inc(z_in[e], 16)
                if not last:
                    second_value(i + 1)
            load(0, 0)
            second_value(0)
            pairs(sp, turn)

        @block.tensor
        def _(pe):
            mm = nc.tensor.matmul
            N.begin(pe, "pe")
            pe.sem_inc(s_mm, 1)
            pe.sem_inc(s_tr, 4)
            pe.sem_inc(s_pv, 2)
            pe.wait_ge(kp_s, 1)
            mm(B[0][:, :], C("swap"), KPR, start=True, stop=True).then_inc(kp_m, 1)
            pe.wait_ge(kp_s, 4)
            pe.wait_ge(z0, 2)

            def swap(i, par):
                N.wait(pe, i, "dve.qrg")
                N.before(pe, i, "act.vt1")
                N.did(mm(B[6][:, :], C("swap"), QRG[par], start=True, stop=True), "pe", "qswap")

            def squares(i, par, e):
                N.wait(pe, i, f"act.kns{e}", "dve.qrc")
                for tb in range(TB):
                    c = e * TB + tb
                    mm(B[7][:, c:c + 1], QNS[:, blk(tb)], C("ones", 0, 1), start=True, stop=False)
                    mm(B[7][:, c:c + 1], QRS[:, blk(tb)], C(f"hone{e}", 0, 1), start=False, stop=True)
                    mm(B[7][:, NI + c:NI + c + 1], KNS[:, blk(tb)], C("ones", 0, 1), start=True, stop=False)
                    last = mm(B[7][:, NI + c:NI + c + 1], KPS[:, blk(tb)], C("hone0", 0, 1), start=False, stop=True)
                N.did(last, "pe", f"sq{e}")

            def key_factors(i, e):
                N.wait(pe, i, f"dve.dg{e}")
                N.did(mm(B[5 + e][:, :], C("ones"), RK[e], start=True, stop=True), "pe", f"rk{e}")

            def value(i, par, e):
                bank = (7, 5)[e]
                if e:
                    pe.wait_ge(v_in, i * 16 + 16)
                else:
                    pe.wait_ge(h_in, i * 80 + 80)
                N.wait(pe, i, ("dve.rqm", "dve.krz0")[e])
                for b in range(TB):
                    last = nc.tensor.transpose(B[bank][:, blk(b)], VV[:, blk(b)], C("ident"))
                N.did(last, "pe", f"v{e}")

            def scores(i, par, n):
                ii, pp, e, tb = at(i, par, n)
                pe.wait_ge(s_b, i * NI + (n + 1))
                if tb == 0:
                    N.wait(pe, ii, f"dve.krz{e}")
                mm(B[n % 2][:, :], QN[pp][e][:, blk(tb)], KN[pp][e], start=True, stop=False)
                mm(B[n % 2][:, :], QRG[pp][:, blk(tb)], KRZ[pp][:, e, :], start=False, stop=True).then_inc(s_mm, 1)

            def turned(i, n):
                pe.wait_ge(s_p, i * NI + (n + 1))
                pe.wait_ge(s_pt, i * NI + (n + 1))
                for b in range(TB):
                    last = nc.tensor.transpose(B[2 + n % 2][:, blk(b)], S_[:, n % 4, blk(b)], C("ident"))
                last.then_inc(s_tr, 1)

            def values(i, par, e):
                pe.wait_ge(s_pt, i * NI + (TB * e + TB + 2))
                pe.wait_ge(s_out, i * 2 + (e + 1))
                N.wait(pe, i, f"act.vt{e}")
                for b in range(TB):
                    last = mm(B[4][:, :], VT[par][e][:, blk(b)], PT[e][:, b, :], start=(b == 0), stop=(b == TB - 1))
                last.then_inc(s_pv, 1)

            def turn(i, par, first, last):
                for n in range(NI):
                    if n + 3 < NI or not last:
                        scores(i, par, n + 3)
                    turned(i, n)
                    if n == 0 and not first:
                        values(i + (-1), 1 - par, 1)
                    if n == TB and not last:
                        for e in heads:
                            key_factors(i + 1, e)
                    if n == TB:
                        values(i, par, 0)
                    if not last:
                        if n == 0:
                            swap(i + 1, 1 - par)
                        if n in (1, 2):
                            squares(i + 1, 1 - par, n - 1)
                        if n in (3, 5):
                            value(i + 1, 1 - par, n // 5)
                if last:
                    values(i, par, 1)
            swap(0, 0)
            for e in heads:
                squares(0, 0, e)
            value(0, 0, 0)
            for e in heads:
                key_factors(0, e)
            value(0, 0, 1)
            for n in range(3):
                scores(0, 0, n)
            pairs(pe, turn)

        @block.scalar
        def _(act):
            Ac = nc.scalar.activation
            N.begin(act, "act")
            act.sem_inc(s_pt, 2)
            act.wait_ge(kp_in, 32)
            Ac(KPS, KPR, ACT.Square).then_inc(kp_q, 1)

            def squares(i, par, e):
                if e:
                    N.wait(act, i, "pe.sq0")
                else:
                    act.wait_ge(q_in, i * 16 + 16)
                    N.did(Ac(QRS, QR, ACT.Square), "act", "qrs")
                    act.wait_ge(h_in, i * 80 + 80)
                N.did(Ac(QNS, QN[par][e], ACT.Square), "act", f"qns{e}")
                N.did(Ac(KNS, KN[par][e], ACT.Square), "act", f"kns{e}")

            def roots(i):
                N.wait(act, i, "dve.rqm")
                N.did(Ac(RQM[:, 2 * NI:4 * NI], RQM[:, 0:2 * NI], ACT.Sqrt), "act", "rqs")

            def value(i, par, e):
                N.wait(act, i, f"pe.v{e}")
                N.did(Ac(VT[par][e], B[(7, 5)[e]][:, :], ACT.Copy), "act", f"vt{e}")

            def exps(i, n):
                j = n % 4
                act.wait_ge(s_max, i * NI + (n + 1))
                Ac(S_[:, j, :], S_[:, j, :], ACT.Exp, bias=MX[:, j:j + 1], accum_out=MX[:, 4 + j:5 + j]).then_inc(s_exp, 1)

            def copy(i, n):
                act.wait_ge(s_tr, i * NI + (n + 5))
                if n % TB == 0:
                    act.wait_ge(s_pv, i * 2 + (n // TB + 1))
                Ac(PT[n // TB][:, :, blk(n % TB)], B[2 + n % 2][:, :].rearrange("p (b t) -> p b t", t=P), ACT.Copy).then_inc(s_pt, 1)

            def high(i, e):
                act.wait_ge(s_out, i * 2 + (e + 2))
                Ac(k.XH[:, i * 2 + e, :], Z[e], ACT.Copy).then_inc(s_xh, 1)

            def turn(i, par, first, last):
                for n in range(NI):
                    if n + 2 < NI or not last:
                        exps(i, n + 2)
                    copy(i, n)
                    if n == 1 and not first:
                        high(i + (-1), 1)
                    if n == TB + 1:
                        high(i, 0)
                    if not last:
                        if n in (0, 1):
                            squares(i + 1, 1 - par, n)
                        if n == 3:
                            roots(i + 1)
                        if n in (4, 6):
                            value(i + 1, 1 - par, n // 6)
                if last:
                    high(i, 1)
            for e in heads:
                squares(0, 0, e)
            roots(0)
            for e in heads:
                value(0, 0, e)
            for n in range(2):
                exps(0, n)
            pairs(act, turn)

        @block.vector
        def _(dve):
            V = nc.vector
            TTn, STT, TS = V.tensor_tensor, V.scalar_tensor_tensor, V.tensor_scalar
            N.begin(dve, "dve")
            dve.sem_inc(s_b, 2)
            dve.sem_inc(s_out, 1)
            dve.sem_inc(s_xl, 2)
            TTn(GK, k.prm("k_gain", 0), k.prm("q_gain", 0), ALU.mult).then_inc(gk, 1)
            dve.wait_ge(kp_q, 1)
            TS(KPR, KPR, k.prm("k_gain", 1), None, ALU.mult).then_inc(kp_s, 1)
            dve.wait_ge(kp_m, 1)
            TTn(SWS, B[0][:, :], SIN, ALU.mult).then_inc(kp_s, 1)
            TTn(KPR, KPR, COS, ALU.mult).then_inc(kp_s, 1)
            dve.wait_ge(kp_s, 3)
            TTn(KPR, KPR, SWS, ALU.add).then_inc(kp_s, 1)
            dve.wait_ge(kp_s, 4)
            dve.wait_ge(z0, 2)
            dve.wait_ge(gk, 1)

            def do(name, ins):
                N.did(ins, "dve", name)

            def rope_q(i, par, part):
                q = QRG[par]
                if part == 0:
                    dve.wait_ge(q_in, i * 16 + 16)
                    do("qrg", TS(q, QR, k.prm("q_gain", 1), None, ALU.mult))
                if part == 1:
                    N.wait(dve, i, "pe.qswap")
                    do("qrc", TTn(SWS, B[6][:, :], SIN, ALU.mult))
                    do("qrsn", TTn(q, q, COS, ALU.mult))
                if part == 2:
                    N.wait(dve, i, "dve.qrsn")
                    do("qrr", TTn(q, q, SWS, ALU.add))

            def means(i):
                N.wait(dve, i, "pe.sq1", "dve.qrr")
                do("rqm", TS(RQM[:, 0:2 * NI], B[7][:, 0:2 * NI], 1.0 / QK, EPS, ALU.mult, ALU.add))

            def factors(i, par):
                N.wait(dve, i, "act.rqs")
                do("rqr", V.reciprocal(RQM[:, 0:2 * NI], RQM[:, 2 * NI:4 * NI]))
                N.wait(dve, i, "dve.rqr")
                do("rqx", TS(RQ[par], RQM[:, 0:NI], QK ** -0.5, None, ALU.mult))
                for e in heads:
                    r = RQM[:, NI + e * TB:NI + (e + 1) * TB].unsqueeze(2).broadcast_to([P, TB, P])
                    do(f"dg{e}", TTn(RK[e].rearrange("p (b t) -> p b t", t=P), C("ident").unsqueeze(1).broadcast_to([P, TB, P]), r, ALU.mult))

            def keys(i, par, e):
                N.wait(dve, i, f"pe.rk{e}")
                do(f"kg{e}", STT(out=KN[par][e], in0=KN[par][e], scalar=GK, in1=B[5 + e][:, :], op0=ALU.mult, op1=ALU.mult))
                do(f"krz{e}", TTn(KRZ[par][rows(e), e, :], KPR[rows(e), :], B[5 + e][rows(e), :], ALU.mult))

            def bias(i, par, n):
                ii, pp, e, tb = at(i, par, n)
                j, I = n % 4, i * NI + n
                dve.wait_ge(s_mm, i * NI + (n + 2))
                dve.wait_ge(s_tr, i * NI + (n + 1))
                if n % NI == 0:
                    N.wait(dve, ii, "dve.rqx")
                c = e * TB + tb
                STT(out=S_[:, j, :], in0=B[n % 2][:, :], scalar=RQ[pp][:, c:c + 1], in1=DM[:, tb, :], op0=ALU.mult, op1=ALU.add).then_inc(s_b, 1)
                dve.wait_ge(s_b, i * NI + (n + 3))
                V.tensor_reduce(MX[:, j:j + 1], S_[:, j, :], AX, ALU.max, negate=True).then_inc(s_max, 1)

            def scale(i, n):
                j = n % 4
                dve.wait_ge(s_exp, i * NI + (n + 1))
                V.reciprocal(MX[:, 8 + j:9 + j], MX[:, 4 + j:5 + j]).then_inc(s_rec, 1)
                dve.wait_ge(s_rec, i * NI + (n + 1))
                TS(S_[:, j, :], S_[:, j, :], MX[:, 8 + j:9 + j], None, ALU.mult).then_inc(s_p, 1)

            def output(i, e):
                dve.wait_ge(s_pv, i * 2 + (e + 3))
                dve.wait_ge(z_in[e], i * 16 + 16)
                TTn(Z[e], B[4][:, :], Z[e], ALU.mult).then_inc(s_out, 1)

            def low(i, e):
                dve.wait_ge(s_xh, i * 2 + (e + 1))
                TTn(k.XL[:, i * 2 + e, :], Z[e], f32(k.XH[:, i * 2 + e, :]), ALU.subtract).then_inc(s_xl, 1)

            def turn(i, par, first, last):
                for n in range(NI):
                    if n + 2 < NI or not last:
                        bias(i, par, n + 2)
                    scale(i, n)
                    if n == 1 and not first:
                        output(i + (-1), 1)
                    if n == 2 and not first:
                        low(i + (-1), 1)
                    if n == TB + 1:
                        output(i, 0)
                    if n == TB + 2:
                        low(i, 0)
                    if not last:
                        if n < 3:
                            rope_q(i + 1, 1 - par, n)
                        if n == 2:
                            means(i + 1)
                        if n == 3:
                            factors(i + 1, 1 - par)
                        if n == 4:
                            for e in heads:
                                keys(i + 1, 1 - par, e)
                if last:
                    output(i, 1)
                    low(i, 1)
            for part in range(3):
                rope_q(0, 0, part)
            means(0)
            factors(0, 0)
            for e in heads:
                keys(0, 0, e)
            for n in range(2):
                bias(0, 0, n)
            pairs(dve, turn)


def diff(k):
    nc, d = k.nc, k.d
    DM = mla_arena(k)["DM"]
    o = [0, 0]

    def take(n, w=0):
        o[w] += n
        assert o[w] <= (ARENA - TB * T, ARENA2)[w], o
        return (k.AR, k.AR2)[w][:, o[w] - n:o[w]]

    def tiles(n, w=0):
        return take(n * T, w).rearrange("p (a t) -> p a t", t=T)
    BM = tiles(TB)
    S_ = take(8 * T).rearrange("p (j c t) -> p j c t", c=2, t=T)
    QN, KN = ([tiles(2) for _ in range(2)] for _ in range(2))
    VV, QS, KS, RS = tiles(2), tiles(2), tiles(2), take(T)
    RQM, RQ, MX, LM = take(16), [take(8), take(8)], take(28), take(8)
    PT, VT = ([tiles(n, 1) for _ in range(2)] for n in (TB, 2))
    Z, TM = tiles(2, 1), tiles(2, 1)
    DG, OS = KS, TM
    B, C = k.PSB, k.c
    HALF = range(2)
    NS = 2 * TB
    N = Steps(k, "diffp",
              pe=["rq", "rk0", "rk1", "v0", "v1"],
              act=["qs0", "qs1", "ks0", "ks1", "rqs", "vt0", "vt1"],
              dve=["rqr", "rqx", "dg0", "dg1", "kg0", "kg1"])
    O = Steps(k, "diffo",
              pe=["pv0", "pv1", "os"],
              act=["os0", "os1", "osq", "xh0", "xh1"],
              dve=["osr", "o0", "o1", "oz0", "oz1", "xl0", "xl1"])
    s_mm, s_b, s_max, s_exp, s_fac, s_pa, s_p, s_tr, s_pt, s_bm = (k.sem("diff_" + x) for x in (
        "scores", "biased", "max", "exps", "factors", "first", "probs", "turned", "pt", "slopes"))
    qk_in, v_in, z_in = k.sem("diff_qk_in"), k.sem("diff_v_in"), k.sem("diff_z_in")
    lp, lm, le = k.sem("lambda_products"), k.sem("lambda_sums"), k.sem("lambda_exps")

    def blk(b):
        return slice(b * P, (b + 1) * P)

    def turns(eng, turn):
        turn(0, 0, False, 2)
        mid = (BH - 3) // 2
        with eng.Fori(0, mid) as it:
            turn(it * 2 + 1, 1, True, 2)
            turn(it * 2 + 2, 0, True, 2)
        for h in range(2 * mid + 1, BH):
            turn(h, h % 2, True, min(2, BH - 1 - h))

    def at(h, par, n):
        return h + n // TB, (par + n // TB) % 2, n % TB

    with nc.Block() as block:
        @block.sync
        def _(sp):
            def pair(buf, c0, h, sem):
                sp.dma_start(buf, k.PROJ[bass.ds(h * 2 + c0, 2), :, :].rearrange("c p t -> p c t")).then_inc(sem, 16)

            def load(h, par):
                pair(QN[par], BQ0, h, qk_in)
                pair(KN[par], BK0, h, qk_in)

            def turn(h, par, before, to_come):
                if to_come == 2:
                    sp.wait_ge(s_mm, h * NS + NS)
                    load(h + 2, par)
                if to_come:
                    N.wait(sp, h + 1, "pe.v1")
                if to_come == 2:
                    pair(VV, BV0, h + 2, v_in)
                if before:
                    O.wait(sp, h + (-1), "dve.oz1")
                pair(Z, BG0, h, z_in)
            load(0, 0)
            pair(VV, BV0, 0, v_in)
            N.wait(sp, 0, "act.ks1")
            load(1, 1)
            N.wait(sp, 0, "pe.v1")
            pair(VV, BV0, 1, v_in)
            turns(sp, turn)

        @block.tensor
        def _(pe):
            mm = nc.tensor.matmul
            N.begin(pe, "pe")
            O.begin(pe, "pe")
            pe.sem_inc(s_tr, 4)
            pe.wait_ge(lp, 3)
            mm(B[7][:, 0:2], C("ones"), LM[:, 0:2], start=True, stop=True).then_inc(lm, 1)
            pe.wait_ge(le, 1)

            def squares(h):
                N.wait(pe, h, "act.ks1")
                for n, x in enumerate((QS, KS)):
                    for c in HALF:
                        for tb in range(TB):
                            at = n * NS + c * TB + tb
                            last = mm(B[4][:, at:at + 1], x[:, c, blk(tb)], C("ones", 0, 1), start=True, stop=True)
                N.did(last, "pe", "rq")

            def key_factors(h):
                N.before(pe, h, "act.vt1")
                for c in HALF:
                    N.wait(pe, h, f"dve.dg{c}")
                    N.did(mm(B[6 + c][:, :], C("ones"), DG[:, c, :], start=True, stop=True), "pe", f"rk{c}")

            def value(h, j):
                if j == 0:
                    pe.wait_ge(v_in, h * 16 + 16)
                N.wait(pe, h, ("dve.kg0", "act.vt0")[j])
                for b in range(TB):
                    last = nc.tensor.transpose(B[6][:, blk(b)], VV[:, j, blk(b)], C("ident"))
                N.did(last, "pe", f"v{j}")

            def scores(h, par, n):
                hh, pp, tb = at(h, par, n)
                if tb == 0:
                    N.wait(pe, hh, "dve.kg1")
                for c in HALF:
                    pe.wait_ge(s_b, h * NS + (2 * n + c + 1))
                    mm(B[c][:, :], QN[pp][:, c, blk(tb)], KN[pp][:, c, :], start=True, stop=True).then_inc(s_mm, 1)

            def turned(h, n):
                pe.wait_ge(s_p, h * TB + (n + 1))
                pe.wait_ge(s_pt, h * TB + (n + 1))
                for b in range(TB):
                    last = nc.tensor.transpose(B[2 + n % 2][:, blk(b)], S_[:, n, 0, blk(b)], C("ident"))
                last.then_inc(s_tr, 1)

            def values(h, par):
                pe.wait_ge(s_pt, h * TB + (TB + 2))
                for j in HALF:
                    for b in range(TB):
                        last = mm(B[4 + j][:, :], VT[par][:, j, blk(b)], PT[par][:, b, :], start=(b == 0), stop=(b == TB - 1))
                    O.did(last, "pe", f"pv{j}")

            def out_squares(h):
                O.wait(pe, h, "act.os1")
                for j in HALF:
                    last = mm(B[7][:, :], C("ones"), OS[:, j, :], start=(j == 0), stop=(j == 1))
                O.did(last, "pe", "os")

            def turn(h, par, before, to_come):
                for n in range(TB):
                    if n + 2 < TB or to_come:
                        scores(h, par, n + 2)
                    turned(h, n)
                    if n == 0 and before:
                        if to_come:
                            N.wait(pe, h + 1, "act.rqs")
                        values(h + (-1), 1 - par)
                    if n == 0 and to_come:
                        key_factors(h + 1)
                    if n in (1, 2) and to_come:
                        value(h + 1, n - 1)
                    if n == 1 and before:
                        if to_come:
                            N.wait(pe, h + 1, "dve.kg1")
                        out_squares(h + (-1))
                    if n == 3 and to_come == 2:
                        if before:
                            O.wait(pe, h + (-1), "dve.o1")
                        squares(h + 2)
                if to_come == 0:
                    values(h, par)
                    out_squares(h)
            squares(0)
            key_factors(0)
            for j in HALF:
                value(0, j)
            squares(1)
            for n in range(2):
                scores(0, 0, n)
            turns(pe, turn)

        @block.scalar
        def _(act):
            Ac = nc.scalar.activation
            N.begin(act, "act")
            O.begin(act, "act")
            act.sem_inc(s_pt, 2)
            act.wait_ge(lm, 1)
            Ac(LM[:, 2:4], B[7][:, 0:2], ACT.Exp).then_inc(le, 1)

            def squares(h, par):
                act.wait_ge(qk_in, h * 32 + 32)
                for c in HALF:
                    N.did(Ac(QS[:, c, :], QN[par][:, c, :], ACT.Square), "act", f"qs{c}")
                N.before(act, h, "dve.kg1")
                for c in HALF:
                    N.did(Ac(KS[:, c, :], KN[par][:, c, :], ACT.Square), "act", f"ks{c}")

            def roots(h):
                N.wait(act, h, "pe.rq")
                N.did(Ac(RQM, B[4][:, 0:2 * NS], ACT.Sqrt, scale=1.0 / HD, bias=LM[:, 6:7]), "act", "rqs")

            def value(h, par, j):
                N.wait(act, h, f"pe.v{j}")
                N.did(Ac(VT[par][:, j, :], B[6][:, :], ACT.Copy), "act", f"vt{j}")

            def exps(h, n):
                for c in HALF:
                    j = 2 * (n % TB) + c
                    act.wait_ge(s_max, h * NS + (2 * n + c + 1))
                    s = S_[:, n % TB, c, :]
                    Ac(s, s, ACT.Exp, bias=MX[:, j:j + 1], accum_out=MX[:, 8 + j:9 + j]).then_inc(s_exp, 1)

            def copy(h, par, n):
                act.wait_ge(s_tr, h * TB + (n + 5))
                Ac(PT[par][:, :, blk(n)], B[2 + n % 2][:, :].rearrange("p (b t) -> p b t", t=P), ACT.Copy).then_inc(s_pt, 1)

            def out_squares(h):
                for j in HALF:
                    O.wait(act, h, f"pe.pv{j}")
                    O.did(Ac(OS[:, j, :], B[4 + j][:, :], ACT.Square), "act", f"os{j}")

            def out_root(h):
                O.wait(act, h, "pe.os")
                O.did(Ac(RS, B[7][:, :], ACT.Sqrt, scale=1.0 / (2 * HD), bias=LM[:, 6:7]), "act", "osq")

            def high(h):
                for j in HALF:
                    O.wait(act, h, f"dve.oz{j}")
                    O.did(Ac(k.XH[:, h * 2 + j, :], TM[:, j, :], ACT.Copy), "act", f"xh{j}")

            def turn(h, par, before, to_come):
                for n in range(TB):
                    if n + 1 < TB or to_come:
                        exps(h, n + 1)
                    copy(h, par, n)
                    if n == 0 and to_come:
                        roots(h + 1)
                    if n == 1 and before:
                        O.before(act, h + (-1), "dve.xl1")
                        out_squares(h + (-1))
                    if n in (1, 2) and to_come:
                        value(h + 1, 1 - par, n - 1)
                    if n == 2 and before:
                        out_root(h + (-1))
                    if n == 2 and to_come == 2:
                        squares(h + 2, par)
                    if n == 3 and before:
                        high(h + (-1))
                if to_come == 0:
                    O.before(act, h, "dve.xl1")
                    out_squares(h)
                    out_root(h)
                    high(h)
            squares(0, 0)
            roots(0)
            for j in HALF:
                value(0, 0, j)
            squares(1, 1)
            exps(0, 0)
            turns(act, turn)

        @block.vector
        def _(dve):
            V = nc.vector
            TTn, STT, TS = V.tensor_tensor, V.scalar_tensor_tensor, V.tensor_scalar
            N.begin(dve, "dve")
            O.begin(dve, "dve")
            dve.sem_inc(s_b, 2)
            for j in HALF:
                TTn(LM[:, j:j + 1], k.prm("lam", 2 * j), k.prm("lam", 2 * j + 1), ALU.mult).then_inc(lp, 1)
            V.memset(LM[:, 6:7], EPS).then_inc(lp, 1)
            TTn(LM[:, 7:8], k.prm("bq_gain"), k.prm("bk_gain"), ALU.mult).then_inc(lp, 1)
            dve.wait_ge(lp, 4)
            dve.wait_ge(le, 1)
            TTn(LM[:, 4:5], LM[:, 3:4], LM[:, 2:3], ALU.subtract).then_inc(le, 1)
            dve.wait_ge(le, 2)
            TS(LM[:, 5:6], LM[:, 4:5], -LAM_INIT, None, ALU.add).then_inc(le, 1)
            dve.wait_ge(le, 3)

            def factors(h, par):
                def do(name, ins):
                    N.did(ins, "dve", name)
                N.wait(dve, h, "act.rqs")
                do("rqr", V.reciprocal(RQM, RQM))
                N.wait(dve, h, "dve.rqr")
                do("rqx", TS(RQ[par], RQM[:, 0:NS], HD ** -0.5, None, ALU.mult))
                for c in HALF:
                    r = RQM[:, NS + c * TB:NS + (c + 1) * TB].unsqueeze(2).broadcast_to([P, TB, P])
                    do(f"dg{c}", TTn(DG[:, c, :].rearrange("p (b t) -> p b t", t=P), C("ident").unsqueeze(1).broadcast_to([P, TB, P]), r, ALU.mult))

            def keys(h, par):
                for c in HALF:
                    N.wait(dve, h, f"pe.rk{c}")
                    N.did(STT(out=KN[par][:, c, :], in0=KN[par][:, c, :], scalar=LM[:, 7:8], in1=B[6 + c][:, :], op0=ALU.mult, op1=ALU.mult), "dve", f"kg{c}")

            def slopes(h, tb):
                TS(BM[:, tb, :], DM[:, tb, :], C("nslope")[:, bass.ds(h, 1)], None, ALU.mult).then_inc(s_bm, 1)

            def bias(h, par, n):
                hh, pp, tb = at(h, par, n)
                dve.wait_ge(s_tr, h * TB + (n + 1))
                dve.wait_ge(s_bm, h * TB + (n + 1))
                if tb == 0:
                    N.wait(dve, hh, "dve.rqx")
                for c in HALF:
                    j, m = 2 * tb + c, 2 * n + c
                    dve.wait_ge(s_mm, h * NS + (m + 1))
                    s = S_[:, tb, c, :]
                    STT(out=s, in0=B[c][:, :], scalar=RQ[pp][:, c * TB + tb:c * TB + tb + 1], in1=BM[:, tb, :], op0=ALU.mult, op1=ALU.add).then_inc(s_b, 1)
                    dve.wait_ge(s_b, h * NS + (m + 3))
                    V.tensor_reduce(MX[:, j:j + 1], s, AX, ALU.max, negate=True).then_inc(s_max, 1)

            def difference(h, n):
                j = 2 * n
                dve.wait_ge(s_exp, h * NS + (2 * n + 2))
                V.reciprocal(MX[:, 16 + j:18 + j], MX[:, 8 + j:10 + j]).then_inc(s_fac, 1)
                dve.wait_ge(s_fac, h * NS + (2 * n + 1))
                TTn(MX[:, 24 + n:25 + n], MX[:, 17 + j:18 + j], LM[:, 5:6], ALU.mult).then_inc(s_fac, 1)
                TS(S_[:, n, 0, :], S_[:, n, 0, :], MX[:, 16 + j:17 + j], None, ALU.mult).then_inc(s_pa, 1)
                dve.wait_ge(s_fac, h * NS + (2 * n + 2))
                dve.wait_ge(s_pa, h * TB + (n + 1))
                STT(out=S_[:, n, 0, :], in0=S_[:, n, 1, :], scalar=MX[:, 24 + n:25 + n], in1=S_[:, n, 0, :], op0=ALU.mult, op1=ALU.add).then_inc(s_p, 1)

            def output(h):
                def do(name, ins):
                    O.did(ins, "dve", name)
                O.wait(dve, h, "act.osq")
                do("osr", V.reciprocal(RS, RS))
                O.wait(dve, h, "dve.osr")
                for j in HALF:
                    do(f"o{j}", STT(out=TM[:, j, :], in0=B[4 + j][:, :], scalar=k.prm("subln", j), in1=RS, op0=ALU.mult, op1=ALU.mult))
                dve.wait_ge(z_in, h * 16 + 16)
                for j in HALF:
                    O.wait(dve, h, f"dve.o{j}")
                    do(f"oz{j}", STT(out=TM[:, j, :], in0=TM[:, j, :], scalar=1.0 - LAM_INIT, in1=Z[:, j, :], op0=ALU.mult, op1=ALU.mult))

            def low(h):
                for j in HALF:
                    O.wait(dve, h, f"act.xh{j}")
                    O.did(TTn(k.XL[:, h * 2 + j, :], TM[:, j, :], f32(k.XH[:, h * 2 + j, :]), ALU.subtract), "dve", f"xl{j}")

            def turn(h, par, before, to_come):
                for n in range(TB):
                    if n + 1 < TB or to_come:
                        bias(h, par, n + 1)
                    if n + 1 < TB and to_come or to_come == 2:
                        slopes(h + (1 + (n + 1) // TB), (n + 1) % TB)
                    difference(h, n)
                    if n == 0 and to_come:
                        factors(h + 1, 1 - par)
                    if n == 1 and to_come:
                        keys(h + 1, 1 - par)
                    if n == 2 and before:
                        output(h + (-1))
                    if n == 3 and before:
                        low(h + (-1))
                if to_come == 0:
                    output(h)
                    low(h)
            for tb in range(TB):
                slopes(0, tb)
            factors(0, 0)
            keys(0, 0)
            bias(0, 0, 0)
            slopes(1, 0)
            turns(dve, turn)


def write_out(k):
    nc = k.nc
    O = k.AR[:, 0:2 * D].rearrange("p (j n) -> p j n", n=D)
    t, c_, out = k.sem("out_turned"), k.sem("out_copied"), [k.sem(f"out_stored{j}") for j in range(2)]
    NG = KT // 4
    with nc.Block() as block:
        @block.tensor
        def _(pe):
            for tb in range(TB):
                for g in range(NG):
                    n = tb * NG + g
                    if n >= 4:
                        pe.wait_ge(c_, n - 3)
                    for c in range(4):
                        last = nc.tensor.transpose(k.PSB[n % 4][:, c * P:(c + 1) * P], k.RES[:, 4 * g + c, tb * P:(tb + 1) * P], k.c("ident"))
                    last.then_inc(t, 1)

        @block.scalar
        def _(act):
            for tb in range(TB):
                if tb >= 2:
                    act.wait_ge(out[tb % 2], 16)
                for g in range(NG):
                    n = tb * NG + g
                    act.wait_ge(t, n + 1)
                    nc.scalar.activation(O[:, tb % 2, g * T:(g + 1) * T], k.PSB[n % 4][:, :], ACT.Copy).then_inc(c_, 1)

        @block.sync
        def _(sp):
            for tb in range(TB):
                sp.wait_ge(c_, (tb + 1) * NG)
                sp.dma_start(k.d["out"][0, tb * P:(tb + 1) * P, :], O[:, tb % 2, :]).then_inc(out[tb % 2], 16)
            sp.wait_ge(out[0], 32)
            sp.wait_ge(out[1], 32)


def build(nc, dram, stop=None):
    with ExitStack() as ctx:
        k = Kernel(nc, ctx, dram)
        setup(k)
        w = dram["w_in"][0, :, :]
        norm(k, KT, "pre_g", ahead=columns(w, 0))
        c_gate, c_za, c_b = 2560, 2584, 3608
        with k.weights():
            project(k, [(20, Q0, columns(w, 0), P, None),
                        (1, G0, columns(w, c_gate, width=NGATE), NGATE, "sigmoid"),
                        (8, ZA0, columns(w, c_za), P, "silu"),
                        (25, R0, columns(w, c_b), P, None),
                        (8, ZB0, columns(w, c_b + 3200), P, "silu")], KT, ahead=True)
        if stop == "proj1":
            return dump(k)
        with k.more():
            nsa_setup(k)
            nsa_heads(k)
        if stop == "nsa":
            return dump(k)
        with k.more():
            rwkv(k)
        if stop == "rwkv":
            return dump(k)
        with k.weights():
            project(k, [(KT, 0, columns(dram["w_out"][0, :, :], 0), P, None)], KT)
        norm(k, KT, "post_g", src=0, add=True)
        if stop == "l1":
            k.dump_res = True
            return dump(k)
        w = dram["a_w_in_2"][0, :, :]
        norm(k, KT, "a_norm", ahead=columns(w, 0))
        with k.weights():
            project(k, [(8, CQ0, columns(w, 0), P, None), (1, KPE0, columns(w, 1024, width=64), 64, None),
                        (KT, AG0, columns(w, 1088), P, "silu")], KT, ahead=True)
        norm(k, 4, "q_norm", src=CQ0)
        norm(k, 4, "kv_norm", src=CKV0, dst=4)
        wq, wkv = dram["a_w_q_up_2"][0, :, :], dram["a_w_kv_up_2"][0, :, :]
        with k.weights():
            project(k, [(AH, QN0, columns(wq, 0, step=192), P, None), (AH // 2, QR0, rope_columns(wq), P, None)], 4)
            project(k, [(2 * AH, KV0, columns(wkv, 0), P, None)], 4, rhs0=4)
        positions(k, "a_", rope=True)
        with k.more():
            mla(k)
        if stop == "mla":
            return dump(k)
        with k.weights():
            project(k, [(KT, 0, columns(dram["a_w_out_2"][0, :, :], 0), P, None)], KT, add=True)
        if stop == "l2":
            k.dump_res = True
            return dump(k)
        w = dram["b_w_in_2"][0, :, :]
        norm(k, KT, "b_norm", ahead=columns(w, 0))
        with k.weights():
            project(k, [(48, 0, columns(w, 0), P, None), (KT, BG0, columns(w, 48 * P), P, "silu")], KT, ahead=True)
        positions(k, "b_", rope=False)
        with k.more():
            diff(k)
        with k.weights():
            project(k, [(KT, 0, columns(dram["b_w_out_2"][0, :, :], 0), P, None)], KT, add=True)
        write_out(k)


def dump(k):
    nc = k.nc
    o = k.sem("dumped")
    with nc.Block() as block:
        @block.sync
        def _(sp):
            sp.dma_start(k.d["out"][0, :, :].rearrange("(a b) n -> a (b n)", a=P), (k.RES if k.dump_res else f32(k.XH[:, :, :]))[:, :, :].rearrange("p k t -> p (k t)")).then_inc(o, 16)
            sp.wait_ge(o, 16)


def kernel(**inputs):
    import concourse.bacc as bacc
    from concourse.bass_utils import run_bass_kernel_spmd

    consts, onehot = constants()
    arrays = {n: np.ascontiguousarray(a) for n, a in inputs.items()}
    arrays["consts"], arrays["onehot"] = consts, onehot
    nc = bacc.Bacc("TRN2", target_bir_lowering=False, num_devices=1)
    dram = {n: nc.dram_tensor(n, a.shape, mybir.dt.from_np(a.dtype), kind="ExternalInput").ap() for n, a in arrays.items()}
    dram["out"] = nc.dram_tensor("out", (1, T, D), F32, kind="ExternalOutput").ap()
    build(nc, dram)
    result = run_bass_kernel_spmd(nc, [arrays], core_ids=[0])
    return result.results[0]["out"]
```
